# Optimizing a Trainium2 kernel written in Bass

```python
import math
import jax, jax.numpy as jnp
from jax import lax
import numpy as np

D_MODEL = 1024
BATCH = 1
SEQ = 1024
DEPTH = 1
DEC_BATCH = 8
DEC_SEQ = 4
PAST_LEN = 2048
PAGE_SIZE = 128

HEAD_DIM = 64
ATTN_HEADS = D_MODEL // HEAD_DIM
KV_HEADS = ATTN_HEADS // 4
GQA_GROUP = ATTN_HEADS // KV_HEADS
WINDOW = 128
N_BUCKETS = 32
MAX_DISTANCE = 128
RET_HEADS = 4
RET_DV = D_MODEL // RET_HEADS
RET_DK = RET_DV // 2
RET_CHUNK = 128
ROPE_BASE = 10000.0
IN_WIDTH = (ATTN_HEADS + 2 * KV_HEADS) * HEAD_DIM + RET_HEADS * (2 * RET_DK + 2 * RET_DV) + 2 * D_MODEL
N_GROUPS = 4
EXPERTS_PER_GROUP = 8
N_EXPERTS = N_GROUPS * EXPERTS_PER_GROUP
TOP_K = 2
EXPERT_FF = D_MODEL // 2
MOE_BLOCK = 128
NORM_EPS = 1e-6
NEG_INF = -1e30

kernel_name = 'hybrid_swa_sink_retention_hmoe_step'

def rms_norm(x, gain):
    x32 = x.astype(jnp.float32)
    y = x32 * lax.rsqrt(jnp.mean(x32 * x32, axis=-1, keepdims=True) + NORM_EPS)
    return (y * gain.astype(jnp.float32)).astype(x.dtype)

def t5_causal_bucket(dist):
    max_exact = N_BUCKETS // 2
    d_f = jnp.maximum(dist, 1).astype(jnp.float32)
    large = max_exact + (jnp.log(d_f / max_exact) / math.log(MAX_DISTANCE / max_exact)
                         * (N_BUCKETS - max_exact)).astype(jnp.int32)
    large = jnp.minimum(large, N_BUCKETS - 1)
    return jnp.where(dist < max_exact, dist, large)

def banded_sink_attention(q, k, v, k_hist, v_hist, hist_valid, sink, rel_bias):
    B, L = q.shape[:2]
    lq = min(WINDOW, L)
    nb = L // lq
    lk = WINDOW + lq
    qb = q.reshape(B, nb, lq, KV_HEADS, GQA_GROUP, HEAD_DIM)
    kb = k.reshape(B, nb, lq, KV_HEADS, HEAD_DIM)
    vb = v.reshape(B, nb, lq, KV_HEADS, HEAD_DIM)
    if nb == 1:
        k_prev, v_prev = k_hist[:, None], v_hist[:, None]
    else:
        k_prev = jnp.concatenate([k_hist[:, None], kb[:, :-1]], axis=1)
        v_prev = jnp.concatenate([v_hist[:, None], vb[:, :-1]], axis=1)
    k_ctx = jnp.concatenate([k_prev, kb], axis=2)
    v_ctx = jnp.concatenate([v_prev, vb], axis=2)
    prev_ok = (jnp.arange(nb) > 0) | hist_valid
    key_ok = jnp.concatenate([jnp.broadcast_to(prev_ok[:, None], (nb, WINDOW)),
                              jnp.ones((nb, lq), dtype=bool)], axis=1)
    dist = jnp.arange(lq)[:, None] + WINDOW - jnp.arange(lk)[None, :]
    band = (dist >= 0) & (dist < WINDOW)
    bias = rel_bias.astype(jnp.float32)[t5_causal_bucket(jnp.clip(dist, 0, WINDOW - 1))]
    bias = jnp.transpose(bias, (2, 0, 1)).reshape(KV_HEADS, GQA_GROUP, lq, lk)
    sink32 = sink.astype(jnp.float32).reshape(KV_HEADS, GQA_GROUP)[None, :, :, None, None]
    scale = HEAD_DIM ** -0.5

    def block(args):
        qn, kn, vn, ok = args
        s = jnp.einsum('bqhgd,bkhd->bhgqk', qn, kn).astype(jnp.float32) * scale + bias
        s = jnp.where(band & ok[None, :], s, NEG_INF)
        m = jnp.maximum(jnp.max(s, axis=-1, keepdims=True), sink32)
        p = jnp.exp(s - m)
        p = p / (jnp.sum(p, axis=-1, keepdims=True) + jnp.exp(sink32 - m))
        return jnp.einsum('bhgqk,bkhd->bqhgd', p.astype(vn.dtype), vn)

    out = lax.map(block, (jnp.moveaxis(qb, 1, 0), jnp.moveaxis(k_ctx, 1, 0),
                          jnp.moveaxis(v_ctx, 1, 0), key_ok))
    return jnp.moveaxis(out, 0, 1).reshape(B, L, ATTN_HEADS * HEAD_DIM)

def rotary(x, pos):
    half = x.shape[-1] // 2
    inv = ROPE_BASE ** (-jnp.arange(half, dtype=jnp.float32) * 2.0 / x.shape[-1])
    ang = pos.astype(jnp.float32)[:, None] * inv[None, :]
    cos = jnp.cos(ang)[None, :, None, :]
    sin = jnp.sin(ang)[None, :, None, :]
    x1, x2 = x[..., :half], x[..., half:]
    return jnp.concatenate([x1 * cos - x2 * sin, x2 * cos + x1 * sin], axis=-1)

def chunkwise_retention(q, k, v, s0):
    B, L, H, dk = q.shape
    dv = v.shape[-1]
    C = min(RET_CHUNK, L)
    nc = L // C
    log_gamma = jnp.log(1.0 - 2.0 ** (-5.0 - jnp.arange(H, dtype=jnp.float32)))
    idx = jnp.arange(C, dtype=jnp.float32)
    diff = idx[:, None] - idx[None, :]
    decay_in = jnp.where((diff >= 0)[..., None],
                         jnp.exp(jnp.maximum(diff, 0.0)[..., None] * log_gamma), 0.0)
    q_dec = jnp.exp((idx + 1.0)[:, None] * log_gamma)
    k_dec = jnp.exp((C - 1.0 - idx)[:, None] * log_gamma)
    c_dec = jnp.exp(C * log_gamma)
    qc = q.reshape(B, nc, C, H, dk)
    kc = k.reshape(B, nc, C, H, dk)
    vc = v.reshape(B, nc, C, H, dv)
    scores = jnp.einsum('bnihd,bnjhd->bnhij', qc, kc) * jnp.transpose(decay_in, (2, 0, 1))
    o_inner = jnp.einsum('bnhij,bnjhe->bnihe', scores, vc)

    def step(S, blk):
        qn, kn, vn = blk
        cross = jnp.einsum('bihd,bhde->bihe', qn * q_dec[None, :, :, None], S)
        S = S * c_dec[None, :, None, None] + jnp.einsum('bjhd,bjhe->bhde', kn * k_dec[None, :, :, None], vn)
        return S, cross

    s_final, cross = lax.scan(step, s0, (jnp.moveaxis(qc, 1, 0), jnp.moveaxis(kc, 1, 0), jnp.moveaxis(vc, 1, 0)))
    o = o_inner + jnp.moveaxis(cross, 0, 1)
    return o.reshape(B, L, H, dv), s_final

def retention_branch(q, k, v, g, s0, pos0):
    B, L = q.shape[:2]
    pos = pos0 + jnp.arange(L)
    q = rotary(q.reshape(B, L, RET_HEADS, RET_DK).astype(jnp.float32), pos)
    k = rotary(k.reshape(B, L, RET_HEADS, RET_DK).astype(jnp.float32), pos) * RET_DK ** -0.5
    v = v.reshape(B, L, RET_HEADS, RET_DV).astype(jnp.float32)
    o, s_new = chunkwise_retention(q, k, v, s0.astype(jnp.float32))
    o = o * lax.rsqrt(jnp.mean(o * o, axis=-1, keepdims=True) + NORM_EPS)
    o = o.reshape(B, L, RET_HEADS * RET_DV).astype(g.dtype) * jax.nn.silu(g)
    return o, s_new.astype(s0.dtype)

def parallel_mixer(xn, k_hist, v_hist, hist_valid, s0, pos0, w_in, attn_sink, rel_bias,
                   w_branch_attn, w_branch_ret, w_out):
    B, L, _ = xn.shape
    widths = [ATTN_HEADS * HEAD_DIM, KV_HEADS * HEAD_DIM, KV_HEADS * HEAD_DIM,
              RET_HEADS * RET_DK, RET_HEADS * RET_DK, RET_HEADS * RET_DV, RET_HEADS * RET_DV,
              D_MODEL, D_MODEL]
    cuts = np.cumsum(widths)[:-1].tolist()
    q_a, k_a, v_a, q_r, k_r, v_r, g_r, gate_a, gate_r = jnp.split(xn @ w_in, cuts, axis=-1)
    q_a = q_a.reshape(B, L, KV_HEADS, GQA_GROUP, HEAD_DIM)
    k_a = k_a.reshape(B, L, KV_HEADS, HEAD_DIM)
    v_a = v_a.reshape(B, L, KV_HEADS, HEAD_DIM)
    attn = banded_sink_attention(q_a, k_a, v_a, k_hist, v_hist, hist_valid, attn_sink, rel_bias)
    ret, s_new = retention_branch(q_r, k_r, v_r, g_r, s0, pos0)
    merged = jax.nn.sigmoid(gate_a) * (attn @ w_branch_attn) + jax.nn.sigmoid(gate_r) * (ret @ w_branch_ret)
    new_k = jnp.concatenate([k_hist, k_a], axis=1)[:, -WINDOW:]
    new_v = jnp.concatenate([v_hist, v_a], axis=1)[:, -WINDOW:]
    return merged @ w_out, new_k, new_v, s_new

def grouped_expert_mlp(xf, experts, gates, w_gate, w_up, w_down):
    T, D = xf.shape
    A = experts.size
    flat_e = experts.reshape(-1)
    flat_g = gates.reshape(-1)
    order = jnp.argsort(flat_e)
    sorted_e = flat_e[order]
    counts = jnp.bincount(flat_e, length=N_EXPERTS)
    padded = (counts + MOE_BLOCK - 1) // MOE_BLOCK * MOE_BLOCK
    pad_end = jnp.cumsum(padded)
    pad_start = pad_end - padded
    grp_start = jnp.cumsum(counts) - counts
    dest = pad_start[sorted_e] + jnp.arange(A) - grp_start[sorted_e]
    n_blocks = -(-A // MOE_BLOCK) + N_EXPERTS
    slot_tok = jnp.full((n_blocks * MOE_BLOCK,), T, jnp.int32).at[dest].set((order // TOP_K).astype(jnp.int32))
    slot_gate = jnp.zeros((n_blocks * MOE_BLOCK,), jnp.float32).at[dest].set(flat_g[order])
    block_expert = jnp.minimum(jnp.searchsorted(pad_end, jnp.arange(n_blocks) * MOE_BLOCK, side='right'),
                               N_EXPERTS - 1)
    x_pad = jnp.concatenate([xf, jnp.zeros((1, D), xf.dtype)], axis=0)

    def run_block(args):
        tok, e = args
        xb = x_pad[tok]
        hb = jax.nn.silu(xb @ w_gate[e]) * (xb @ w_up[e])
        return hb @ w_down[e]

    yb = lax.map(run_block, (slot_tok.reshape(n_blocks, MOE_BLOCK), block_expert))
    y = jnp.zeros((T + 1, D), jnp.float32).at[slot_tok].add(yb.reshape(-1, D).astype(jnp.float32) * slot_gate[:, None])
    return y[:T].astype(xf.dtype)

def hierarchical_moe(xn, w_router_group, b_router_group, w_router_expert, b_router_expert, w_gate, w_up, w_down):
    B, L, D = xn.shape
    xf = xn.reshape(B * L, D)
    x32 = xf.astype(jnp.float32)
    p_group = jax.nn.softmax(x32 @ w_router_group.astype(jnp.float32) + b_router_group.astype(jnp.float32), axis=-1)
    g_idx = jnp.argmax(p_group, axis=-1).astype(jnp.int32)
    g_w = jnp.max(p_group, axis=-1)
    fine = (x32 @ w_router_expert.astype(jnp.float32) + b_router_expert.astype(jnp.float32))
    fine = fine.reshape(B * L, N_GROUPS, EXPERTS_PER_GROUP)
    fine = jnp.einsum('tge,tg->te', fine, jax.nn.one_hot(g_idx, N_GROUPS, dtype=jnp.float32))
    top_p, top_i = lax.top_k(jax.nn.softmax(fine, axis=-1), TOP_K)
    gates = g_w[:, None] * top_p / jnp.sum(top_p, axis=-1, keepdims=True)
    experts = g_idx[:, None] * EXPERTS_PER_GROUP + top_i.astype(jnp.int32)
    y = grouped_expert_mlp(xf, experts, gates, w_gate, w_up, w_down)
    return y.reshape(B, L, D)

def decoder_layer(x, k_hist, v_hist, hist_valid, s0, pos0, norm_mix, w_in, attn_sink, rel_bias,
                  w_branch_attn, w_branch_ret, w_out, norm_ffn, w_router_group, b_router_group,
                  w_router_expert, b_router_expert, w_gate, w_up, w_down):
    h, new_k, new_v, s_new = parallel_mixer(rms_norm(x, norm_mix), k_hist, v_hist, hist_valid, s0, pos0,
                                            w_in, attn_sink, rel_bias, w_branch_attn, w_branch_ret, w_out)
    x = x + h
    x = x + hierarchical_moe(rms_norm(x, norm_ffn), w_router_group, b_router_group,
                             w_router_expert, b_router_expert, w_gate, w_up, w_down)
    return x, new_k, new_v, s_new

def setup_inputs(seed: int = 0) -> dict:
    key = jax.random.key(seed)
    ks = jax.random.split(key, 24)

    def nrm(k, shape, scale):
        return jax.random.normal(k, shape, jnp.float32) * scale

    attn_w = ATTN_HEADS * HEAD_DIM
    ret_w = RET_HEADS * RET_DV
    return {
        'x_prompt': nrm(ks[0], (BATCH, SEQ, D_MODEL), 1.0),
        'x_sample': nrm(ks[1], (DEC_BATCH, DEC_SEQ, D_MODEL), 1.0),
        'cache_k': nrm(ks[2], (DEPTH, DEC_BATCH, WINDOW, KV_HEADS, HEAD_DIM), 1.0),
        'cache_v': nrm(ks[3], (DEPTH, DEC_BATCH, WINDOW, KV_HEADS, HEAD_DIM), 1.0),
        'state_ret': nrm(ks[4], (DEPTH, DEC_BATCH, RET_HEADS, RET_DK, RET_DV), 0.3),
        'norm_mix': 1.0 + nrm(ks[5], (DEPTH, D_MODEL), 0.02),
        'w_in': nrm(ks[6], (DEPTH, D_MODEL, IN_WIDTH), D_MODEL ** -0.5),
        'attn_sink': nrm(ks[7], (DEPTH, ATTN_HEADS), 0.5),
        'rel_bias': nrm(ks[8], (N_BUCKETS, ATTN_HEADS), 0.5),
        'w_branch_attn': nrm(ks[9], (DEPTH, attn_w, D_MODEL), attn_w ** -0.5),
        'w_branch_ret': nrm(ks[10], (DEPTH, ret_w, D_MODEL), ret_w ** -0.5),
        'w_out': nrm(ks[11], (DEPTH, D_MODEL, D_MODEL), D_MODEL ** -0.5),
        'norm_ffn': 1.0 + nrm(ks[12], (DEPTH, D_MODEL), 0.02),
        'w_router_group': nrm(ks[13], (DEPTH, D_MODEL, N_GROUPS), D_MODEL ** -0.5),
        'b_router_group': nrm(ks[14], (DEPTH, N_GROUPS), 0.01),
        'w_router_expert': nrm(ks[15], (DEPTH, D_MODEL, N_EXPERTS), D_MODEL ** -0.5),
        'b_router_expert': nrm(ks[16], (DEPTH, N_EXPERTS), 0.01),
        'w_gate': nrm(ks[17], (DEPTH, N_EXPERTS, D_MODEL, EXPERT_FF), D_MODEL ** -0.5),
        'w_up': nrm(ks[18], (DEPTH, N_EXPERTS, D_MODEL, EXPERT_FF), D_MODEL ** -0.5),
        'w_down': nrm(ks[19], (DEPTH, N_EXPERTS, EXPERT_FF, D_MODEL), EXPERT_FF ** -0.5),
        'norm_final': 1.0 + nrm(ks[20], (D_MODEL,), 0.02),
    }

def reference(x_prompt, x_sample, cache_k, cache_v, state_ret, norm_mix, w_in, attn_sink, rel_bias,
              w_branch_attn, w_branch_ret, w_out, norm_ffn, w_router_group, b_router_group,
              w_router_expert, b_router_expert, w_gate, w_up, w_down, norm_final):
    yp, ys = x_prompt, x_sample
    bp = x_prompt.shape[0]
    pk, pv, ps, sk, sv, ss = [], [], [], [], [], []
    for layer in range(DEPTH):
        weights = (norm_mix[layer], w_in[layer], attn_sink[layer], rel_bias, w_branch_attn[layer],
                   w_branch_ret[layer], w_out[layer], norm_ffn[layer], w_router_group[layer],
                   b_router_group[layer], w_router_expert[layer], b_router_expert[layer],
                   w_gate[layer], w_up[layer], w_down[layer])
        hist0 = jnp.zeros((bp, WINDOW, KV_HEADS, HEAD_DIM), x_prompt.dtype)
        s_zero = jnp.zeros((bp, RET_HEADS, RET_DK, RET_DV), state_ret.dtype)
        yp, k1, v1, s1 = decoder_layer(yp, hist0, hist0, False, s_zero, 0, *weights)
        ys, k2, v2, s2 = decoder_layer(ys, cache_k[layer], cache_v[layer], True, state_ret[layer], PAST_LEN, *weights)
        pk.append(k1)
        pv.append(v1)
        ps.append(s1)
        sk.append(k2)
        sv.append(v2)
        ss.append(s2)
    return (rms_norm(yp, norm_final), rms_norm(ys, norm_final), jnp.stack(pk), jnp.stack(pv), jnp.stack(ps),
            jnp.stack(sk), jnp.stack(sv), jnp.stack(ss))


_drawn_inputs = setup_inputs


def setup_inputs(seed=0):
    import zlib

    import numpy as np

    out = dict(_drawn_inputs(seed))
    spreads = {}
    factors = {'attn_sink': 8.0, 'b_router_expert': 4.257, 'norm_final': 2.948}
    for name, (base, spread) in spreads.items():
        noise = np.random.default_rng([zlib.crc32(name.encode()), seed]).standard_normal(out[name].shape)
        drawn = base * np.exp(spread * noise) if base else spread * noise
        out[name] = __import__('jax').numpy.asarray(drawn.astype(out[name].dtype))
    for name, factor in factors.items():
        out[name] = (out[name] * factor).astype(out[name].dtype)
    return out
```

```python
import math
from contextlib import ExitStack

import numpy as np

import concourse.bass as bass
from concourse import mybir

F32 = mybir.dt.float32
F32R = mybir.dt.float32r
I32 = mybir.dt.int32
U32 = mybir.dt.uint32
ACT = mybir.ActivationFunctionType
ALU = mybir.AluOpType
AX = mybir.AxisListType.X
ds = bass.ds

P = 128
D = 1024
KT = D // P
SEQ = 1024
NB = SEQ // P
DB, DL = 8, 4
NS = DB * DL
T = SEQ + NS
NT = NB + 1
TG = T // 3
HD = 64
KVH, GQA = 4, 4
HEADS = KVH * GQA
WINDOW = 128
BUCKETS = 32
SKEW = 3 * P
RH, DK, DV = 4, 128, 256
DVT = DV // P
PAST = 2048
EPS = 1e-6
NEG = -1e30
C_Q, C_K, C_V = 0, 1024, 1280
C_QR, C_KR, C_VR, C_GR, C_GA, C_GRT = 1536, 2048, 2560, 3584, 4608, 5632
NG, EPG = 4, 8
NE = NG * EPG
FF = 512
FT = FF // P
MAXBLK = T // P + 1
MAXOVER = 2 * T // P
SLOTS = (NE + MAXOVER) * P
ZW = 512


def rows_of(t):
    return P if t < NB else NS


def apart(eng, ch):
    eng.sem_inc(ch.passed, 1)


class Chip:
    pass


def constants():
    c = {}
    c["ident"] = np.eye(P, dtype=np.float32)

    def bucket(dist):
        d = np.maximum(dist, 1).astype(np.float32)
        large = 16 + (np.log(d / np.float32(16)) / np.float32(math.log(8.0)) * np.float32(16)).astype(np.int32)
        return np.where(dist < 16, dist, np.minimum(large, BUCKETS - 1))

    dist = 2 * P - 1 - np.arange(SKEW)
    ok = (dist >= 0) & (dist < WINDOW)
    c["skew_hot"] = ((bucket(np.clip(dist, 0, WINDOW - 1))[None] == np.arange(BUCKETS)[:, None]) & ok[None]).astype(np.float32)
    c["skew_mask"] = np.broadcast_to(np.where(ok, 0.0, NEG), (HEADS, SKEW)).astype(np.float32).copy()
    samp = np.zeros((BUCKETS, DL, P + NS), np.float32)
    mask = np.full((P, P + NS), NEG, np.float32)
    for i in range(DL):
        for col in range(P + NS):
            dd = i + P - col if col < P else i - (col - P) % DL
            if 0 <= dd < WINDOW:
                samp[bucket(np.array(dd)), i, col] = 1.0
                for r in range(P):
                    if r % DL == i and (col < P or (col - P) // DL == r // 16):
                        mask[r, col] = 0.0
    c["samp_hot"] = samp
    c["samp_mask"] = mask
    sink = np.zeros((HEADS, KVH, P), np.float32)
    for r in range(P):
        for k in range(KVH):
            sink[k * GQA + 2 * ((r // DL) % 2) + (r // (2 * DL)) % 2, k, r] = 1.0
    c["sink_hot"] = sink
    half = DK // 2
    inv = np.float32(10000.0) ** (-np.arange(half, dtype=np.float32) * np.float32(2.0) / np.float32(DK))
    pos = np.concatenate([np.arange(SEQ), np.tile(PAST + np.arange(DL), DB), np.zeros(P - NS)]).astype(np.float32)
    ang = (pos[:, None] * inv[None].astype(np.float32)).astype(np.float32)
    c["cos"] = np.cos(ang).astype(np.float32).reshape(NT, P, half).transpose(1, 0, 2).copy()
    c["sin"] = np.sin(ang).astype(np.float32).reshape(NT, P, half).transpose(1, 0, 2).copy()
    lg = np.log(np.float32(1.0) - np.float32(2.0) ** (np.float32(-5.0) - np.arange(RH, dtype=np.float32))).astype(np.float32)
    idx = np.arange(P, dtype=np.float32)
    diff = idx[None, :] - idx[:, None]
    dec = np.where(diff >= 0, np.exp(np.maximum(diff, 0)[None] * lg[:, None, None]), 0)
    c["decay"] = (np.float32(DK ** -0.5) * dec).transpose(1, 0, 2).astype(np.float32).copy()
    tok = np.arange(NS)
    same = tok[:, None] // DL == tok[None] // DL
    sdiff = (tok[None] % DL - tok[:, None] % DL).astype(np.float32)
    sdec = np.where(same & (sdiff >= 0), np.exp(np.maximum(sdiff, 0)[None] * lg[:, None, None]), 0)
    c["samp_decay"] = (np.float32(DK ** -0.5) * sdec).transpose(1, 0, 2).astype(np.float32).copy()
    c["q_decay"] = np.exp((idx + 1)[:, None] * lg).astype(np.float32)
    c["k_decay"] = (np.float32(DK ** -0.5) * np.exp((P - 1 - idx)[:, None] * lg)).astype(np.float32)
    c["samp_q_decay"] = np.exp((tok % DL + 1).astype(np.float32)[:, None] * lg).astype(np.float32)
    kd = np.float32(DK ** -0.5) * np.exp((DL - 1 - tok % DL).astype(np.float32)[:, None] * lg).astype(np.float32)
    c["samp_k_decay"] = ((tok[:, None, None] // DL == np.arange(DB)[None, :, None]) * kd[:, None, :]).astype(np.float32)
    c["c_decay"] = np.broadcast_to(np.exp(P * lg).astype(np.float32), (P, RH)).copy()
    c["samp_c_decay"] = np.broadcast_to(np.exp(DL * lg).astype(np.float32), (P, RH)).copy()
    c["ones"] = np.ones((P, P), np.float32)
    c["before"] = (np.arange(P)[:, None] < np.arange(P)[None]).astype(np.float32)
    c["iota"] = np.broadcast_to(np.arange(P, dtype=np.float32), (P, P)).copy()
    c["tokens"] = (np.arange(NT)[None] * P + np.arange(P)[:, None]).astype(np.int32)
    valid = np.zeros((P, NT), np.float32)
    valid[:, NB] = np.where(np.arange(P) < NS, 0.0, 1000.0)
    c["no_expert"] = valid
    c["zero_slots"] = np.zeros((SLOTS // P, P), np.int32)
    return c


def split_matmuls(pe, out, lhs, rhs, first, last):
    (lh, ll), (rh, rl) = lhs, rhs
    pe.matmul(out, lh, rh, start=first, stop=False)
    pe.matmul(out, lh, rl, start=False, stop=False)
    return pe.matmul(out, ll, rh, start=False, stop=last)


def t_layout_product(pe, banks, w, x):
    for k in range(KT):
        for n, (a, b) in enumerate(((0, 0), (0, 1), (1, 0))):
            for g in range(3):
                mm = pe.matmul(banks[g][:, 0:TG], w[a][:, k, :], x[b][:, k, g * TG:(g + 1) * TG],
                               start=(k == 0 and n == 0), stop=(k == KT - 1 and n == 2))
    return mm


def stage_norm(nc, ch):
    sem = ch.sem
    x_in, scale_done = [sem("n_x0"), sem("n_x1")], sem("n_scaled")
    gain_in, sq_done, ms_done, root_done, rstd_done = sem("n_gain"), sem("n_sq"), sem("n_ms"), sem("n_root"), sem("n_rstd")
    turned, hi_done, lo_done = sem("n_turned"), sem("n_hi"), sem("n_lo")
    tab_in, relx_zero, relx_done, bias_mm, bias_sum, bias_out = (
        sem("n_tab"), sem("n_relx0"), sem("n_relx"), sem("n_bmm"), sem("n_bsum"), sem("n_bout"))
    with ExitStack() as st:
        sb = ch.sbuf(st)
        xb = sb("n_xb", [P, 2, D])
        xs = sb("n_xs", [P, 2, D])
        junk = sb("n_junk", [P, D])
        gain = sb("n_gainrow", [P, D])
        stat = sb("n_stat", [P, 2, 4])
        relb = sb("n_relb", [BUCKETS, HEADS])
        hot = sb("n_skewhot", [BUCKETS, SKEW])
        mask = sb("n_skewmask", [HEADS, SKEW])
        shot = sb("n_samphot", [BUCKETS, DL, P + NS])
        smask = sb("n_sampmask", [P, P + NS])
        sinkhot = sb("n_sinkhot", [HEADS, KVH, P])
        sinkcol = sb("n_sinkcol", [HEADS, 1])
        skew = sb("n_skew", [HEADS, SKEW])
        relx = sb("n_relx", [BUCKETS, KVH, DL, P])
        banks = ch.banks

        def source(t):
            if isinstance(t, int) and t == NB:
                return ch.x_sample
            return ch.x_prompt[ds(t * P, P), :]

        with nc.Block() as block:
            @block.sync
            def _(sp):
                sp.dma_start(gain[:], ch.norm_mix.broadcast_to([P, D])).then_inc(gain_in, 16)

                def load(i, s, t):
                    if isinstance(i, int) or s >= 0:
                        sp.wait_ge(scale_done, i * 2)
                    m = NS if isinstance(t, int) else P
                    sp.dma_start(xb[0:m, s, :], source(t)).then_inc(x_in[s], 16)

                with sp.Fori(0, NB // 2) as i:
                    for s in range(2):
                        load(i, s, i * 2 + s)
                load(NB // 2, 0, NB)
                sp.wait_ge(bias_sum, 1)
                sp.dma_start(ch.skew.rearrange("h (q u) -> h q u", u=SKEW),
                             skew[:].rearrange("h (o u) -> h o u", o=1).broadcast_to([HEADS, P, SKEW])).then_inc(bias_out, 16)
                sp.wait_ge(bias_out, 16)

            @block.gpsimd
            def _(pool):
                for dst, src in ((ch.ident, ch.c["ident"]), (relb, ch.rel_bias), (hot, ch.c["skew_hot"]), (mask, ch.c["skew_mask"]), (shot, ch.c["samp_hot"]),
                                 (smask, ch.c["samp_mask"]), (sinkhot, ch.c["sink_hot"]), (sinkcol, ch.attn_sink)):
                    pool.dma_start(dst[:], src).then_inc(tab_in, 16)
                pool.wait_ge(tab_in, 16 * 8)

            @block.scalar
            def _(act):
                def front(i, s, m):
                    t = i * 2 + s
                    act.wait_ge(x_in[s], i * 16 + 16)
                    act.activation(junk[0:m, :], xb[0:m, s, :], ACT.Square, accum_out=stat[0:m, s, 0:1]).then_inc(sq_done, 1)
                    act.wait_ge(ms_done, t + 1)
                    act.activation(stat[0:m, s, 2:3], stat[0:m, s, 1:2], ACT.Sqrt).then_inc(root_done, 1)

                def back(i, s, m):
                    t = i * 2 + s
                    for b in range(2):
                        act.wait_ge(turned, t * 2 + b + 1)
                        act.activation(ch.xH[:, 4 * b:4 * b + 4, ds(t * P, m)],
                                       banks[2 * s + b][:].rearrange("p (k m) -> p k m", m=P)[:, :, 0:m], ACT.Copy).then_inc(hi_done, 1)

                with act.Fori(0, NB // 2) as i:
                    front(i, 0, P)
                    front(i, 1, P)
                    back(i, 0, P)
                    back(i, 1, P)
                front(NB // 2, 0, NS)
                back(NB // 2, 0, NS)

            @block.vector
            def _(dve):
                def front(i, s, m):
                    t = i * 2 + s
                    dve.wait_ge(sq_done, t + 1)
                    dve.tensor_scalar(stat[0:m, s, 1:2], stat[0:m, s, 0:1], 1.0 / D, EPS, ALU.mult, ALU.add).then_inc(ms_done, 1)
                    dve.wait_ge(root_done, t + 1)
                    dve.reciprocal(stat[0:m, s, 3:4], stat[0:m, s, 2:3]).then_inc(rstd_done, 1)
                    dve.wait_ge(rstd_done, t + 1)
                    dve.wait_ge(turned, i * 4)
                    dve.scalar_tensor_tensor(out=xs[0:m, s, :], in0=xb[0:m, s, :], scalar=stat[0:m, s, 3:4], in1=gain[0:m, :],
                                             op0=ALU.mult, op1=ALU.mult).then_inc(scale_done, 1)

                def back(i, s, m):
                    t = i * 2 + s
                    for b in range(2):
                        dve.wait_ge(hi_done, t * 2 + b + 1)
                        cols = ds(t * P, m)
                        dve.tensor_tensor(ch.xL[:, 4 * b:4 * b + 4, cols],
                                          banks[2 * s + b][:].rearrange("p (k m) -> p k m", m=P)[:, :, 0:m],
                                          ch.xH[:, 4 * b:4 * b + 4, cols].bitcast(F32), ALU.subtract).then_inc(lo_done, 1)

                dve.wait_ge(gain_in, 16)
                with dve.Fori(0, NB // 2) as i:
                    front(i, 0, P)
                    front(i, 1, P)
                    back(i, 0, P)
                    back(i, 1, P)
                front(NB // 2, 0, NS)
                back(NB // 2, 0, NS)
                dve.memset(relx[:], 0.0).then_inc(relx_zero, 1)
                dve.wait_ge(relx_zero, 1)
                dve.wait_ge(tab_in, 16 * 8)
                for c in range(KVH):
                    for i in range(DL):
                        for par in range(2):
                            dst = relx[:, c, i, :].rearrange("w (b r f j) -> w b r f j", r=2, f=2, j=DL)[:, :, par, :, i]
                            src = relb[:, c * GQA:(c + 1) * GQA].rearrange("w (f r) -> w r f", r=2)[:, par:par + 1, :]
                            dve.tensor_copy(dst, src.broadcast_to([BUCKETS, DB, 2])).then_inc(relx_done, 1)
                dve.wait_ge(bias_mm, 1)
                dve.tensor_tensor(skew[:], banks[4][0:HEADS, 0:SKEW], mask[:], ALU.add).then_inc(bias_sum, 1)
                for c in range(KVH):
                    dve.wait_ge(bias_mm, c + 2)
                    dve.tensor_tensor(ch.sampbias[:, c, :], banks[5 + c % 2][:, 0:P + NS], smask[:], ALU.add).then_inc(bias_sum, 1)
                dve.wait_ge(bias_mm, KVH + 2)
                dve.tensor_scalar(ch.negsink_rows[:], banks[7][:, 0:KVH], -1.0, None, ALU.mult).then_inc(bias_sum, 1)

            @block.tensor
            def _(pe):
                def turn(i, s, m):
                    t = i * 2 + s
                    pe.wait_ge(scale_done, t + 1)
                    pe.wait_ge(lo_done, i * 4)
                    for b in range(2):
                        for k in range(4):
                            tr = pe.transpose(banks[2 * s + b][:, k * P:k * P + m], xs[0:m, s, (4 * b + k) * P:(4 * b + k + 1) * P],
                                              ch.ident[0:m, 0:m])
                        tr.then_inc(turned, 1)

                pe.wait_ge(tab_in, 16 * 8)
                with pe.Fori(0, NB // 2) as i:
                    turn(i, 0, P)
                    turn(i, 1, P)
                turn(NB // 2, 0, NS)
                pe.matmul(banks[4][0:HEADS, 0:SKEW], relb[:], hot[:], start=True, stop=True).then_inc(bias_mm, 1)
                pe.wait_ge(relx_done, KVH * DL * 2)
                for c in range(KVH):
                    if c >= 2:
                        pe.wait_ge(bias_sum, c)
                    for i in range(DL):
                        mm = pe.matmul(banks[5 + c % 2][:, 0:P + NS], relx[:, c, i, :], shot[:, i, :], start=(i == 0), stop=(i == DL - 1))
                    mm.then_inc(bias_mm, 1)
                for c in range(KVH):
                    mm = pe.matmul(banks[7][:, c:c + 1], sinkhot[:, c, :], sinkcol[:], start=True, stop=True)
                mm.then_inc(bias_mm, 1)


def stage_kv(nc, ch):
    sem = ch.sem
    w_in, hi_done, lo_done, kv_mm, k_out, v_out, stored, zeroed = (
        [sem("kv_w0"), sem("kv_w1")], sem("kv_hi"), sem("kv_lo"), sem("kv_mm"), sem("kv_kout"), sem("kv_vout"), sem("kv_st"), sem("kv_zero"))
    with ExitStack() as st:
        sb = ch.sbuf(st)
        raw = sb("kv_raw", [P, 2, KT, P])
        wH, wL = sb("kv_wH", [P, KT, 4 * P], F32R), sb("kv_wL", [P, KT, 4 * P], F32R)
        banks = ch.banks
        with nc.Block() as block:
            @block.sync
            def _(sp):
                for q in range(4):
                    if q >= 2:
                        sp.wait_ge(lo_done, q - 1)
                    sp.dma_start(raw[:, q % 2], ch.w_in[:, :, C_K + q * P:C_K + (q + 1) * P]).then_inc(w_in[q % 2], 16)
                sp.dma_start(ch.new_k_sample[:, 0:WINDOW - DL, :], ch.cache_k[:, DL:WINDOW, :]).then_inc(stored, 16)
                sp.dma_start(ch.new_v_sample[:, 0:WINDOW - DL, :], ch.cache_v[:, DL:WINDOW, :]).then_inc(stored, 16)
                sp.wait_ge(k_out, NT)
                sp.dma_start(ch.new_k_prompt, ch.K[:, NB - 1, :]).then_inc(stored, 16)
                sp.wait_ge(v_out, NT)
                sp.dma_start(ch.new_v_prompt, ch.V[:, NB - 1, :]).then_inc(stored, 16)
                for b in range(DB):
                    sp.dma_start(ch.new_k_sample[b, WINDOW - DL:WINDOW, :], ch.K[b * DL:(b + 1) * DL, NB, :]).then_inc(stored, 16)
                    sp.dma_start(ch.new_v_sample[b, WINDOW - DL:WINDOW, :], ch.V[b * DL:(b + 1) * DL, NB, :]).then_inc(stored, 16)
                sp.wait_ge(stored, 16 * (4 + 2 * DB))

            @block.gpsimd
            def _(pool):
                pool.memset(ch.K[:, NB, :], 0.0).then_inc(zeroed, 1)
                pool.memset(ch.V[:, NB, :], 0.0).then_inc(zeroed, 1)

            @block.scalar
            def _(act):
                for q in range(4):
                    act.wait_ge(w_in[q % 2], 16 * (q // 2 + 1))
                    act.activation(wH[:, :, q * P:(q + 1) * P], raw[:, q % 2], ACT.Copy).then_inc(hi_done, 1)
                act.wait_ge(zeroed, 2)
                for t in range(NT):
                    m = rows_of(t)
                    act.wait_ge(kv_mm, t + 1)
                    act.activation(ch.K[0:m, t, :], banks[t % 2][0:m, 0:2 * P], ACT.Copy).then_inc(k_out, 1)
                    act.activation(ch.V[0:m, t, :], banks[t % 2][0:m, 2 * P:4 * P], ACT.Copy).then_inc(v_out, 1)

            @block.vector
            def _(dve):
                for q in range(4):
                    dve.wait_ge(hi_done, q + 1)
                    dve.tensor_tensor(wL[:, :, q * P:(q + 1) * P], raw[:, q % 2], wH[:, :, q * P:(q + 1) * P].bitcast(F32),
                                      ALU.subtract).then_inc(lo_done, 1)

            @block.tensor
            def _(pe):
                pe.wait_ge(lo_done, 4)
                for t in range(NT):
                    m = rows_of(t)
                    if t >= 2:
                        pe.wait_ge(k_out, t - 1)
                        pe.wait_ge(v_out, t - 1)
                    for k in range(KT):
                        cols = slice(t * P, t * P + m)
                        mm = split_matmuls(pe, banks[t % 2][0:m, :], (ch.xH[:, k, cols], ch.xL[:, k, cols]),
                                           (wH[:, k, :], wL[:, k, :]), k == 0, k == KT - 1)
                    mm.then_inc(kv_mm, 1)


def stage_attention(nc, ch):
    sem = ch.sem
    w_in = [sem("a_w0"), sem("a_w1")]
    bias_in, ck_in, cv_in = sem("a_bias"), sem("a_ck"), sem("a_cv")
    kd_done, vd_done, kt_turned, kt_done = sem("a_kd"), sem("a_vd"), sem("a_ktt"), sem("a_kt")
    hi_done, lo_done, q_mm, q_out = sem("a_hi"), sem("a_lo"), sem("a_qmm"), sem("a_qout")
    s_mm, s_sum, m_red, nm_done, d_done = sem("a_smm"), sem("a_ssum"), sem("a_mred"), sem("a_nm"), sem("a_d")
    p_exp, sink_exp, den_done, rcp_done, p_norm = sem("a_pexp"), sem("a_sexp"), sem("a_den"), sem("a_rcp"), sem("a_pnorm")
    p_turned, pt_hi, pt_lo, o_mm, o_out = sem("a_pt"), sem("a_pth"), sem("a_ptl"), sem("a_omm"), sem("a_oout")
    z_mm, z_out, z_red, z_nm, z_d, z_exp, z_sexp, z_den, z_rcp, z_norm = (
        sem("z_mm"), sem("z_out"), sem("z_red"), sem("z_nm"), sem("z_d"), sem("z_exp"), sem("z_sexp"), sem("z_den"), sem("z_rcp"), sem("z_norm"))
    stored, sink_in, z_par = sem("a_stored"), sem("a_sink"), sem("z_par")
    zeros_done, y_zeroed = sem("a_zeros"), sem("a_yzero")
    Y_ROWS = (SLOTS - NE * P) // KVH
    S_PER = NB
    Z_PER, Z_OUT = 6, 5
    with ExitStack() as st:
        sb = ch.sbuf(st)
        raw = sb("a_raw", [P, 2, KT, P])
        wH, wL = sb("a_wH", [P, 2, KT, P], F32R), sb("a_wL", [P, 2, KT, P], F32R)
        out = sb("a_out", [P, KT, T])
        qT = sb("a_qT", [P, 2, T])
        kT = sb("a_kT", [P, T])
        Kd, Vd = sb("a_Kd", [P, NT, 2, HD]), sb("a_Vd", [P, NT, 2, HD])
        bias = sb("a_bias_t", [P, GQA, 2 * P])
        S = sb("a_S", [P, 2, GQA, 2 * P])
        PT = sb("a_PT", [P, 2, GQA, P])
        sinkrow, negsink = sb("a_sinkrow", [P, HEADS]), sb("a_negsink", [P, HEADS])
        nm, dd, es, rs, rcp, ninv = (sb("a_" + n, [P, 2, GQA]) for n in ("nm", "dd", "es", "rs", "rcp", "den"))
        cK, cV = sb("a_cK", [P, DB, 2, HD]), sb("a_cV", [P, DB, 2, HD])
        cKT = sb("a_cKT", [P, DB, P])
        ZT = sb("a_ZT", [P, 2, P])
        Z = sb("a_Z", [P, P + NS])
        zs = sb("a_zs", [P, 6])
        zeros = sb("a_zeros_t", [P, 1, ZW])
        banks = ch.banks
        b7 = banks[7]

        def dup(ap, n):
            return ap.rearrange("p n (o d) -> p n o d", o=1).broadcast_to([P, n, 2, HD])

        def s_bank(n, g):
            return banks[2 * (n % 2) + g % 2][:, (g // 2) * 2 * P:(g // 2 + 1) * 2 * P]

        def cols_of(n):
            return slice(P, 2 * P) if n == 0 else slice(0, 2 * P)

        with nc.Block() as block:
            @block.sync
            def _(sp):
                sp.wait_ge(zeros_done, 1)
                sp.dma_start(sinkrow[:], ch.attn_sink_row.broadcast_to([P, HEADS])).then_inc(sink_in, 16)
                with sp.Fori(0, KVH) as c:
                    for f in range(2):
                        sp.wait_ge(lo_done, c * 2)
                        apart(sp, ch)
                        sp.dma_start(raw[:, f], ch.w_in[:, :, ds(c * 256 + f * P, P)]).then_inc(w_in[f], 16)
                    sp.wait_ge(s_sum, c * S_PER)
                    apart(sp, ch)
                    sp.dma_start(bias[:], ch.skew_read[:, ds(c * GQA, GQA), :]).then_inc(bias_in, 16)
                    sp.dma_start(ch.y_d[ds(c * Y_ROWS + NE * P, Y_ROWS), :].rearrange("(p r) (a b) -> p (r a) b", p=P, b=ZW),
                                 zeros[:].broadcast_to([P, Y_ROWS * D // (P * ZW), ZW])).then_inc(y_zeroed, 16)
                    sp.wait_ge(z_mm, c * Z_PER)
                    for b in range(DB):
                        for o in range(2):
                            sp.dma_start(cK[:, b, o, :], ch.cache_k[b, :, ds(c * HD, HD)]).then_inc(ck_in, 16)
                            sp.dma_start(cV[:, b, o, :], ch.cache_v[b, :, ds(c * HD, HD)]).then_inc(cv_in, 16)
                sp.wait_ge(o_out, KVH * 2 * NB)
                sp.wait_ge(z_norm, KVH * 4)
                sp.dma_start(ch.attn_t, out[:]).then_inc(stored, 16)
                sp.wait_ge(stored, 16)
                sp.wait_ge(y_zeroed, 16 * KVH)

            @block.gpsimd
            def _(pool):
                pool.memset(zeros[:], 0.0).then_inc(zeros_done, 1)
                with pool.Fori(0, KVH) as c:
                    pool.wait_ge(kt_turned, c * 3)
                    pool.tensor_copy(Kd[:], dup(ch.K[:, :, ds(c * HD, HD)], NT)).then_inc(kd_done, 1)
                    pool.wait_ge(o_mm, c * NB)
                    pool.wait_ge(z_mm, c * Z_PER)
                    pool.tensor_copy(Vd[:], dup(ch.V[:, :, ds(c * HD, HD)], NT)).then_inc(vd_done, 1)
                    for n in range(NB):
                        pool.wait_ge(rcp_done, c * NB + n + 1)
                        w = cols_of(n)
                        pool.tensor_tensor(S[:, n % 2, :, w], S[:, n % 2, :, w],
                                           rcp[:, n % 2, :].rearrange("p (g o) -> p g o", o=1).broadcast_to([P, GQA, w.stop - w.start]),
                                           ALU.mult).then_inc(p_norm, 1)

            @block.scalar
            def _(act):
                with act.Fori(0, KVH) as c:
                    act.wait_ge(q_mm, c * 2)
                    for f in range(2):
                        act.wait_ge(w_in[f], c * 16 + 16)
                        act.activation(wH[:, f], raw[:, f], ACT.Copy).then_inc(hi_done, 1)
                    for f in range(2):
                        act.wait_ge(q_mm, c * 2 + f + 1)
                        for g in range(3):
                            ins = act.activation(qT[:, f, g * TG:(g + 1) * TG], banks[3 * f + g][:, 0:TG], ACT.Copy, scale=HD ** -0.5)
                        ins.then_inc(q_out, 1)

                    def exps(n):
                        s, w = n % 2, cols_of(n)
                        act.wait_ge(nm_done, c * NB + n + 1)
                        for g in range(GQA):
                            ins = act.activation(S[:, s, g, w], S[:, s, g, w], ACT.Exp, bias=nm[:, s, g:g + 1], accum_out=rs[:, s, g:g + 1])
                        ins.then_inc(p_exp, 1)
                        act.wait_ge(d_done, c * NB + n + 1)
                        act.activation(es[:, s, :], dd[:, s, :], ACT.Exp).then_inc(sink_exp, 1)

                    def out_evac(n):
                        act.wait_ge(o_mm, c * NB + n + 1)
                        for par in range(2):
                            r = slice(par * HD, (par + 1) * HD)
                            act.activation(out[r, ds(c * 2, 2), n * P:(n + 1) * P],
                                           banks[6][r, :].rearrange("p (r f i) -> p r f i", r=2, f=2)[:, par], ACT.Copy).then_inc(o_out, 1)

                    def sampled(step):
                        act.wait_ge(z_mm, c * Z_PER + step + 1)
                        if step in (0, 1):
                            act.activation(cKT[:, 4 * step:4 * step + 4, :], b7[:].rearrange("p (b k) -> p b k", b=4), ACT.Copy).then_inc(z_out, 1)
                        if step == 4:
                            act.activation(ZT[:, 0, :], b7[:, 0:P], ACT.Copy)
                            act.activation(ZT[0:NS, 1, :], b7[0:NS, P:2 * P], ACT.Copy).then_inc(z_out, 1)

                    def sampled_exp():
                        act.wait_ge(z_nm, c + 1)
                        act.activation(Z[:], Z[:], ACT.Exp, bias=zs[:, 0:1], accum_out=zs[:, 1:2]).then_inc(z_exp, 1)
                        act.wait_ge(z_d, c + 1)
                        act.activation(zs[:, 3:4], zs[:, 2:3], ACT.Exp).then_inc(z_sexp, 1)

                    for n in range(NB):
                        exps(n)
                        if n >= 1:
                            out_evac(n - 1)
                        act.wait_ge(p_turned, c * 2 * NB + 2 * n + 1)
                        act.activation(PT[:, 0], banks[4][:].rearrange("p (g i) -> p g i", g=GQA), ACT.Copy).then_inc(pt_hi, 1)
                        if n in (1, 2, 5):
                            sampled({1: 0, 2: 1, 5: 4}[n])
                        if n == 4:
                            sampled_exp()
                    out_evac(NB - 1)

            @block.vector
            def _(dve):
                dve.wait_ge(sink_in, 16)
                dve.tensor_scalar(negsink[:].rearrange("p (c r f) -> p c r f", r=2, f=2), sinkrow[:].rearrange("p (c f r) -> p c r f", r=2, f=2),
                                  -1.0, None, ALU.mult).then_inc(z_rcp, 1)
                dve.wait_ge(z_rcp, 1)
                with dve.Fori(0, KVH) as c:
                    for f in range(2):
                        dve.wait_ge(hi_done, c * 2 + f + 1)
                        dve.tensor_tensor(wL[:, f], raw[:, f], wH[:, f].bitcast(F32), ALU.subtract).then_inc(lo_done, 1)
                    for q in range(3):
                        dve.wait_ge(kt_turned, c * 3 + q + 1)
                        w = 4 * P if q < 2 else NS
                        dve.tensor_copy(kT[:, q * 4 * P:q * 4 * P + w], banks[6 + q % 2][:, 0:w]).then_inc(kt_done, 1)
                    dve.wait_ge(bias_in, c * 16 + 16)

                    def front(n):
                        s, w = n % 2, cols_of(n)
                        m = c * NB + n + 1
                        dve.wait_ge(s_mm, m)
                        if n >= 2:
                            dve.wait_ge(p_turned, c * 2 * NB + 2 * (n - 1))
                        for h in range(2):
                            ins = dve.tensor_tensor(S[:, s, 2 * h:2 * h + 2, w], banks[2 * s + h][:].rearrange("p (g k) -> p g k", g=2)[:, :, w],
                                                    bias[:].rearrange("p (f r) k -> p r f k", r=2)[:, h, :, w], ALU.add)
                        ins.then_inc(s_sum, 1)
                        dve.wait_ge(s_sum, m)
                        dve.tensor_reduce(nm[:, s, :], S[:, s, :, w], AX, ALU.max, negate=True).then_inc(m_red, 1)
                        dve.wait_ge(m_red, m)
                        dve.tensor_tensor(nm[:, s, :], nm[:, s, :], negsink[:, ds(c * GQA, GQA)], ALU.min).then_inc(nm_done, 1)
                        dve.wait_ge(nm_done, m)
                        dve.tensor_tensor(dd[:, s, :], nm[:, s, :], negsink[:, ds(c * GQA, GQA)], ALU.subtract).then_inc(d_done, 1)

                    def back(n):
                        s = n % 2
                        m = c * NB + n + 1
                        dve.wait_ge(p_exp, m)
                        dve.wait_ge(sink_exp, m)
                        dve.tensor_tensor(ninv[:, s, :], rs[:, s, :], es[:, s, :], ALU.add).then_inc(den_done, 1)
                        dve.wait_ge(den_done, m)
                        dve.reciprocal(rcp[:, s, :], ninv[:, s, :]).then_inc(rcp_done, 1)

                    def turned_copy(n):
                        dve.wait_ge(p_turned, c * 2 * NB + 2 * n + 2)
                        dve.tensor_copy(PT[:, 1], banks[5][:].rearrange("p (g i) -> p g i", g=GQA)).then_inc(pt_lo, 1)

                    def sampled(step):
                        dve.wait_ge(z_mm, c * Z_PER + step + 1)
                        if step == 2:
                            dve.tensor_copy(ZT[:, 0, :], b7[:, 0:P])
                            dve.tensor_copy(ZT[0:NS, 1, :], b7[0:NS, P:2 * P]).then_inc(z_out, 1)
                        if step == 3:
                            dve.tensor_tensor(Z[:], b7[:, 0:P + NS], ch.sampbias[:, ds(c, 1), :].rearrange("p o k -> p (o k)"), ALU.add).then_inc(z_out, 1)
                            dve.wait_ge(z_out, c * Z_OUT + 4)
                            dve.tensor_reduce(zs[:, 0:1], Z[:], AX, ALU.max, negate=True).then_inc(z_red, 1)
                            dve.wait_ge(z_red, c * 2 + 1)
                            dve.tensor_tensor(zs[:, 0:1], zs[:, 0:1], ch.negsink_rows[:, ds(c, 1)], ALU.min).then_inc(z_nm, 1)
                            dve.wait_ge(z_nm, c + 1)
                            dve.tensor_tensor(zs[:, 2:3], zs[:, 0:1], ch.negsink_rows[:, ds(c, 1)], ALU.subtract).then_inc(z_d, 1)
                        if step == 5:
                            for par in range(2):
                                r = slice(par * HD, (par + 1) * HD)
                                for b in range(2):
                                    dve.tensor_copy(out[r, ds(c * 2 + b, 1), SEQ:T].rearrange("p o (b i) -> p (o b) i", i=DL),
                                                    b7[r, 0:P].rearrange("p (b r f i) -> p r f b i", b=DB, r=2, f=2)[:, par, b]).then_inc(z_norm, 1)

                    def sampled_norm():
                        dve.wait_ge(z_exp, c + 1)
                        dve.wait_ge(z_sexp, c + 1)
                        dve.tensor_tensor(zs[:, 4:5], zs[:, 1:2], zs[:, 3:4], ALU.add).then_inc(z_den, 1)
                        dve.wait_ge(z_den, c + 1)
                        dve.reciprocal(zs[:, 5:6], zs[:, 4:5]).then_inc(z_rcp, 1)
                        dve.wait_ge(z_rcp, c + 2)
                        dve.tensor_scalar(Z[:], Z[:], zs[:, 5:6], None, ALU.mult).then_inc(z_red, 1)

                    front(0)
                    for n in range(NB):
                        if n + 1 < NB:
                            front(n + 1)
                        back(n)
                        turned_copy(n)
                        if n in (3, 4, 6):
                            sampled({3: 2, 4: 3, 6: 5}[n])
                        if n == 4:
                            sampled_norm()

            @block.tensor
            def _(pe):
                with pe.Fori(0, KVH) as c:
                    pe.wait_ge(kd_done, c + 1)
                    pe.wait_ge(z_norm, c * 4)
                    pe.wait_ge(o_out, c * 2 * NB)
                    for q in range(3):
                        if q == 2:
                            pe.wait_ge(kt_done, c * 3 + 1)
                        for t in range(q * 4, min(q * 4 + 4, NT)):
                            tr = pe.transpose(banks[6 + q % 2][:, (t - q * 4) * P:(t - q * 4 + 1) * P],
                                              Kd[:, t].rearrange("p o d -> p (o d)"), ch.ident[:])
                        tr.then_inc(kt_turned, 1)
                    pe.wait_ge(s_sum, c * NB)
                    pe.wait_ge(pt_hi, c * NB)
                    pe.wait_ge(pt_lo, c * NB)
                    for f in range(2):
                        pe.wait_ge(lo_done, c * 2 + f + 1)
                        t_layout_product(pe, banks[3 * f:3 * f + 3], (wH[:, f], wL[:, f]), (ch.xH, ch.xL)).then_inc(q_mm, 1)
                    pe.wait_ge(kt_done, c * 3 + 3)
                    pe.wait_ge(q_out, c * 2 + 2)
                    pe.wait_ge(vd_done, c + 1)

                    def scores(n):
                        if n >= 2:
                            pe.wait_ge(s_sum, c * NB + n - 1)
                        keys = slice(max(n - 1, 0) * P, (n + 1) * P)
                        for g in range(GQA):
                            r = slice((g % 2) * HD, (g % 2 + 1) * HD)
                            mm = pe.matmul(s_bank(n, g)[:, cols_of(n)], qT[r, g // 2, n * P:(n + 1) * P], kT[r, keys], start=True, stop=True)
                        mm.then_inc(s_mm, 1)

                    def turn(n):
                        pe.wait_ge(p_norm, c * NB + n + 1)
                        for kb in range(2):
                            pe.wait_ge(pt_hi if kb == 0 else pt_lo, c * NB + n)
                            for g in range(GQA):
                                src = kb if n > 0 else 1
                                tr = pe.transpose(banks[4 + kb][:, g * P:(g + 1) * P], S[:, n % 2, g, src * P:(src + 1) * P], ch.ident[:])
                            tr.then_inc(p_turned, 1)

                    def weigh(n):
                        pe.wait_ge(pt_hi, c * NB + n + 1)
                        pe.wait_ge(pt_lo, c * NB + n + 1)
                        pe.wait_ge(o_out, c * 2 * NB + 2 * n)
                        for kb in range(0 if n else 1, 2):
                            mm = pe.matmul(banks[6][:], Vd[:, n - 1 + kb].rearrange("p o d -> p (o d)"), PT[:, kb].rearrange("p g i -> p (g i)"),
                                           start=(kb == (0 if n else 1)), stop=(kb == 1))
                        mm.then_inc(o_mm, 1)

                    def sampled(step):
                        if step:
                            pe.wait_ge(z_out, c * Z_OUT + step)
                        if step in (0, 1):
                            pe.wait_ge(ck_in, c * (32 * DB) + 32 * DB)
                            for b in range(4):
                                mm = pe.transpose(b7[:, b * P:(b + 1) * P], cK[:, 4 * step + b].rearrange("p o d -> p (o d)"), ch.ident[:])
                        if step == 2:
                            for par in range(2):
                                r = slice(par * HD, (par + 1) * HD)
                                qs = qT[r, :, SEQ:T].rearrange("p f (b i) -> p b f i", b=DB)
                                for b in range(DB):
                                    pe.matmul(b7[:, b * 16 + par * 8:b * 16 + par * 8 + 8].rearrange("p (f i) -> p f i", f=2),
                                              cKT[r, b, :], qs[:, b], start=True, stop=True)
                                mm = pe.matmul(b7[0:NS, P:2 * P].rearrange("p (b r f i) -> p r b f i", r=2, f=2, i=DL)[:, par],
                                               kT[r, SEQ:T], qs, start=True, stop=True)
                                if par == 0:
                                    mm.then_inc(z_par, 1)
                                    pe.wait_ge(z_par, c + 1)
                        if step == 3:
                            pe.transpose(b7[:, 0:P], ZT[:, 0, :], ch.ident[:])
                            mm = pe.transpose(b7[:, P:P + NS], ZT[0:NS, 1, :], ch.ident[0:NS, 0:NS])
                        if step == 4:
                            pe.wait_ge(z_red, c * 2 + 2)
                            pe.transpose(b7[:, 0:P], Z[:, 0:P], ch.ident[:])
                            mm = pe.transpose(b7[0:NS, P:2 * P], Z[:, P:P + NS], ch.ident[:])
                        if step == 5:
                            pe.wait_ge(cv_in, c * (32 * DB) + 32 * DB)
                            pe.matmul(b7[:, 0:P], Vd[0:NS, NB].rearrange("p o d -> p (o d)"), ZT[0:NS, 1, :], start=True, stop=False)
                            for b in range(DB):
                                mm = pe.matmul(b7[:, b * 16:(b + 1) * 16], cV[:, b].rearrange("p o d -> p (o d)"), ZT[:, 0, b * 16:(b + 1) * 16],
                                               start=False, stop=(b == DB - 1))
                        mm.then_inc(z_mm, 1)

                    scores(0)
                    for n in range(NB):
                        if n + 1 < NB:
                            scores(n + 1)
                        if n >= 1:
                            weigh(n - 1)
                        turn(n)
                        if n < Z_PER:
                            sampled(n)
                    weigh(NB - 1)


def stage_branch_attn(nc, ch, br):
    sem = ch.sem
    KINDS = 3
    w_in = [sem(f"b_w{q}") for q in range(KINDS)]
    hi_done, lo_done, mm_done = sem("b_hi"), sem("b_lo"), sem("b_mm")
    a_in, a_hi, a_lo = [sem("b_a0"), sem("b_a1")], sem("b_ahi"), sem("b_alo")
    ga_out, gr_out, m1_out, gr_st, m1_st = sem("b_ga"), sem("b_gr"), sem("b_m1"), sem("b_grst"), sem("b_m1st")
    brH, brL = br
    with ExitStack() as st:
        sb = ch.sbuf(st)
        raw = sb("b_raw", [P, KINDS, KT, P])
        wH, wL = sb("b_wH", [P, KINDS, KT, P], F32R), sb("b_wL", [P, KINDS, KT, P], F32R)
        a_raw = sb("b_araw", [P, 2, T])
        ga, gr, m1 = sb("b_ga_s", [P, T]), sb("b_gr_s", [P, T]), sb("b_m1_s", [P, T])
        banks = ch.banks

        def bank_set(m2, q):
            b = 3 * ((m2 * KINDS + q) % 2)
            return banks[b:b + 3]

        with nc.Block() as block:
            @block.sync
            def _(sp):
                def load(m, q):
                    src = (ch.w_in[:, :, ds(m * P + C_GA, P)], ch.w_in[:, :, ds(m * P + C_GRT, P)], ch.w_attn[:, :, ds(m * P, P)])[q]
                    sp.dma_start(raw[:, q], src).then_inc(w_in[q], 16)

                for q in range(KINDS):
                    load(0, q)
                for k in range(KT):
                    if k >= 2:
                        sp.wait_ge(a_lo, k - 1)
                    sp.dma_start(a_raw[:, k % 2], ch.attn_t[:, k, :]).then_inc(a_in[k % 2], 16)
                with sp.Fori(1, KT) as m:
                    for q in range(KINDS):
                        sp.wait_ge(lo_done, m * KINDS - KINDS + q + 1)
                        apart(sp, ch)
                        load(m, q)

            @block.gpsimd
            def _(pool):
                with pool.Fori(0, KT) as m:
                    pool.wait_ge(gr_out, m + 1)
                    apart(pool, ch)
                    pool.dma_start(ch.gate_t[:, ds(m, 1), :].rearrange("p o t -> p (o t)"), gr[:]).then_inc(gr_st, 16)
                    pool.wait_ge(m1_out, m + 1)
                    apart(pool, ch)
                    pool.dma_start(ch.m1_t[:, ds(m, 1), :].rearrange("p o t -> p (o t)"), m1[:]).then_inc(m1_st, 16)
                pool.wait_ge(gr_st, 16 * KT)
                pool.wait_ge(m1_st, 16 * KT)

            @block.scalar
            def _(act):
                for k in range(KT):
                    act.wait_ge(a_in[k % 2], 16 * (k // 2 + 1))
                    act.activation(brH[:, k, :], a_raw[:, k % 2], ACT.Copy).then_inc(a_hi, 1)
                with act.Fori(0, KT // 2) as j:
                    for m2 in range(2):
                        m = j * 2 + m2
                        for q in range(KINDS):
                            act.wait_ge(w_in[q], m * 16 + 16)
                            act.wait_ge(mm_done, m * KINDS)
                            act.activation(wH[:, q], raw[:, q], ACT.Copy).then_inc(hi_done, 1)
                        act.wait_ge(m1_out, m)
                        act.wait_ge(gr_st, m * 16)
                        for q, dst, done in ((0, ga, ga_out), (1, gr, gr_out)):
                            act.wait_ge(mm_done, m * KINDS + q + 1)
                            for g in range(3):
                                ins = act.activation(dst[:, g * TG:(g + 1) * TG], bank_set(m2, q)[g][:, 0:TG], ACT.Sigmoid)
                            ins.then_inc(done, 1)

            @block.vector
            def _(dve):
                for k in range(KT):
                    dve.wait_ge(a_hi, k + 1)
                    dve.tensor_tensor(brL[:, k, :], a_raw[:, k % 2], brH[:, k, :].bitcast(F32), ALU.subtract).then_inc(a_lo, 1)
                with dve.Fori(0, KT // 2) as j:
                    for m2 in range(2):
                        m = j * 2 + m2
                        for q in range(KINDS):
                            dve.wait_ge(hi_done, m * KINDS + q + 1)
                            dve.tensor_tensor(wL[:, q], raw[:, q], wH[:, q].bitcast(F32), ALU.subtract).then_inc(lo_done, 1)
                        dve.wait_ge(mm_done, m * KINDS + 3)
                        dve.wait_ge(ga_out, m + 1)
                        dve.wait_ge(m1_st, m * 16)
                        for g in range(3):
                            cols = slice(g * TG, (g + 1) * TG)
                            ins = dve.tensor_tensor(m1[:, cols], bank_set(m2, 2)[g][:, 0:TG], ga[:, cols], ALU.mult)
                        ins.then_inc(m1_out, 1)

            @block.tensor
            def _(pe):
                with pe.Fori(0, KT // 2) as j:
                    for m2 in range(2):
                        m = j * 2 + m2
                        for q, free in ((0, (gr_out, m)), (1, (m1_out, m)), (2, (ga_out, m + 1))):
                            pe.wait_ge(lo_done, m * KINDS + q + 1)
                            pe.wait_ge(*free)
                            if q == 2:
                                pe.wait_ge(a_lo, KT)
                            t_layout_product(pe, bank_set(m2, q), (wH[:, q], wL[:, q]), (ch.xH, ch.xL) if q < 2 else (brH, brL)).then_inc(mm_done, 1)


def stage_retention(nc, ch, ret):
    sem = ch.sem
    ORDER = [(C_GR, DV, 4), (C_GR + P, DV, 5), (C_QR, DK, 0), (C_KR, DK, 1), (C_VR, DV, 2), (C_VR + P, DV, 3)]
    PIECES = len(ORDER)
    w_in = [sem("r_w0"), sem("r_w1")]
    tab_in, hi_done, lo_done, g_mm, sg_done, g_done = sem("r_tab"), sem("r_hi"), sem("r_lo"), sem("r_gmm"), sem("r_sg"), sem("r_g")
    p_mm, v_out, rot_a, rot_b, rot_done = sem("r_pmm"), sem("r_v"), sem("r_ra"), sem("r_rb"), sem("r_rot")
    turned, t_out, s_mm, s_out, o_mm, st_mm, st_out = (
        sem("r_t"), sem("r_tout"), sem("r_smm"), sem("r_sout"), sem("r_omm"), sem("r_stmm"), sem("r_stout"))
    sq_done, ss_mm, ms_done, root_done, rstd_done, og_done, r_done = (
        sem("r_sq"), sem("r_ssmm"), sem("r_ms"), sem("r_root"), sem("r_rstd"), sem("r_og"), sem("r_r"))
    s0_in, s0_new, s0_stored, stored = sem("r_s0"), sem("r_s0n"), sem("r_s0s"), sem("r_stored")
    km_done, z_mm, dec_done = sem("r_km"), sem("r_zmm"), sem("r_dec")
    with ExitStack() as st:
        sb = ch.sbuf(st)
        raw = sb("r_raw", [P, 2, KT, P])
        wH, wL = sb("r_wH", [P, KT, PIECES * P], F32R), sb("r_wL", [P, KT, PIECES * P], F32R)
        gs = sb("r_gs", [P, DVT, T])
        cos, sin = sb("r_cos", [P, NT, DK // 2]), sb("r_sin", [P, NT, DK // 2])
        decay, sdecay = sb("r_decay", [P, RH, P]), sb("r_sdecay", [NS, RH, NS])
        qdec, kdec, sqdec, cdec, scdec = (sb("r_" + n, [m, RH]) for n, m in (("qdec", P), ("kdec", P), ("sqdec", NS), ("cdec", P), ("scdec", P)))
        skdec = sb("r_skdec", [NS, DB, RH])
        dec = sb("r_dec_h", [P, 3])
        ones = sb("r_ones", [P, P])
        ta, tb = sb("r_ta", [P, 2, DK]), sb("r_tb", [P, 2, DK])
        rot = sb("r_rotd", [P, 2, 4, DK])
        v = sb("r_vn", [P, 3, DV])
        qkT = sb("r_qkT", [P, 3, P])
        sT = sb("r_sT", [P, P])
        S = sb("r_S", [P, DV])
        sq, og = sb("r_sqv", [P, DVT, P]), sb("r_ogv", [P, DVT, P])
        rstd = sb("r_rstdv", [P, P])
        S0 = sb("r_S0", [P, DB, DV])
        kmask = sb("r_kmask", [NS, 2, DK])
        banks = ch.banks
        half = DK // 2

        def out_bank(t, f):
            m = rows_of(t)
            if t == NB:
                return banks[4 + 3 * f][:, 0:m]
            return banks[4 + 3 * (t % 2)][:, f * P:f * P + m]

        def state_bank(b):
            return banks[5 if b % 2 else 3][:, 0:DV]

        with nc.Block() as block:
            @block.sync
            def _(sp):
                for dst, name in ((cos, "cos"), (sin, "sin"), (decay, "decay"), (sdecay, "samp_decay"), (qdec, "q_decay"), (kdec, "k_decay"),
                                  (sqdec, "samp_q_decay"), (cdec, "c_decay"), (scdec, "samp_c_decay"), (skdec, "samp_k_decay"), (ones, "ones")):
                    sp.dma_start(dst[:], ch.c[name]).then_inc(tab_in, 16)
                with sp.Fori(0, RH) as h:
                    for p, (c0, step, _) in enumerate(ORDER):
                        sp.wait_ge(lo_done, h * PIECES + max(p - 1, 0))
                        apart(sp, ch)
                        sp.dma_start(raw[:, p % 2], ch.w_in[:, :, ds(h * step + c0, P)]).then_inc(w_in[p % 2], 16)

            @block.gpsimd
            def _(pool):
                pool.wait_ge(tab_in, 16 * 11)
                with pool.Fori(0, RH) as h:
                    pool.wait_ge(rot_done, h * NT)
                    pool.tensor_copy(dec[:, 0:1], qdec[:, ds(h, 1)])
                    pool.tensor_copy(dec[:, 1:2], kdec[:, ds(h, 1)])
                    pool.tensor_copy(dec[0:NS, 2:3], sqdec[:, ds(h, 1)]).then_inc(dec_done, 1)
                    pool.wait_ge(s0_stored, h * 16)
                    apart(pool, ch)
                    pool.dma_start(S0[:], ch.state_ret[:, ds(h, 1)].rearrange("b o d e -> d (b o) e")).then_inc(s0_in, 16)
                    for t in range(NT):
                        m = rows_of(t)
                        n = h * NT + t + 1
                        r = rot[0:m, t % 2]
                        a, b = (x[0:m].rearrange("p a (s d) -> p a s d", s=2) for x in (ta, tb))
                        dst = r.rearrange("p (a b) (s d) -> p a b s d", b=2, s=2)[:, :, 0]
                        pool.wait_ge(rot_a, n)
                        if t >= 2:
                            pool.wait_ge(turned, n - 2)
                            pool.wait_ge(st_mm, h * NB + t - 1)
                        else:
                            pool.wait_ge(turned, h * NT)
                            pool.wait_ge(st_mm, h * NB)
                            pool.wait_ge(km_done, h * DB)
                        pool.tensor_tensor(dst[:, :, 0], a[:, :, 0], b[:, :, 1], ALU.subtract)
                        pool.tensor_tensor(dst[:, :, 1], a[:, :, 1], b[:, :, 0], ALU.add).then_inc(rot_b, 1)
                        pool.wait_ge(rot_b, n)
                        pool.wait_ge(dec_done, h + 1)
                        apart(pool, ch)
                        col = 0 if t < NB else 2
                        pool.tensor_scalar(r[:, 1, :], r[:, 0, :], dec[0:m, col:col + 1], None, ALU.mult)
                        pool.tensor_scalar(r[:, 3, :], r[:, 2, :], dec[0:m, 1:2], None, ALU.mult).then_inc(rot_done, 1)
                    pool.wait_ge(st_out, h * NB + NB)
                    apart(pool, ch)
                    pool.dma_start(ch.new_state_prompt[ds(h, 1)].rearrange("o d e -> d (o e)"), S[:]).then_inc(stored, 16)
                    pool.wait_ge(s0_new, h * DB + DB)
                    apart(pool, ch)
                    pool.dma_start(ch.new_state_sample[:, ds(h, 1)].rearrange("b o d e -> d (b o) e"), S0[:]).then_inc(s0_stored, 16)
                pool.wait_ge(stored, 16 * RH)
                pool.wait_ge(s0_stored, 16 * RH)

            @block.scalar
            def _(act):
                with act.Fori(0, RH) as h:
                    for p, (_, _, slot) in enumerate(ORDER):
                        act.wait_ge(w_in[p % 2], h * 48 + 16 * (p // 2 + 1))
                        if p == 0:
                            act.wait_ge(g_mm, h * 2)
                        if p == 2:
                            act.wait_ge(p_mm, h * NT)
                        act.activation(wH[:, :, slot * P:(slot + 1) * P], raw[:, p % 2], ACT.Copy).then_inc(hi_done, 1)
                    act.wait_ge(r_done, h * NT)
                    for f in range(DVT):
                        act.wait_ge(g_mm, h * 2 + f + 1)
                        for g in range(3):
                            ins = act.activation(gs[:, f, g * TG:(g + 1) * TG], banks[3 * f + g][:, 0:TG], ACT.Sigmoid)
                        ins.then_inc(sg_done, 1)

                    def evac_v(t):
                        m = rows_of(t)
                        act.wait_ge(p_mm, h * NT + t + 1)
                        if t >= 3:
                            act.wait_ge(o_mm, h * NT + t - 2)
                            act.wait_ge(st_mm, h * NB + t - 2)
                        else:
                            act.wait_ge(o_mm, h * NT)
                            act.wait_ge(z_mm, h * DB)
                        act.activation(v[0:m, t % 3], banks[t % 2][0:m, 2 * P:4 * P], ACT.Copy).then_inc(v_out, 1)

                    evac_v(0)
                    evac_v(1)
                    for t in range(NT):
                        m = rows_of(t)
                        act.wait_ge(turned, h * NT + t + 1)
                        act.activation(qkT[:, :, 0:m], banks[2][:, 0:3 * P].rearrange("p (a i) -> p a i", a=3)[:, :, 0:m], ACT.Copy).then_inc(t_out, 1)
                        if t + 2 < NT:
                            evac_v(t + 2)
                        act.wait_ge(o_mm, h * NT + t + 1)
                        act.wait_ge(ss_mm, h * NT + t)
                        for f in range(DVT):
                            ins = act.activation(sq[:, f, 0:m], out_bank(t, f), ACT.Square)
                        ins.then_inc(sq_done, 1)
                        act.wait_ge(ms_done, h * NT + t + 1)
                        act.activation(rstd[:, 0:m], rstd[:, 0:m], ACT.Sqrt).then_inc(root_done, 1)

            @block.vector
            def _(dve):
                dve.wait_ge(tab_in, 16 * 11)
                with dve.Fori(0, RH) as h:
                    for p, (_, _, slot) in enumerate(ORDER):
                        dve.wait_ge(hi_done, h * PIECES + p + 1)
                        cols = slice(slot * P, (slot + 1) * P)
                        dve.tensor_tensor(wL[:, :, cols], raw[:, p % 2], wH[:, :, cols].bitcast(F32), ALU.subtract).then_inc(lo_done, 1)
                    for f in range(DVT):
                        dve.wait_ge(sg_done, h * 2 + f + 1)
                        for g in range(3):
                            cols = slice(g * TG, (g + 1) * TG)
                            ins = dve.tensor_tensor(gs[:, f, cols], banks[3 * f + g][:, 0:TG], gs[:, f, cols], ALU.mult)
                        ins.then_inc(g_done, 1)

                    def products(t):
                        m = rows_of(t)
                        x = banks[t % 2][0:m, 0:2 * P].rearrange("p (a d) -> p a d", a=4)
                        dve.wait_ge(v_out, h * NT + t + 1)
                        dve.wait_ge(rot_b, h * NT + t)
                        for dst, tab in ((ta, cos), (tb, sin)):
                            ins = dve.tensor_tensor(dst[0:m].rearrange("p a (s d) -> p (a s) d", s=2), x,
                                                    tab[0:m, t, :].rearrange("p (a d) -> p a d", a=1).broadcast_to([m, 4, half]), ALU.mult)
                        ins.then_inc(rot_a, 1)

                    products(0)
                    products(1)
                    for t in range(NT):
                        m = rows_of(t)
                        n = h * NT + t + 1
                        dve.wait_ge(s_mm, n)
                        dve.tensor_tensor(sT[0:m, 0:m], banks[3][0:m, 0:m],
                                          (decay if t < NB else sdecay)[0:m, ds(h, 1), 0:m].rearrange("p o i -> p (o i)"), ALU.mult).then_inc(s_out, 1)
                        if t + 2 < NT:
                            products(t + 2)
                        if t < NB:
                            dve.wait_ge(st_mm, h * NB + t + 1)
                            if t == 0:
                                dve.wait_ge(stored, h * 16)
                                dve.tensor_copy(S[:], banks[5][:, 0:DV]).then_inc(st_out, 1)
                            else:
                                dve.scalar_tensor_tensor(out=S[:], in0=S[:], scalar=cdec[:, ds(h, 1)], in1=banks[5][:, 0:DV],
                                                         op0=ALU.mult, op1=ALU.add).then_inc(st_out, 1)
                        else:
                            dve.wait_ge(s0_in, h * 16 + 16)
                            for b in range(DB + 1):
                                if b < DB:
                                    if b >= 2:
                                        dve.wait_ge(z_mm, h * DB + b - 1)
                                    dve.tensor_scalar(kmask[:, b % 2], rot[0:NS, t % 2, 2, :], skdec[:, b, ds(h, 1)], None, ALU.mult).then_inc(km_done, 1)
                                if b >= 1:
                                    dve.wait_ge(z_mm, h * DB + b)
                                    dve.scalar_tensor_tensor(out=S0[:, b - 1], in0=S0[:, b - 1], scalar=scdec[:, ds(h, 1)], in1=state_bank(b - 1),
                                                             op0=ALU.mult, op1=ALU.add).then_inc(s0_new, 1)
                        dve.wait_ge(sq_done, n)
                        dve.wait_ge(r_done, n - 1)
                        for f in range(DVT):
                            ins = dve.tensor_tensor(og[:, f, 0:m], out_bank(t, f), gs[:, f, t * P:t * P + m], ALU.mult)
                        ins.then_inc(og_done, 1)
                        dve.wait_ge(ss_mm, n)
                        dve.tensor_scalar(rstd[:, 0:m], banks[6][:, 0:m], 1.0 / DV, EPS, ALU.mult, ALU.add).then_inc(ms_done, 1)
                        dve.wait_ge(root_done, n)
                        dve.reciprocal(rstd[:, 0:m], rstd[:, 0:m]).then_inc(rstd_done, 1)
                        dve.wait_ge(rstd_done, n)
                        dve.wait_ge(og_done, n)
                        dve.tensor_tensor(ret[:, ds(h * DVT, DVT), t * P:t * P + m], og[:, :, 0:m],
                                          rstd[:, 0:m].rearrange("p (o i) -> p o i", o=1).broadcast_to([P, DVT, m]), ALU.mult).then_inc(r_done, 1)

            @block.tensor
            def _(pe):
                pe.wait_ge(tab_in, 16 * 11)
                with pe.Fori(0, RH) as h:
                    pe.wait_ge(v_out, h * NT)
                    pe.wait_ge(og_done, h * NT)
                    pe.wait_ge(sq_done, h * NT)
                    pe.wait_ge(s0_new, h * DB)
                    for f in range(DVT):
                        pe.wait_ge(lo_done, h * PIECES + f + 1)
                        w = [x[:, :, (4 + f) * P:(5 + f) * P] for x in (wH, wL)]
                        t_layout_product(pe, banks[3 * f:3 * f + 3], w, (ch.xH, ch.xL)).then_inc(g_mm, 1)

                    def project(t, ks):
                        m = rows_of(t)
                        if ks[0] == 0:
                            if t < 2:
                                pe.wait_ge(g_done, h * 2 + 1)
                            else:
                                pe.wait_ge(v_out, h * NT + t - 1)
                                pe.wait_ge(rot_a, h * NT + t - 1)
                        for k in ks:
                            mm = split_matmuls(pe, banks[t % 2][0:m, :], (ch.xH[:, k, t * P:t * P + m], ch.xL[:, k, t * P:t * P + m]),
                                               (wH[:, k, 0:4 * P], wL[:, k, 0:4 * P]), k == 0, k == KT - 1)
                        if ks[-1] == KT - 1:
                            mm.then_inc(p_mm, 1)

                    def sum_squares(t):
                        m = rows_of(t)
                        pe.wait_ge(sq_done, h * NT + t + 1)
                        pe.wait_ge(ms_done, h * NT + t)
                        for f in range(DVT):
                            mm = pe.matmul(banks[6][:, 0:m], ones[:], sq[:, f, 0:m], start=(f == 0), stop=(f == DVT - 1))
                        mm.then_inc(ss_mm, 1)

                    pe.wait_ge(lo_done, h * PIECES + PIECES)
                    project(0, range(KT))
                    project(1, range(KT))
                    pe.wait_ge(g_done, h * 2 + 2)
                    for t in range(NT):
                        m = rows_of(t)
                        n = h * NT + t + 1
                        pe.wait_ge(rot_done, n)
                        pe.wait_ge(t_out, n - 1)
                        if t == NB:
                            apart(pe, ch)
                        for a in range(3):
                            tr = pe.transpose(banks[2][:, a * P:a * P + m], rot[0:m, t % 2, a, :], ch.ident[0:m, 0:m])
                        tr.then_inc(turned, 1)
                        if t >= 1:
                            sum_squares(t - 1)
                        if t + 2 < NT:
                            project(t + 2, range(KT // 2))
                        pe.wait_ge(t_out, n)
                        pe.wait_ge(s_out, n - 1)
                        pe.matmul(banks[3][0:m, 0:m], qkT[:, 2, 0:m], qkT[:, 0, 0:m], start=True, stop=True).then_inc(s_mm, 1)
                        if t + 2 < NT:
                            project(t + 2, range(KT // 2, KT))
                        pe.wait_ge(s_out, n)
                        pe.wait_ge(v_out, n)
                        if t >= 2:
                            pe.wait_ge(og_done, n - 2 if t < NB else n - 1)
                            pe.wait_ge(sq_done, n - 2 if t < NB else n - 1)
                        if t < NB:
                            if t:
                                pe.wait_ge(st_out, h * NB + t)
                            for f in range(DVT):
                                cols = slice(f * P, (f + 1) * P)
                                mm = pe.matmul(out_bank(t, f), v[:, t % 3, cols], sT[:], start=True, stop=(t == 0))
                                if t:
                                    mm = pe.matmul(out_bank(t, f), S[:, cols], qkT[:, 1, :], start=False, stop=True)
                            mm.then_inc(o_mm, 1)
                            pe.matmul(banks[5][:, 0:DV], rot[:, t % 2, 3, :], v[:, t % 3], start=True, stop=True).then_inc(st_mm, 1)
                        else:
                            pe.wait_ge(s0_in, h * 16 + 16)
                            for f in range(DVT):
                                pe.matmul(out_bank(t, f), v[0:m, t % 3, f * P:(f + 1) * P], sT[0:m, 0:m], start=True, stop=False)
                                for b in range(DB):
                                    mm = pe.matmul(out_bank(t, f)[:, b * DL:(b + 1) * DL], S0[:, b, f * P:(f + 1) * P],
                                                   qkT[:, 1, b * DL:(b + 1) * DL], start=False, stop=(b == DB - 1))
                            mm.then_inc(o_mm, 1)
                            pe.wait_ge(st_out, h * NB + NB)
                            for b in range(DB):
                                if b >= 2:
                                    pe.wait_ge(s0_new, h * DB + b - 1)
                                pe.wait_ge(km_done, h * DB + b + 1)
                                pe.matmul(state_bank(b), kmask[:, b % 2], v[0:NS, t % 3], start=True, stop=True).then_inc(z_mm, 1)
                    sum_squares(NT - 1)


def stage_merge(nc, ch, ret):
    sem = ch.sem
    w_in, hi_done, lo_done, mm_done = [sem("m_w0"), sem("m_w1")], sem("m_hi"), sem("m_lo"), sem("m_mm")
    r_hi, r_lo, g_in, g_mul, sum_done, mh_done, ml_done = (
        sem("m_rhi"), sem("m_rlo"), [sem("m_g0"), sem("m_g1")], sem("m_gmul"), sem("m_sum"), sem("m_mh"), sem("m_ml"))
    with ExitStack() as st:
        sb = ch.sbuf(st)
        rH, rL = sb("m_rH", [P, KT, T], F32R), sb("m_rL", [P, KT, T], F32R)
        raw = sb("m_raw", [P, 2, KT, P])
        wH, wL = sb("m_wH", [P, 2, KT, P], F32R), sb("m_wL", [P, 2, KT, P], F32R)
        gate, m1 = sb("m_gate", [P, 1, T]), sb("m_m1", [P, 1, T])
        banks = ch.banks
        with nc.Block() as block:
            @block.sync
            def _(sp):
                with sp.Fori(0, KT // 2) as j:
                    for s in range(2):
                        m = j * 2 + s
                        sp.wait_ge(lo_done, j * 2)
                        apart(sp, ch)
                        sp.dma_start(raw[:, s], ch.w_ret[:, :, ds(m * P, P)]).then_inc(w_in[s], 16)

            @block.gpsimd
            def _(pool):
                with pool.Fori(0, KT) as m:
                    pool.wait_ge(ml_done, m)
                    apart(pool, ch)
                    pool.dma_start(gate[:, 0], ch.gate_t[:, ds(m, 1), :].rearrange("p o t -> p (o t)")).then_inc(g_in[0], 16)
                    pool.dma_start(m1[:, 0], ch.m1_t[:, ds(m, 1), :].rearrange("p o t -> p (o t)")).then_inc(g_in[1], 16)

            @block.scalar
            def _(act):
                for k in range(KT):
                    act.activation(rH[:, k, :], ret[:, k, :], ACT.Copy).then_inc(r_hi, 1)
                with act.Fori(0, KT // 2) as j:
                    for s in range(2):
                        act.wait_ge(w_in[s], j * 16 + 16)
                        act.wait_ge(mm_done, j * 2)
                        act.activation(wH[:, s], raw[:, s], ACT.Copy).then_inc(hi_done, 1)
                    for s in range(2):
                        m = j * 2 + s
                        act.wait_ge(sum_done, m + 1)
                        act.activation(ch.xH[:, ds(m, 1), :], gate[:], ACT.Copy).then_inc(mh_done, 1)

            @block.vector
            def _(dve):
                for k in range(KT):
                    dve.wait_ge(r_hi, k + 1)
                    dve.tensor_tensor(rL[:, k, :], ret[:, k, :], rH[:, k, :].bitcast(F32), ALU.subtract).then_inc(r_lo, 1)
                with dve.Fori(0, KT // 2) as j:
                    for s in range(2):
                        dve.wait_ge(hi_done, j * 2 + s + 1)
                        dve.tensor_tensor(wL[:, s], raw[:, s], wH[:, s].bitcast(F32), ALU.subtract).then_inc(lo_done, 1)
                    for s in range(2):
                        m = j * 2 + s
                        dve.wait_ge(mm_done, m + 1)
                        dve.wait_ge(g_in[0], m * 16 + 16)
                        dve.wait_ge(g_in[1], m * 16 + 16)
                        for g in range(3):
                            cols = slice(g * TG, (g + 1) * TG)
                            ins = dve.tensor_tensor(gate[:, 0, cols], banks[3 * s + g][:, 0:TG], gate[:, 0, cols], ALU.mult)
                        ins.then_inc(g_mul, 1)
                        dve.wait_ge(g_mul, m + 1)
                        dve.tensor_tensor(gate[:], gate[:], m1[:], ALU.add).then_inc(sum_done, 1)
                        dve.wait_ge(mh_done, m + 1)
                        dve.tensor_tensor(ch.xL[:, ds(m, 1), :], gate[:], ch.xH[:, ds(m, 1), :].bitcast(F32), ALU.subtract).then_inc(ml_done, 1)

            @block.tensor
            def _(pe):
                pe.wait_ge(r_lo, KT)
                with pe.Fori(0, KT // 2) as j:
                    for s in range(2):
                        pe.wait_ge(lo_done, j * 2 + s + 1)
                        pe.wait_ge(g_mul, j * 2)
                        t_layout_product(pe, banks[3 * s:3 * s + 3], (wH[:, s], wL[:, s]), (rH, rL)).then_inc(mm_done, 1)


def stage_out(nc, ch):
    sem = ch.sem
    w_in, hi_done, lo_done, mm_done, x_in = [sem("o_w0"), sem("o_w1")], sem("o_hi"), sem("o_lo"), sem("o_mm"), [sem("o_x0"), sem("o_x1")]
    tab_in, add_done, sq_done, ms_done, root_done, rstd_done, xn_done = (
        sem("o_tab"), sem("o_add"), sem("o_sq"), sem("o_ms"), sem("o_root"), sem("o_rstd"), sem("o_xn"))
    x2_st, xn_st, turned, t_out0, t_out1, r_mm, r_out = ([sem("o_x2s0"), sem("o_x2s1")], [sem("o_xns0"), sem("o_xns1")], sem("o_t"), sem("o_to0"), sem("o_to1"),
                                                        sem("o_rmm"), sem("o_rout"))
    NH = D // 512
    with ExitStack() as st:
        sb = ch.sbuf(st)
        raw = sb("o_raw", [P, 2, KT, P])
        wH, wL = sb("o_wH", [P, KT, D], F32R), sb("o_wL", [P, KT, D], F32R)
        xin, x2, xn = sb("o_xin", [P, 2, D]), sb("o_x2s", [P, 2, D]), sb("o_xns", [P, 2, D])
        junk, gain = sb("o_junk", [P, D]), sb("o_gain", [P, D])
        stat = sb("o_stat", [P, 2, 4])
        xT = sb("o_xT", [P, KT, P])
        wr, rb = sb("o_wr", [P, KT, NG + NE]), sb("o_rb", [P, NG + NE])
        banks = ch.banks
        with nc.Block() as block:
            @block.sync
            def _(sp):
                for q in range(KT):
                    if q >= 2:
                        sp.wait_ge(lo_done, q - 1)
                    sp.dma_start(raw[:, q % 2], ch.w_out[:, :, q * P:(q + 1) * P]).then_inc(w_in[q % 2], 16)
                for t in range(NT):
                    m, s = rows_of(t), t % 2
                    if t >= 2:
                        sp.wait_ge(add_done, t - 1)
                    src = ch.x_sample if t == NB else ch.x_prompt[t * P:(t + 1) * P, :]
                    sp.dma_start(xin[0:m, s], src).then_inc(x_in[s], 16)

            @block.gpsimd
            def _(pool):
                for dst, src in ((gain[:], ch.norm_ffn.broadcast_to([P, D])), (wr[:, :, 0:NG], ch.w_rg), (wr[:, :, NG:], ch.w_re),
                                 (rb[:, 0:NG], ch.b_rg.broadcast_to([P, NG])), (rb[:, NG:], ch.b_re.broadcast_to([P, NE]))):
                    pool.dma_start(dst, src).then_inc(tab_in, 16)
                for t in range(NT):
                    m, s = rows_of(t), t % 2
                    pool.wait_ge(add_done, t + 1)
                    pool.dma_start(ch.x2_d[t * P:t * P + m, :], x2[0:m, s]).then_inc(x2_st[s], 16)
                    pool.wait_ge(xn_done, t + 1)
                    pool.dma_start(ch.xn2_d[t * P:t * P + m, :], xn[0:m, s]).then_inc(xn_st[s], 16)
                for s in range(2):
                    n = 16 * ((NT + 1 - s) // 2)
                    pool.wait_ge(x2_st[s], n)
                    pool.wait_ge(xn_st[s], n)

            @block.scalar
            def _(act):
                for q in range(KT):
                    act.wait_ge(w_in[q % 2], 16 * (q // 2 + 1))
                    act.activation(wH[:, :, q * P:(q + 1) * P], raw[:, q % 2], ACT.Copy).then_inc(hi_done, 1)

                def front(t):
                    m, s = rows_of(t), t % 2
                    act.wait_ge(add_done, t + 1)
                    act.activation(junk[0:m], x2[0:m, s], ACT.Square, accum_out=stat[0:m, s, 0:1]).then_inc(sq_done, 1)
                    act.wait_ge(ms_done, t + 1)
                    act.activation(stat[0:m, s, 2:3], stat[0:m, s, 1:2], ACT.Sqrt).then_inc(root_done, 1)

                def back(t):
                    m = rows_of(t)
                    act.wait_ge(turned, t * 2 + 1)
                    act.activation(xT[:, 0:4, 0:m], banks[4][:].rearrange("p (k i) -> p k i", k=4)[:, :, 0:m], ACT.Copy).then_inc(t_out0, 1)

                for t in range(NT + 1):
                    if t < NT:
                        front(t)
                    if t >= 1:
                        back(t - 1)

            @block.vector
            def _(dve):
                dve.memset(ch.logits[:], 0.0).then_inc(r_out, 1)
                for q in range(KT):
                    dve.wait_ge(hi_done, q + 1)
                    cols = slice(q * P, (q + 1) * P)
                    dve.tensor_tensor(wL[:, :, cols], raw[:, q % 2], wH[:, :, cols].bitcast(F32), ALU.subtract).then_inc(lo_done, 1)
                dve.wait_ge(tab_in, 16 * 5)

                def front(t):
                    m, s = rows_of(t), t % 2
                    dve.wait_ge(mm_done, t + 1)
                    dve.wait_ge(x_in[s], 16 * (t // 2 + 1))
                    if t >= 2:
                        dve.wait_ge(x2_st[s], 16 * (t // 2))
                        dve.wait_ge(sq_done, t - 1)
                    for f in range(NH):
                        cols = slice(f * 512, (f + 1) * 512)
                        ins = dve.tensor_tensor(x2[0:m, s, cols], banks[2 * s + f][0:m, :], xin[0:m, s, cols], ALU.add)
                    ins.then_inc(add_done, 1)
                    dve.wait_ge(sq_done, t + 1)
                    dve.tensor_scalar(stat[0:m, s, 1:2], stat[0:m, s, 0:1], 1.0 / D, EPS, ALU.mult, ALU.add).then_inc(ms_done, 1)
                    dve.wait_ge(root_done, t + 1)
                    dve.reciprocal(stat[0:m, s, 3:4], stat[0:m, s, 2:3]).then_inc(rstd_done, 1)
                    dve.wait_ge(rstd_done, t + 1)
                    if t >= 2:
                        dve.wait_ge(xn_st[s], 16 * (t // 2))
                        dve.wait_ge(turned, 2 * (t - 1))
                    dve.scalar_tensor_tensor(out=xn[0:m, s], in0=x2[0:m, s], scalar=stat[0:m, s, 3:4], in1=gain[0:m],
                                             op0=ALU.mult, op1=ALU.mult).then_inc(xn_done, 1)

                def back(t):
                    m = rows_of(t)
                    dve.wait_ge(turned, t * 2 + 2)
                    dve.tensor_copy(xT[:, 4:8, 0:m], banks[5][:].rearrange("p (k i) -> p k i", k=4)[:, :, 0:m]).then_inc(t_out1, 1)
                    dve.wait_ge(r_mm, t + 1)
                    dve.wait_ge(r_out, 1)
                    dve.tensor_tensor(ch.logits[0:m, t, :], banks[6][0:m, 0:NG + NE], rb[0:m, :], ALU.add).then_inc(r_out, 1)

                for t in range(NT + 1):
                    if t < NT:
                        front(t)
                    if t >= 1:
                        back(t - 1)

            @block.tensor
            def _(pe):
                def project(t):
                    m, s = rows_of(t), t % 2
                    if t >= 2:
                        pe.wait_ge(add_done, t - 1)
                    for f in range(NH):
                        for k in range(KT):
                            rows, cols = slice(t * P, t * P + m), slice(f * 512, (f + 1) * 512)
                            mm = split_matmuls(pe, banks[2 * s + f][0:m, :], (ch.xH[:, k, rows], ch.xL[:, k, rows]),
                                               (wH[:, k, cols], wL[:, k, cols]), k == 0, k == KT - 1)
                    mm.then_inc(mm_done, 1)

                def route(t):
                    m, s = rows_of(t), t % 2
                    pe.wait_ge(xn_done, t + 1)
                    pe.wait_ge(t_out0, t)
                    pe.wait_ge(t_out1, t)
                    for b in range(2):
                        for k in range(4):
                            tr = pe.transpose(banks[4 + b][:, k * P:k * P + m], xn[0:m, s, (4 * b + k) * P:(4 * b + k + 1) * P], ch.ident[0:m, 0:m])
                        tr.then_inc(turned, 1)
                    pe.wait_ge(t_out0, t + 1)
                    pe.wait_ge(t_out1, t + 1)
                    pe.wait_ge(r_out, t + 1)
                    for k in range(KT):
                        mm = pe.matmul(banks[6][0:m, 0:NG + NE], xT[:, k, 0:m], wr[:, k, :], start=(k == 0), stop=(k == KT - 1))
                    mm.then_inc(r_mm, 1)

                pe.wait_ge(tab_in, 16 * 5)
                pe.wait_ge(lo_done, KT)
                for t in range(NT + 1):
                    if t < NT:
                        project(t)
                    if t >= 1:
                        route(t - 1)


def stage_route(nc, ch):
    sem = ch.sem
    step, tab_in, e_done, c_mm, scat, zeroed = sem("t_step"), sem("t_tab"), sem("t_exp"), sem("t_mm"), sem("t_scat"), sem("t_zero")
    with ExitStack() as st:
        sb = ch.sbuf(st)
        iota = sb("t_iota", [P, P])
        before, ones = sb("t_before", [P, P]), sb("t_ones", [P, P])
        tokens = sb("t_tokens", [P, NT], I32)
        noexp = sb("t_noexp", [P, NT])
        g8, gm8, f8, fm8 = (sb("t_" + n, [P, NT, 8]) for n in ("g8", "gm8", "f8", "fm8"))
        gi8, fi8 = sb("t_gi8", [P, NT, 8], U32), sb("t_fi8", [P, NT, 8], U32)
        gidx, gw, e2, den = (sb("t_" + n, [P, NT]) for n in ("gidx", "gw", "e2", "den"))
        eg, goh = sb("t_eg", [P, NT, NG]), sb("t_goh", [P, NT, NG])
        prod = sb("t_prod", [P, NT, EPG, NG])
        eid = sb("t_eid", [P, NT, 2])
        hot = sb("t_hot", [P, NT, 2, NE])
        both, tot, before_t, slotv, over = (sb("t_" + n, [P, NT, NE]) for n in ("both", "tot", "tp", "slotv", "over"))
        cnt, nov, delta, scan = sb("t_cnt", [P, NE]), sb("t_nov", [P, NE]), sb("t_delta", [P, NE]), sb("t_scan", [P, 2, NE])
        thr, cmp = sb("t_thr", [P, MAXBLK - 1]), sb("t_cmp", [P, NE, MAXOVER])
        slotp, slotf = sb("t_slotp", [P, NT, 2, NE]), sb("t_slotf", [P, NT, 2])
        tabf = sb("t_tabf", [P, 1 + MAXOVER])
        banks = ch.banks

        def across(ap, n):
            return ap.rearrange("p (a o) -> p a o", o=1).broadcast_to([P, ap.shape[1], n])

        with nc.Block() as block:
            @block.sync
            def _(sp):
                for dst, name in ((iota, "iota"), (before, "before"), (ones, "ones"), (tokens, "tokens"), (noexp, "no_expert")):
                    sp.dma_start(dst[:], ch.c[name]).then_inc(tab_in, 16)
                sp.dma_start(ch.toktab.rearrange("(b p) o -> b (p o)", p=P), ch.c["zero_slots"]).then_inc(zeroed, 16)

            @block.scalar
            def _(act):
                act.wait_ge(step, ch.route_steps["group"])
                act.activation(eg[:], eg[:], ACT.Exp).then_inc(e_done, 1)
                act.wait_ge(step, ch.route_steps["pair"])
                act.activation(e2[:], e2[:], ACT.Exp).then_inc(e_done, 1)

            @block.vector
            def _(dve):
                count = [0]

                def done(ins):
                    ins.then_inc(step, 1)
                    count[0] += 1
                    dve.wait_ge(step, count[0])

                dve.wait_ge(tab_in, 16 * 5)
                LG = ch.logits
                done(dve.memset(g8[:], -3e38))
                done(dve.tensor_copy(g8[:, :, 0:NG], LG[:, :, 0:NG]))
                for t in range(NT):
                    done(dve.max(gm8[:, t, :], g8[:, t, :]))
                    done(dve.max_index(gi8[:, t, :], gm8[:, t, :], g8[:, t, :]))
                done(dve.tensor_tensor(eg[:], LG[:, :, 0:NG], gm8[:, :, 0:1].broadcast_to([P, NT, NG]), ALU.subtract))
                assert count[0] == ch.route_steps["group"]
                done(dve.tensor_copy(gidx[:], gi8[:, :, 0]))
                done(dve.tensor_tensor(goh[:], across(gidx[:], NG), iota[:, None, 0:NG].broadcast_to([P, NT, NG]), ALU.is_equal))
                done(dve.tensor_tensor(prod[:], LG[:, :, NG:].rearrange("p t (g e) -> p t e g", g=NG),
                                       goh[:].rearrange("p t (o g) -> p t o g", o=1).broadcast_to([P, NT, EPG, NG]), ALU.mult))
                done(dve.tensor_reduce(f8[:], prod[:], AX, ALU.add))
                for t in range(NT):
                    done(dve.max(fm8[:, t, :], f8[:, t, :]))
                    done(dve.max_index(fi8[:, t, :], fm8[:, t, :], f8[:, t, :]))
                done(dve.tensor_tensor(e2[:], fm8[:, :, 1], fm8[:, :, 0], ALU.subtract))
                assert count[0] == ch.route_steps["pair"]
                done(dve.tensor_copy(eid[:], fi8[:, :, 0:2]))
                done(dve.scalar_tensor_tensor(out=gidx[:], in0=gidx[:], scalar=float(EPG), in1=noexp[:], op0=ALU.mult, op1=ALU.add))
                done(dve.tensor_tensor(eid[:], eid[:], across(gidx[:], 2), ALU.add))
                done(dve.tensor_tensor(hot[:].rearrange("p t k e -> p (t k) e"), across(eid[:].rearrange("p t k -> p (t k)"), NE),
                                       iota[:, None, 0:NE].broadcast_to([P, 2 * NT, NE]), ALU.is_equal))
                done(dve.tensor_tensor(both[:], hot[:, :, 0, :], hot[:, :, 1, :], ALU.add))
                assert count[0] == ch.route_steps["hot"]
                dve.wait_ge(e_done, 2)
                done(dve.tensor_reduce(den[:], eg[:], AX, ALU.add))
                done(dve.reciprocal(gw[:], den[:]))
                done(dve.tensor_scalar(den[:], e2[:], 1.0, None, ALU.add))
                done(dve.reciprocal(den[:], den[:]))
                done(dve.tensor_tensor(ch.gates[:, :, 0], gw[:], den[:], ALU.mult))
                done(dve.tensor_tensor(ch.gates[:, :, 1], ch.gates[:, :, 0], e2[:], ALU.mult))
                dve.wait_ge(c_mm, 1)
                done(dve.tensor_copy(tot[:], banks[1][:, 0:NT * NE].rearrange("p (t e) -> p t e", t=NT)))
                done(dve.memset(before_t[:, 0, :], 0.0))
                for t in range(1, NT):
                    done(dve.tensor_tensor(before_t[:, t, :], before_t[:, t - 1, :], tot[:, t - 1, :], ALU.add))
                done(dve.tensor_tensor(cnt[:], before_t[:, NT - 1, :], tot[:, NT - 1, :], ALU.add))
                done(dve.tensor_tensor(slotv[:], banks[0][:, 0:NT * NE].rearrange("p (t e) -> p t e", t=NT), before_t[:], ALU.add))
                done(dve.tensor_scalar(thr[:], iota[:, 1:MAXBLK], float(P), None, ALU.mult))
                done(dve.tensor_tensor(cmp[:, :, 0:MAXBLK - 1], across(cnt[:], MAXBLK - 1), thr[:, None, :].broadcast_to([P, NE, MAXBLK - 1]), ALU.is_gt))
                done(dve.tensor_reduce(nov[:], cmp[:, :, 0:MAXBLK - 1], AX, ALU.add))
                done(dve.tensor_copy(scan[:, 0, :], nov[:]))
                a, sh = 0, 1
                while sh < NE:
                    done(dve.tensor_copy(scan[:, 1 - a, 0:sh], scan[:, a, 0:sh]))
                    done(dve.tensor_tensor(scan[:, 1 - a, sh:NE], scan[:, a, sh:NE], scan[:, a, 0:NE - sh], ALU.add))
                    a, sh = 1 - a, sh * 2
                end = scan[:, a, :]
                done(dve.tensor_tensor(delta[:], end, nov[:], ALU.subtract))
                done(dve.tensor_tensor(delta[:], delta[:], iota[:, 0:NE], ALU.subtract))
                done(dve.tensor_scalar(delta[:], delta[:], float(NE - 1), float(P), ALU.add, ALU.mult))
                done(dve.tensor_scalar(over[:], slotv[:], float(P), None, ALU.is_ge))
                done(dve.tensor_tensor(over[:], over[:], delta[:, None, :].broadcast_to([P, NT, NE]), ALU.mult))
                done(dve.tensor_tensor(slotv[:], slotv[:], over[:], ALU.add))
                done(dve.tensor_scalar(delta[:], iota[:, 0:NE], float(P), None, ALU.mult))
                done(dve.tensor_tensor(slotv[:], slotv[:], delta[:, None, :].broadcast_to([P, NT, NE]), ALU.add))
                for k in range(2):
                    done(dve.tensor_tensor(slotp[:, :, k, :], hot[:, :, k, :], slotv[:], ALU.mult))
                done(dve.tensor_reduce(slotf[:], slotp[:], AX, ALU.add))
                done(dve.tensor_copy(ch.slots[:], slotf[:]))
                assert count[0] == ch.route_steps["slots"]
                done(dve.tensor_copy(tabf[:, 0:1], scan[:, a, NE - 1:NE]))
                done(dve.tensor_tensor(cmp[:].rearrange("p e j -> p (e j)").rearrange("p (j e) -> p j e", e=NE),
                                       scan[:, a:a + 1, :].broadcast_to([P, MAXOVER, NE]), across(iota[:, 0:MAXOVER], NE), ALU.is_le))
                done(dve.tensor_reduce(tabf[:, 1:], cmp[:].rearrange("p e j -> p (e j)").rearrange("p (j e) -> p j e", e=NE), AX, ALU.add))
                done(dve.tensor_scalar(tabf[:, 1:], tabf[:, 1:], float(NE - 1), None, ALU.min))
                done(dve.tensor_copy(ch.beyond[:], tabf[0:1, :]))

            @block.tensor
            def _(pe):
                pe.wait_ge(tab_in, 16 * 5)
                pe.wait_ge(step, ch.route_steps["hot"])
                flat = both[:].rearrange("p t e -> p (t e)")
                pe.matmul(banks[0][:, 0:NT * NE], before[:], flat, start=True, stop=True)
                pe.matmul(banks[1][:, 0:NT * NE], ones[:], flat, start=True, stop=True).then_inc(c_mm, 1)

            @block.gpsimd
            def _(pool):
                pool.wait_ge(tab_in, 16 * 5)
                pool.wait_ge(zeroed, 16)
                pool.wait_ge(step, ch.route_steps["slots"])
                for t in range(NT):
                    m = rows_of(t)
                    for k in range(2):
                        pool.indirect_dma_start(out=ch.toktab, out_offset=bass.IndirectOffsetOnAxis(ap=ch.slots[0:m, t, k:k + 1], axis=0),
                                                in_=tokens[0:m, t:t + 1], in_offset=None).then_inc(scat, 16)
                pool.wait_ge(scat, 16 * 2 * NT)


def stage_experts(nc, ch):
    sem = ch.sem
    NQ = 4
    w_in = {kind: [sem(f"e_w{kind}{q}") for q in range(NQ)] for kind in "gud"}
    w_hi, w_lo, used = ({kind: sem(f"e_{n}{kind}") for kind in "gud"} for n in ("hi", "lo", "use"))
    idx_in, rows_in, x_turned, x_hi, x_lo = sem("e_idx"), sem("e_rows"), sem("e_xt"), sem("e_xhi"), sem("e_xlo")
    sig, mul, h_done, h_turned, h_hi, h_lo, y_a, y_b, y_st, go = (
        sem("e_sig"), sem("e_mul"), sem("e_h"), sem("e_ht"), sem("e_hhi"), sem("e_hlo"), sem("e_ya"), sem("e_yb"), sem("e_yst"), sem("e_go"))
    with ExitStack() as st:
        sb = ch.sbuf(st)
        raw = {k: sb(f"e_raw{k}", [P, NQ, 1024]) for k in "gud"}
        H = {k: sb(f"e_H{k}", [P, NQ, 1024], F32R) for k in "gud"}
        L = {k: sb(f"e_L{k}", [P, NQ, 1024], F32R) for k in "gud"}
        idx = sb("e_idxs", [P, 1], I32)
        rows = sb("e_rowss", [P, D])
        xH, xL = sb("e_xH", [P, KT, P], F32R), sb("e_xL", [P, KT, P], F32R)
        hH, hL = sb("e_hH", [P, FT, P], F32R), sb("e_hL", [P, FT, P], F32R)
        sg, h = sb("e_sg", [P, FF]), sb("e_hs", [P, FF])
        y = sb("e_y", [P, D])
        banks = ch.banks
        XT, G, U, HT, Y = banks[0:2], banks[2], banks[3], banks[4], banks[5:7]

        def src(kind, e, q):
            if kind == "d":
                return ch.w_down[ds(e, 1)].rearrange("o (k p) n -> p (o k) n", p=P)[:, q, :]
            w = {"g": ch.w_gate, "u": ch.w_up}[kind]
            return w[ds(e, 1)].rearrange("o (k p) n -> p (o k) n", p=P)[:, 2 * q:2 * q + 2, :]

        def walk(eng, body):
            body(0, True, 2)
            with eng.Fori(1, NE - 2) as e:
                body(e, False, 2)
            body(NE - 2, False, 1)
            body(NE - 1, False, 0)

        with nc.Block() as block:
            @block.sync
            def _(sp):
                def load(kind, e, first=False):
                    for q in range(NQ):
                        if not first:
                            sp.wait_ge(w_lo[kind], (e - 1) * NQ + q + 1)
                        dst = raw[kind][:, q]
                        if kind != "d":
                            dst = dst.rearrange("p (k n) -> p k n", k=2)
                        sp.dma_start(dst, src(kind, e, q)).then_inc(w_in[kind][q], 16)

                def body(e, first, left):
                    if not first:
                        load("d", e)
                    if left >= 2:
                        load("g", e + 2)
                        load("u", e + 2)

                for kind in "gud":
                    load(kind, 0, True)
                for kind in "gu":
                    load(kind, 1)
                walk(sp, body)

            @block.gpsimd
            def _(pool):
                def gather(e):
                    pool.wait_ge(x_turned, e * 2)
                    apart(pool, ch)
                    pool.dma_start(idx[:], ch.toktab[ds(e * P, P), :]).then_inc(idx_in, 16)
                    pool.wait_ge(idx_in, e * 16 + 16)
                    apart(pool, ch)
                    pool.indirect_dma_start(out=rows[:], out_offset=None, in_=ch.xn2_d,
                                            in_offset=bass.IndirectOffsetOnAxis(ap=idx[:, 0:1], axis=0)).then_inc(rows_in, 16)

                def store(e):
                    pool.wait_ge(y_a, e + 1)
                    pool.wait_ge(y_b, e + 1)
                    apart(pool, ch)
                    pool.dma_start(ch.y_d[ds(e * P, P), :], y[:]).then_inc(y_st, 16)

                def body(e, first, left):
                    if left >= 1:
                        gather(e + 1)
                    if not first:
                        store(e - 1)

                pool.memset(idx[:], 0).then_inc(go, 1)
                pool.wait_ge(go, 1)
                gather(0)
                walk(pool, body)
                store(NE - 1)
                pool.wait_ge(y_st, 16 * NE)

            @block.scalar
            def _(act):
                def split_hi(kind, e):
                    for q in range(NQ):
                        act.wait_ge(w_in[kind][q], e * 16 + 16)
                        act.wait_ge(used[kind], e * NQ + q + 1)
                        act.activation(H[kind][:, q], raw[kind][:, q], ACT.Copy).then_inc(w_hi[kind], 1)

                def rows_hi(e):
                    for b in range(2):
                        act.wait_ge(x_turned, e * 2 + b + 1)
                        act.activation(xH[:, 4 * b:4 * b + 4].rearrange("p k i -> p (k i)"), XT[b][:], ACT.Copy).then_inc(x_hi, 1)

                def hidden_hi(e):
                    act.wait_ge(h_turned, e + 1)
                    act.activation(hH[:].rearrange("p k i -> p (k i)"), HT[:], ACT.Copy).then_inc(h_hi, 1)

                def gate_sigmoid(e):
                    act.wait_ge(used["g"], e * NQ + 2 * NQ)
                    act.wait_ge(h_done, e)
                    act.activation(sg[:], G[:], ACT.Sigmoid).then_inc(sig, 1)

                def out_evac(e):
                    act.wait_ge(used["d"], e * NQ + 2 * NQ)
                    act.wait_ge(y_st, e * 16)
                    act.activation(y[:, 0:512], Y[0][:], ACT.Copy).then_inc(y_a, 1)

                def body(e, first, left):
                    if not first:
                        split_hi("d", e - 1)
                        hidden_hi(e - 1)
                    if left >= 1:
                        split_hi("g", e + 1)
                        rows_hi(e + 1)
                    gate_sigmoid(e)
                    if left >= 1:
                        split_hi("u", e + 1)
                    if not first:
                        out_evac(e - 1)

                split_hi("g", 0)
                rows_hi(0)
                split_hi("u", 0)
                walk(act, body)
                split_hi("d", NE - 1)
                hidden_hi(NE - 1)
                out_evac(NE - 1)

            @block.vector
            def _(dve):
                def split_lo(kind, e):
                    for q in range(NQ):
                        dve.wait_ge(w_hi[kind], e * NQ + q + 1)
                        dve.tensor_tensor(L[kind][:, q], raw[kind][:, q], H[kind][:, q].bitcast(F32), ALU.subtract).then_inc(w_lo[kind], 1)

                def rows_lo(e):
                    for b in range(2):
                        dve.wait_ge(x_hi, e * 2 + b + 1)
                        cols = slice(4 * b, 4 * b + 4)
                        dve.tensor_tensor(xL[:, cols].rearrange("p k i -> p (k i)"), XT[b][:], xH[:, cols].rearrange("p k i -> p (k i)").bitcast(F32),
                                          ALU.subtract).then_inc(x_lo, 1)

                def hidden_lo(e):
                    dve.wait_ge(h_hi, e + 1)
                    dve.tensor_tensor(hL[:].rearrange("p k i -> p (k i)"), HT[:], hH[:].rearrange("p k i -> p (k i)").bitcast(F32),
                                      ALU.subtract).then_inc(h_lo, 1)

                def hidden(e):
                    dve.wait_ge(sig, e + 1)
                    dve.wait_ge(h_turned, e)
                    dve.tensor_tensor(h[:], G[:], sg[:], ALU.mult).then_inc(mul, 1)
                    dve.wait_ge(mul, e + 1)
                    dve.wait_ge(used["u"], e * NQ + 2 * NQ)
                    dve.tensor_tensor(h[:], U[:], h[:], ALU.mult).then_inc(h_done, 1)

                def out_evac(e):
                    dve.wait_ge(used["d"], e * NQ + 2 * NQ)
                    dve.wait_ge(y_st, e * 16)
                    dve.tensor_copy(y[:, 512:1024], Y[1][:]).then_inc(y_b, 1)

                def body(e, first, left):
                    if not first:
                        split_lo("d", e - 1)
                        hidden_lo(e - 1)
                    if left >= 1:
                        split_lo("g", e + 1)
                        rows_lo(e + 1)
                    hidden(e)
                    if left >= 1:
                        split_lo("u", e + 1)
                    if not first:
                        out_evac(e - 1)

                split_lo("g", 0)
                rows_lo(0)
                split_lo("u", 0)
                walk(dve, body)
                split_lo("d", NE - 1)
                hidden_lo(NE - 1)
                out_evac(NE - 1)

            @block.tensor
            def _(pe):
                def product(kind, out, e):
                    for q in range(NQ):
                        pe.wait_ge(w_lo[kind], e * NQ + q + 1)
                        for k2 in range(2):
                            k, cols = 2 * q + k2, slice(k2 * 512, (k2 + 1) * 512)
                            mm = split_matmuls(pe, out[:], (xH[:, k, :], xL[:, k, :]), (H[kind][:, q, cols], L[kind][:, q, cols]), k == 0, k == KT - 1)
                        mm.then_inc(used[kind], 1)

                def down(e):
                    pe.wait_ge(h_lo, e + 1)
                    pe.wait_ge(y_a, e)
                    pe.wait_ge(y_b, e)
                    for q in range(NQ):
                        pe.wait_ge(w_lo["d"], e * NQ + q + 1)
                        for f in range(2):
                            cols = slice(f * 512, (f + 1) * 512)
                            mm = split_matmuls(pe, Y[f][:], (hH[:, q, :], hL[:, q, :]), (H["d"][:, q, cols], L["d"][:, q, cols]), q == 0, q == NQ - 1)
                        mm.then_inc(used["d"], 1)

                def turn_rows(e):
                    pe.wait_ge(rows_in, e * 16 + 16)
                    pe.wait_ge(x_lo, e * 2)
                    for b in range(2):
                        for k in range(4):
                            tr = pe.transpose(XT[b][:, k * P:(k + 1) * P], rows[:, (4 * b + k) * P:(4 * b + k + 1) * P], ch.ident[:])
                        tr.then_inc(x_turned, 1)

                def turn_hidden(e):
                    pe.wait_ge(h_done, e + 1)
                    pe.wait_ge(h_lo, e)
                    for k in range(FT):
                        tr = pe.transpose(HT[:, k * P:(k + 1) * P], h[:, k * P:(k + 1) * P], ch.ident[:])
                    tr.then_inc(h_turned, 1)

                def body(e, first, left):
                    pe.wait_ge(x_lo, e * 2 + 2)
                    pe.wait_ge(h_done, e)
                    product("g", G, e)
                    if not first:
                        turn_hidden(e - 1)
                    product("u", U, e)
                    if left >= 1:
                        turn_rows(e + 1)
                    if not first:
                        down(e - 1)

                for kind in "gud":
                    pe.sem_inc(used[kind], NQ)
                turn_rows(0)
                walk(pe, body)
                turn_hidden(NE - 1)
                down(NE - 1)


def stage_beyond(nc, ch):
    sem = ch.sem
    w_in, idx_in, rows_in, x_turned, x_out, g_mm, u_mm, sig, mul, h_done, h_turned, h_out, d_mm, y_out, y_st, go = (
        sem("v_" + n) for n in ("w", "idx", "rows", "xt", "xo", "g", "u", "sig", "mul", "h", "ht", "ho", "d", "y", "yst", "go"))
    with ExitStack() as st:
        sb = ch.sbuf(st)
        wg, wu = sb("v_wg", [P, KT, FF]), sb("v_wu", [P, KT, FF])
        wd = sb("v_wd", [P, FT, D])
        idx = sb("v_idx_s", [P, 1], I32)
        rows, xT = sb("v_rows_s", [P, D]), sb("v_xT", [P, KT, P])
        sg, h, hT = sb("v_sg", [P, FF]), sb("v_h_s", [P, FF]), sb("v_hT", [P, FT, P])
        y = sb("v_y_s", [P, D])
        banks = ch.banks

        def each(eng, body):
            n = eng.value_load(ch.beyond[0:1, 0:1], min_val=0, max_val=MAXOVER)
            with eng.If(n > 0):
                with eng.Fori(0, n) as j:
                    body(j)

        with nc.Block() as block:
            @block.sync
            def _(sp):
                def body(j):
                    sp.wait_ge(d_mm, j)
                    e = sp.value_load(ch.beyond[0:1, ds(j + 1, 1)], min_val=0, max_val=NE - 1)
                    for dst, w in ((wg, ch.w_gate), (wu, ch.w_up), (wd, ch.w_down)):
                        sp.dma_start(dst[:], w[ds(e, 1)].rearrange("o (k p) n -> p (o k) n", p=P)).then_inc(w_in, 16)
                each(sp, body)

            @block.gpsimd
            def _(pool):
                def body(j):
                    pool.wait_ge(y_st, j * 16)
                    apart(pool, ch)
                    pool.dma_start(idx[:], ch.toktab[ds(j * P + NE * P, P), :]).then_inc(idx_in, 16)
                    pool.wait_ge(idx_in, j * 16 + 16)
                    apart(pool, ch)
                    pool.indirect_dma_start(out=rows[:], out_offset=None, in_=ch.xn2_d,
                                            in_offset=bass.IndirectOffsetOnAxis(ap=idx[:, 0:1], axis=0)).then_inc(rows_in, 16)
                    pool.wait_ge(y_out, j + 1)
                    apart(pool, ch)
                    pool.dma_start(ch.y_d[ds(j * P + NE * P, P), :], y[:]).then_inc(y_st, 16)
                    pool.wait_ge(y_st, j * 16 + 16)
                pool.memset(idx[:], 0).then_inc(go, 1)
                pool.wait_ge(go, 1)
                each(pool, body)

            @block.scalar
            def _(act):
                def body(j):
                    act.wait_ge(x_turned, j + 1)
                    for b in range(2):
                        ins = act.activation(xT[:, 4 * b:4 * b + 4].rearrange("p k i -> p (k i)"), banks[b][:], ACT.Copy)
                    ins.then_inc(x_out, 1)
                    act.wait_ge(u_mm, j + 1)
                    act.activation(sg[:], banks[2][:], ACT.Sigmoid).then_inc(sig, 1)
                    act.wait_ge(h_turned, j + 1)
                    act.activation(hT[:].rearrange("p k i -> p (k i)"), banks[4][:], ACT.Copy).then_inc(h_out, 1)
                    act.wait_ge(d_mm, j + 1)
                    act.wait_ge(y_st, j * 16)
                    for f in range(2):
                        ins = act.activation(y[:, f * 512:(f + 1) * 512], banks[5 + f][:], ACT.Copy)
                    ins.then_inc(y_out, 1)
                each(act, body)

            @block.vector
            def _(dve):
                def body(j):
                    dve.wait_ge(sig, j + 1)
                    dve.tensor_tensor(h[:], banks[2][:], sg[:], ALU.mult).then_inc(mul, 1)
                    dve.wait_ge(mul, j + 1)
                    dve.tensor_tensor(h[:], banks[3][:], h[:], ALU.mult).then_inc(h_done, 1)
                each(dve, body)

            @block.tensor
            def _(pe):
                def body(j):
                    pe.wait_ge(rows_in, j * 16 + 16)
                    for k in range(KT):
                        tr = pe.transpose(banks[k // 4][:, (k % 4) * P:(k % 4 + 1) * P], rows[:, k * P:(k + 1) * P], ch.ident[:])
                    tr.then_inc(x_turned, 1)
                    pe.wait_ge(x_out, j + 1)
                    pe.wait_ge(w_in, j * 48 + 48)
                    for bank, w, done in ((banks[2], wg, g_mm), (banks[3], wu, u_mm)):
                        for k in range(KT):
                            mm = pe.matmul(bank[:], xT[:, k, :], w[:, k, :], start=(k == 0), stop=(k == KT - 1))
                        mm.then_inc(done, 1)
                    pe.wait_ge(h_done, j + 1)
                    for k in range(FT):
                        tr = pe.transpose(banks[4][:, k * P:(k + 1) * P], h[:, k * P:(k + 1) * P], ch.ident[:])
                    tr.then_inc(h_turned, 1)
                    pe.wait_ge(h_out, j + 1)
                    pe.wait_ge(y_out, j)
                    for f in range(2):
                        for k in range(FT):
                            mm = pe.matmul(banks[5 + f][:], hT[:, k, :], wd[:, k, f * 512:(f + 1) * 512], start=(k == 0), stop=(k == FT - 1))
                    mm.then_inc(d_mm, 1)
                each(pe, body)


def stage_combine(nc, ch):
    sem = ch.sem
    AHEAD = 4
    g_in, y_in, x_in, m_done, a_done, sq_done, ms_done, root_done, rstd_done, o_done, o_st = (
        sem("c_gain"), [sem(f"c_y{s}") for s in range(AHEAD)], [sem(f"c_x{s}") for s in range(AHEAD)], sem("c_m"), sem("c_a"), sem("c_sq"), sem("c_ms"), sem("c_root"),
        sem("c_rstd"), sem("c_o"), [sem("c_st0"), sem("c_st1")])
    with ExitStack() as st:
        sb = ch.sbuf(st)
        Y, x2, o = sb("c_Y", [P, AHEAD, 2, D]), sb("c_x2s", [P, AHEAD, D]), sb("c_os", [P, 2, D])
        junk, gain, stat = sb("c_junk", [P, D]), sb("c_gains", [P, D]), sb("c_stat", [P, 2, 4])
        with nc.Block() as block:
            @block.sync
            def _(sp):
                sp.dma_start(gain[:], ch.norm_final.broadcast_to([P, D])).then_inc(g_in, 16)
                for t in range(NT):
                    m, s = rows_of(t), t % AHEAD
                    if t >= AHEAD:
                        sp.wait_ge(m_done, t - AHEAD + 1)
                    sp.dma_start(x2[0:m, s], ch.x2_d[t * P:t * P + m, :]).then_inc(x_in[s], 16)

            @block.gpsimd
            def _(pool):
                for t in range(NT):
                    m, s = rows_of(t), t % AHEAD
                    if t >= AHEAD:
                        pool.wait_ge(o_done, t - AHEAD + 1)
                    for k in range(2):
                        pool.indirect_dma_start(out=Y[0:m, s, k, :], out_offset=None, in_=ch.y_d,
                                                in_offset=bass.IndirectOffsetOnAxis(ap=ch.slots[0:m, t, k:k + 1], axis=0)).then_inc(y_in[s], 16)

            @block.scalar
            def _(act):
                def store(t):
                    m, s = rows_of(t), t % 2
                    act.wait_ge(o_done, t + 1)
                    dst = ch.y_sample if t == NB else ch.y_prompt[t * P:(t + 1) * P, :]
                    act.dma_start(dst, o[0:m, s]).then_inc(o_st[s], 16)

                for t in range(NT):
                    m, s = rows_of(t), t % 2
                    act.wait_ge(a_done, t + 1)
                    act.activation(junk[0:m], Y[0:m, t % AHEAD, 0], ACT.Square, accum_out=stat[0:m, s, 0:1]).then_inc(sq_done, 1)
                    act.wait_ge(ms_done, t + 1)
                    act.activation(stat[0:m, s, 2:3], stat[0:m, s, 1:2], ACT.Sqrt).then_inc(root_done, 1)
                    store(t)
                for s in range(2):
                    act.wait_ge(o_st[s], 16 * ((NT + 1 - s) // 2))

            @block.vector
            def _(dve):
                dve.wait_ge(g_in, 16)
                for t in range(NT):
                    m, s = rows_of(t), t % 2
                    a = t % AHEAD
                    dve.wait_ge(y_in[a], 32 * (t // AHEAD + 1))
                    dve.wait_ge(x_in[a], 16 * (t // AHEAD + 1))
                    y0, y1 = Y[0:m, a, 0], Y[0:m, a, 1]
                    dve.scalar_tensor_tensor(out=y0, in0=y0, scalar=ch.gates[0:m, t, 0:1], in1=x2[0:m, a], op0=ALU.mult, op1=ALU.add).then_inc(m_done, 1)
                    dve.wait_ge(m_done, t + 1)
                    dve.scalar_tensor_tensor(out=y0, in0=y1, scalar=ch.gates[0:m, t, 1:2], in1=y0, op0=ALU.mult, op1=ALU.add).then_inc(a_done, 1)
                    dve.wait_ge(sq_done, t + 1)
                    dve.tensor_scalar(stat[0:m, s, 1:2], stat[0:m, s, 0:1], 1.0 / D, EPS, ALU.mult, ALU.add).then_inc(ms_done, 1)
                    dve.wait_ge(root_done, t + 1)
                    dve.reciprocal(stat[0:m, s, 3:4], stat[0:m, s, 2:3]).then_inc(rstd_done, 1)
                    dve.wait_ge(rstd_done, t + 1)
                    if t >= 2:
                        dve.wait_ge(o_st[s], 16 * (t // 2))
                    dve.scalar_tensor_tensor(out=o[0:m, s], in0=y0, scalar=stat[0:m, s, 3:4], in1=gain[0:m],
                                             op0=ALU.mult, op1=ALU.mult).then_inc(o_done, 1)


CONSTS = ("ident", "skew_hot", "skew_mask", "samp_hot", "samp_mask", "sink_hot", "cos", "sin", "decay", "samp_decay", "q_decay", "k_decay",
          "samp_q_decay", "samp_k_decay", "c_decay", "samp_c_decay", "ones", "before", "iota", "tokens", "no_expert", "zero_slots")
INPUTS = ("x_prompt", "x_sample", "cache_k", "cache_v", "state_ret", "norm_mix", "w_in", "attn_sink", "rel_bias", "w_branch_attn",
          "w_branch_ret", "w_out", "norm_ffn", "w_router_group", "b_router_group", "w_router_expert", "b_router_expert", "w_gate",
          "w_up", "w_down", "norm_final")
OUTPUTS = (("y_prompt", (1, SEQ, D)), ("y_sample", (DB, DL, D)), ("new_k_prompt", (1, 1, WINDOW, KVH, HD)), ("new_v_prompt", (1, 1, WINDOW, KVH, HD)),
           ("new_state_prompt", (1, 1, RH, DK, DV)), ("new_k_sample", (1, DB, WINDOW, KVH, HD)), ("new_v_sample", (1, DB, WINDOW, KVH, HD)),
           ("new_state_sample", (1, DB, RH, DK, DV)))


def hybrid_decoder_layer(nc, ins, outs, consts, stages=99):
    ch = Chip()
    ch.c = consts
    ch.route_steps = {"group": 3 + 2 * NT, "pair": 3 + 2 * NT + 4 + 2 * NT + 1}
    ch.route_steps["hot"] = ch.route_steps["pair"] + 5
    ch.route_steps["slots"] = ch.route_steps["hot"] + 6 + 2 + (NT - 1) + 2 + 4 + 2 * 5 + 8 + 4
    k_tiles = lambda w: w.rearrange("o (k p) n -> p (o k) n", p=P)
    ch.x_prompt = ins["x_prompt"].rearrange("b t d -> (b t) d")
    ch.x_sample = ins["x_sample"].rearrange("b t d -> (b t) d")
    ch.cache_k, ch.cache_v = (ins[n].rearrange("o b w h d -> (o b) w (h d)") for n in ("cache_k", "cache_v"))
    ch.state_ret = ins["state_ret"].rearrange("o b h d e -> (o b) h d e")
    ch.norm_mix, ch.norm_ffn = ins["norm_mix"], ins["norm_ffn"]
    ch.norm_final = ins["norm_final"].rearrange("(o d) -> o d", o=1)
    ch.w_in, ch.w_attn, ch.w_ret, ch.w_out = (k_tiles(ins[n]) for n in ("w_in", "w_branch_attn", "w_branch_ret", "w_out"))
    ch.w_rg, ch.w_re = k_tiles(ins["w_router_group"]), k_tiles(ins["w_router_expert"])
    ch.b_rg, ch.b_re = ins["b_router_group"], ins["b_router_expert"]
    ch.attn_sink, ch.attn_sink_row = ins["attn_sink"].rearrange("o h -> h o"), ins["attn_sink"]
    ch.rel_bias = ins["rel_bias"]
    ch.w_gate, ch.w_up, ch.w_down = (ins[n].rearrange("o e a b -> (o e) a b") for n in ("w_gate", "w_up", "w_down"))
    ch.y_prompt = outs["y_prompt"].rearrange("b t d -> (b t) d")
    ch.y_sample = outs["y_sample"].rearrange("b t d -> (b t) d")
    ch.new_k_prompt, ch.new_v_prompt = (outs[n].rearrange("o b w h d -> (o b w) (h d)") for n in ("new_k_prompt", "new_v_prompt"))
    ch.new_k_sample, ch.new_v_sample = (outs[n].rearrange("o b w h d -> (o b) w (h d)") for n in ("new_k_sample", "new_v_sample"))
    ch.new_state_prompt = outs["new_state_prompt"].rearrange("o b h d e -> (o b h) d e")
    ch.new_state_sample = outs["new_state_sample"].rearrange("o b h d e -> (o b) h d e")

    skew = nc.dram_tensor("skew", [HEADS, P * SKEW], F32).ap()
    ch.skew = skew
    ch.skew_read = bass.AP(skew.tensor, P - 1, [[SKEW - 1, P], [P * SKEW, HEADS], [1, 2 * P]])
    ch.attn_t = nc.dram_tensor("attn_t", [P, KT, T], F32).ap()
    ch.gate_t = nc.dram_tensor("gate_t", [P, KT, T], F32).ap()
    ch.m1_t = nc.dram_tensor("m1_t", [P, KT, T], F32).ap()
    ch.x2_d = nc.dram_tensor("x2_d", [T, D], F32).ap()
    ch.xn2_d = nc.dram_tensor("xn2_d", [T, D], F32).ap()
    ch.toktab = nc.dram_tensor("toktab", [SLOTS, 1], I32).ap()
    ch.y_d = nc.dram_tensor("y_d", [SLOTS, D], F32).ap()

    with ExitStack() as top:
        ch.sem = lambda name: nc.alloc_semaphore(name=name)
        ch.sbuf = lambda st: (lambda name, shape, dt=F32: st.enter_context(nc.sbuf_tensor(name, shape, dt)))
        sb = ch.sbuf(top)
        ch.passed = ch.sem("passed")
        mixer_sems = []

        def mixer_sem(name):
            mixer_sems.append(nc.alloc_semaphore(name=name))
            return mixer_sems[-1]

        ch.sem = mixer_sem
        ch.banks = [top.enter_context(nc.psum_tensor(f"bank{i}", [P, 512], F32)) for i in range(8)]
        ch.ident = sb("identity", [P, P])
        ch.logits = sb("logits", [P, NT, NG + NE])
        ch.slots, ch.gates = sb("slots", [P, NT, 2], I32), sb("gates", [P, NT, 2])
        ch.beyond = sb("beyond", [1, 1 + MAXOVER], I32)
        with ExitStack() as xs:
            sb = ch.sbuf(xs)
            ch.xH, ch.xL = sb("xH", [P, KT, T], F32R), sb("xL", [P, KT, T], F32R)
            with ExitStack() as at:
                sb = ch.sbuf(at)
                ch.sampbias, ch.negsink_rows = sb("sampbias", [P, KVH, P + NS]), sb("negsink_rows", [P, KVH])
                stage_norm(nc, ch)
                if stages < 2:
                    return ch
                ch.K, ch.V = sb("K", [P, NT, KVH * HD]), sb("V", [P, NT, KVH * HD])
                stage_kv(nc, ch)
                if stages < 3:
                    return ch
                stage_attention(nc, ch)
                if stages < 4:
                    return ch
            with ExitStack() as bs:
                sb = ch.sbuf(bs)
                br = sb("brH", [P, KT, T], F32R), sb("brL", [P, KT, T], F32R)
                stage_branch_attn(nc, ch, br)
            if stages < 5:
                return ch
            with ExitStack() as rs:
                ret = ch.sbuf(rs)("ret", [P, KT, T])
                stage_retention(nc, ch, ret)
                if stages < 6:
                    return ch
                stage_merge(nc, ch, ret)
            if stages < 7:
                return ch
            stage_out(nc, ch)
        if stages < 8:
            return ch
        nc.clear_and_free_semaphores(mixer_sems)
        nc.all_engine_barrier()
        ch.sem = lambda name: nc.alloc_semaphore(name=name)
        stage_route(nc, ch)
        if stages < 9:
            return ch
        stage_experts(nc, ch)
        stage_beyond(nc, ch)
        stage_combine(nc, ch)
    return ch


def kernel(**inputs):
    import concourse.bacc as bacc
    from concourse.bass_utils import run_bass_kernel_spmd

    nc = bacc.Bacc("TRN2", target_bir_lowering=False, num_devices=1)
    arrays, ins, outs, consts = {}, {}, {}, {}
    for name in INPUTS:
        a = np.ascontiguousarray(inputs[name])
        arrays[f"in_{name}"] = a
        ins[name] = nc.dram_tensor(f"in_{name}", a.shape, mybir.dt.from_np(a.dtype), kind="ExternalInput").ap()
    for name, a in constants().items():
        a = np.ascontiguousarray(a)
        arrays[f"const_{name}"] = a
        consts[name] = nc.dram_tensor(f"const_{name}", a.shape, mybir.dt.from_np(a.dtype), kind="ExternalInput").ap()
    for name, shape in OUTPUTS:
        outs[name] = nc.dram_tensor(f"out_{name}", shape, F32, kind="ExternalOutput").ap()
    hybrid_decoder_layer(nc, ins, outs, consts)
    r = run_bass_kernel_spmd(nc, [arrays], core_ids=[0])
    return tuple(r.results[0][f"out_{name}"] for name, _ in OUTPUTS)
```

```python
import math
from contextlib import ExitStack

import numpy as np

import concourse.bass as bass
from concourse import mybir

F32 = mybir.dt.float32
F32R = mybir.dt.float32r
I32 = mybir.dt.int32
U32 = mybir.dt.uint32
ACT = mybir.ActivationFunctionType
ALU = mybir.AluOpType
AX = mybir.AxisListType.X
ds = bass.ds

P = 128
D = 1024
KT = D // P
SEQ = 1024
NB = SEQ // P
DB, DL = 8, 4
NS = DB * DL
T = SEQ + NS
NT = NB + 1
TG = T // 3
HD = 64
KVH, GQA = 4, 4
HEADS = KVH * GQA
WINDOW = 128
BUCKETS = 32
SKEW = 3 * P
RH, DK, DV = 4, 128, 256
DVT = DV // P
PAST = 2048
EPS = 1e-6
NEG = -1e30
C_Q, C_K, C_V = 0, 1024, 1280
C_QR, C_KR, C_VR, C_GR, C_GA, C_GRT = 1536, 2048, 2560, 3584, 4608, 5632
NG, EPG = 4, 8
NE = NG * EPG
FF = 512
FT = FF // P
MAXBLK = T // P + 1
MAXOVER = 2 * T // P
SLOTS = (NE + MAXOVER) * P
ZW = 512


def rows_of(t):
    return P if t < NB else NS


def apart(eng, ch):
    eng.sem_inc(ch.passed, 1)


class Chip:
    pass


def constants():
    c = {}
    c["ident"] = np.eye(P, dtype=np.float32)

    def bucket(dist):
        d = np.maximum(dist, 1).astype(np.float32)
        large = 16 + (np.log(d / np.float32(16)) / np.float32(math.log(8.0)) * np.float32(16)).astype(np.int32)
        return np.where(dist < 16, dist, np.minimum(large, BUCKETS - 1))

    dist = 2 * P - 1 - np.arange(SKEW)
    ok = (dist >= 0) & (dist < WINDOW)
    c["skew_hot"] = ((bucket(np.clip(dist, 0, WINDOW - 1))[None] == np.arange(BUCKETS)[:, None]) & ok[None]).astype(np.float32)
    c["skew_mask"] = np.broadcast_to(np.where(ok, 0.0, NEG), (HEADS, SKEW)).astype(np.float32).copy()
    samp = np.zeros((BUCKETS, DL, P + NS), np.float32)
    mask = np.full((P, P + NS), NEG, np.float32)
    for i in range(DL):
        for col in range(P + NS):
            dd = i + P - col if col < P else i - (col - P) % DL
            if 0 <= dd < WINDOW:
                samp[bucket(np.array(dd)), i, col] = 1.0
                for r in range(P):
                    if r % DL == i and (col < P or (col - P) // DL == r // 16):
                        mask[r, col] = 0.0
    c["samp_hot"] = samp
    c["samp_mask"] = mask
    sink = np.zeros((HEADS, KVH, P), np.float32)
    for r in range(P):
        for k in range(KVH):
            sink[k * GQA + 2 * ((r // DL) % 2) + (r // (2 * DL)) % 2, k, r] = 1.0
    c["sink_hot"] = sink
    half = DK // 2
    inv = np.float32(10000.0) ** (-np.arange(half, dtype=np.float32) * np.float32(2.0) / np.float32(DK))
    pos = np.concatenate([np.arange(SEQ), np.tile(PAST + np.arange(DL), DB), np.zeros(P - NS)]).astype(np.float32)
    ang = (pos[:, None] * inv[None].astype(np.float32)).astype(np.float32)
    c["cos"] = np.cos(ang).astype(np.float32).reshape(NT, P, half).transpose(1, 0, 2).copy()
    c["sin"] = np.sin(ang).astype(np.float32).reshape(NT, P, half).transpose(1, 0, 2).copy()
    lg = np.log(np.float32(1.0) - np.float32(2.0) ** (np.float32(-5.0) - np.arange(RH, dtype=np.float32))).astype(np.float32)
    idx = np.arange(P, dtype=np.float32)
    diff = idx[None, :] - idx[:, None]
    dec = np.where(diff >= 0, np.exp(np.maximum(diff, 0)[None] * lg[:, None, None]), 0)
    c["decay"] = (np.float32(DK ** -0.5) * dec).transpose(1, 0, 2).astype(np.float32).copy()
    tok = np.arange(NS)
    same = tok[:, None] // DL == tok[None] // DL
    sdiff = (tok[None] % DL - tok[:, None] % DL).astype(np.float32)
    sdec = np.where(same & (sdiff >= 0), np.exp(np.maximum(sdiff, 0)[None] * lg[:, None, None]), 0)
    c["samp_decay"] = (np.float32(DK ** -0.5) * sdec).transpose(1, 0, 2).astype(np.float32).copy()
    c["q_decay"] = np.exp((idx + 1)[:, None] * lg).astype(np.float32)
    c["k_decay"] = (np.float32(DK ** -0.5) * np.exp((P - 1 - idx)[:, None] * lg)).astype(np.float32)
    c["samp_q_decay"] = np.exp((tok % DL + 1).astype(np.float32)[:, None] * lg).astype(np.float32)
    kd = np.float32(DK ** -0.5) * np.exp((DL - 1 - tok % DL).astype(np.float32)[:, None] * lg).astype(np.float32)
    c["samp_k_decay"] = ((tok[:, None, None] // DL == np.arange(DB)[None, :, None]) * kd[:, None, :]).astype(np.float32)
    c["c_decay"] = np.broadcast_to(np.exp(P * lg).astype(np.float32), (P, RH)).copy()
    c["samp_c_decay"] = np.broadcast_to(np.exp(DL * lg).astype(np.float32), (P, RH)).copy()
    c["ones"] = np.ones((P, P), np.float32)
    c["before"] = (np.arange(P)[:, None] < np.arange(P)[None]).astype(np.float32)
    c["iota"] = np.broadcast_to(np.arange(P, dtype=np.float32), (P, P)).copy()
    c["tokens"] = (np.arange(NT)[None] * P + np.arange(P)[:, None]).astype(np.int32)
    valid = np.zeros((P, NT), np.float32)
    valid[:, NB] = np.where(np.arange(P) < NS, 0.0, 1000.0)
    c["no_expert"] = valid
    c["zero_slots"] = np.zeros((SLOTS // P, P), np.int32)
    return c


def split_matmuls(pe, out, lhs, rhs, first, last):
    (lh, ll), (rh, rl) = lhs, rhs
    pe.matmul(out, lh, rh, start=first, stop=False)
    pe.matmul(out, lh, rl, start=False, stop=False)
    return pe.matmul(out, ll, rh, start=False, stop=last)


def t_layout_product(pe, banks, w, x, ready=None):
    for k in range(KT):
        if ready:
            ready(k)
        for n, (a, b) in enumerate(((0, 0), (0, 1), (1, 0))):
            for g in range(3):
                mm = pe.matmul(banks[g][:, 0:TG], w[a][:, k, :], x[b][:, k, g * TG:(g + 1) * TG],
                               start=(k == 0 and n == 0), stop=(k == KT - 1 and n == 2))
    return mm


def first_loads(sp, ch, stage):
    sources = {"kv": (ch.w_in[:, :, C_K:C_K + P], ch.w_in[:, :, C_K + P:C_K + 2 * P]),
               "attention": (ch.w_in[:, :, 0:P], ch.w_in[:, :, P:2 * P]),
               "branch": (ch.w_in[:, :, C_GA:C_GA + P], ch.w_in[:, :, C_GRT:C_GRT + P], ch.w_attn[:, :, 0:P]),
               "retention": (ch.w_in[:, :, C_GR:C_GR + P], ch.w_in[:, :, C_GR + P:C_GR + 2 * P]),
               "merge": (ch.w_ret[:, :, 0:P], ch.w_ret[:, :, P:2 * P]),
               "out": (ch.w_out[:, :, 0:P], ch.w_out[:, :, P:2 * P])}[stage]
    for slot, src in enumerate(sources):
        sp.dma_start(ch.raw[:, slot], src).then_inc(ch.w_sems[stage][slot], 16)


def stage_norm(nc, ch):
    sem = ch.sem
    x_in, scale_done = [sem("n_x0"), sem("n_x1")], sem("n_scaled")
    gain_in, sq_done, ms_done, root_done, rstd_done = sem("n_gain"), sem("n_sq"), sem("n_ms"), sem("n_root"), sem("n_rstd")
    turned, hi_done, lo_done = sem("n_turned"), sem("n_hi"), sem("n_lo")
    tab_in, relx_zero, relx_done, bias_mm, bias_sum, bias_out = (
        sem("n_tab"), sem("n_relx0"), sem("n_relx"), sem("n_bmm"), sem("n_bsum"), sem("n_bout"))
    with ExitStack() as st:
        sb = ch.sbuf(st)
        xb = sb("n_xb", [P, 2, D])
        xs = sb("n_xs", [P, 2, D])
        junk = sb("n_junk", [P, D])
        gain = sb("n_gainrow", [P, D])
        stat = sb("n_stat", [P, 2, 4])
        relb = sb("n_relb", [BUCKETS, HEADS])
        hot = sb("n_skewhot", [BUCKETS, SKEW])
        mask = sb("n_skewmask", [HEADS, SKEW])
        shot = sb("n_samphot", [BUCKETS, DL, P + NS])
        smask = sb("n_sampmask", [P, P + NS])
        sinkhot = sb("n_sinkhot", [HEADS, KVH, P])
        sinkcol = sb("n_sinkcol", [HEADS, 1])
        skew = sb("n_skew", [HEADS, SKEW])
        relx = sb("n_relx", [BUCKETS, KVH, DL, P])
        banks = ch.banks

        def source(t):
            if isinstance(t, int) and t == NB:
                return ch.x_sample
            return ch.x_prompt[ds(t * P, P), :]

        with nc.Block() as block:
            @block.sync
            def _(sp):
                sp.dma_start(gain[:], ch.norm_mix.broadcast_to([P, D])).then_inc(gain_in, 16)

                def load(i, s, t):
                    if isinstance(i, int) or s >= 0:
                        sp.wait_ge(scale_done, i * 2)
                    m = NS if isinstance(t, int) else P
                    sp.dma_start(xb[0:m, s, :], source(t)).then_inc(x_in[s], 16)

                with sp.Fori(0, NB // 2) as i:
                    for s in range(2):
                        load(i, s, i * 2 + s)
                load(NB // 2, 0, NB)
                first_loads(sp, ch, "kv")
                sp.wait_ge(bias_sum, 1)
                sp.dma_start(ch.skew.rearrange("h (q u) -> h q u", u=SKEW),
                             skew[:].rearrange("h (o u) -> h o u", o=1).broadcast_to([HEADS, P, SKEW])).then_inc(bias_out, 16)
                sp.wait_ge(bias_out, 16)

            @block.gpsimd
            def _(pool):
                for dst, src in ((ch.ident, ch.c["ident"]), (relb, ch.rel_bias), (hot, ch.c["skew_hot"]), (mask, ch.c["skew_mask"]), (shot, ch.c["samp_hot"]),
                                 (smask, ch.c["samp_mask"]), (sinkhot, ch.c["sink_hot"]), (sinkcol, ch.attn_sink)):
                    pool.dma_start(dst[:], src).then_inc(tab_in, 16)
                pool.wait_ge(tab_in, 16 * 8)

            @block.scalar
            def _(act):
                def front(i, s, m):
                    t = i * 2 + s
                    act.wait_ge(x_in[s], i * 16 + 16)
                    act.activation(junk[0:m, :], xb[0:m, s, :], ACT.Square, accum_out=stat[0:m, s, 0:1]).then_inc(sq_done, 1)
                    act.wait_ge(ms_done, t + 1)
                    act.activation(stat[0:m, s, 2:3], stat[0:m, s, 1:2], ACT.Sqrt).then_inc(root_done, 1)

                def back(i, s, m):
                    t = i * 2 + s
                    for b in range(2):
                        act.wait_ge(turned, t * 2 + b + 1)
                        act.activation(ch.xH[:, 4 * b:4 * b + 4, ds(t * P, m)],
                                       banks[2 * s + b][:].rearrange("p (k m) -> p k m", m=P)[:, :, 0:m], ACT.Copy).then_inc(hi_done, 1)

                with act.Fori(0, NB // 2) as i:
                    front(i, 0, P)
                    front(i, 1, P)
                    back(i, 0, P)
                    back(i, 1, P)
                front(NB // 2, 0, NS)
                back(NB // 2, 0, NS)

            @block.vector
            def _(dve):
                def front(i, s, m):
                    t = i * 2 + s
                    dve.wait_ge(sq_done, t + 1)
                    dve.tensor_scalar(stat[0:m, s, 1:2], stat[0:m, s, 0:1], 1.0 / D, EPS, ALU.mult, ALU.add).then_inc(ms_done, 1)
                    dve.wait_ge(root_done, t + 1)
                    dve.reciprocal(stat[0:m, s, 3:4], stat[0:m, s, 2:3]).then_inc(rstd_done, 1)
                    dve.wait_ge(rstd_done, t + 1)
                    dve.wait_ge(turned, i * 4)
                    dve.scalar_tensor_tensor(out=xs[0:m, s, :], in0=xb[0:m, s, :], scalar=stat[0:m, s, 3:4], in1=gain[0:m, :],
                                             op0=ALU.mult, op1=ALU.mult).then_inc(scale_done, 1)

                def back(i, s, m):
                    t = i * 2 + s
                    for b in range(2):
                        dve.wait_ge(hi_done, t * 2 + b + 1)
                        cols = ds(t * P, m)
                        dve.tensor_tensor(ch.xL[:, 4 * b:4 * b + 4, cols],
                                          banks[2 * s + b][:].rearrange("p (k m) -> p k m", m=P)[:, :, 0:m],
                                          ch.xH[:, 4 * b:4 * b + 4, cols].bitcast(F32), ALU.subtract).then_inc(lo_done, 1)

                dve.wait_ge(gain_in, 16)
                with dve.Fori(0, NB // 2) as i:
                    front(i, 0, P)
                    front(i, 1, P)
                    back(i, 0, P)
                    back(i, 1, P)
                front(NB // 2, 0, NS)
                back(NB // 2, 0, NS)
                dve.memset(relx[:], 0.0).then_inc(relx_zero, 1)
                dve.wait_ge(relx_zero, 1)
                dve.wait_ge(tab_in, 16 * 8)
                for c in range(KVH):
                    for i in range(DL):
                        for par in range(2):
                            dst = relx[:, c, i, :].rearrange("w (b r f j) -> w b r f j", r=2, f=2, j=DL)[:, :, par, :, i]
                            src = relb[:, c * GQA:(c + 1) * GQA].rearrange("w (f r) -> w r f", r=2)[:, par:par + 1, :]
                            dve.tensor_copy(dst, src.broadcast_to([BUCKETS, DB, 2])).then_inc(relx_done, 1)
                dve.wait_ge(bias_mm, 1)
                dve.tensor_tensor(skew[:], banks[4][0:HEADS, 0:SKEW], mask[:], ALU.add).then_inc(bias_sum, 1)
                for c in range(KVH):
                    dve.wait_ge(bias_mm, c + 2)
                    dve.tensor_tensor(ch.sampbias[:, c, :], banks[5 + c % 2][:, 0:P + NS], smask[:], ALU.add).then_inc(bias_sum, 1)
                dve.wait_ge(bias_mm, KVH + 2)
                dve.tensor_scalar(ch.negsink_rows[:], banks[7][:, 0:KVH], -1.0, None, ALU.mult).then_inc(bias_sum, 1)

            @block.tensor
            def _(pe):
                def turn(i, s, m):
                    t = i * 2 + s
                    pe.wait_ge(scale_done, t + 1)
                    pe.wait_ge(lo_done, i * 4)
                    for b in range(2):
                        for k in range(4):
                            tr = pe.transpose(banks[2 * s + b][:, k * P:k * P + m], xs[0:m, s, (4 * b + k) * P:(4 * b + k + 1) * P],
                                              ch.ident[0:m, 0:m])
                        tr.then_inc(turned, 1)

                pe.wait_ge(tab_in, 16 * 8)
                with pe.Fori(0, NB // 2) as i:
                    turn(i, 0, P)
                    turn(i, 1, P)
                turn(NB // 2, 0, NS)
                pe.matmul(banks[4][0:HEADS, 0:SKEW], relb[:], hot[:], start=True, stop=True).then_inc(bias_mm, 1)
                pe.wait_ge(relx_done, KVH * DL * 2)
                for c in range(KVH):
                    if c >= 2:
                        pe.wait_ge(bias_sum, c)
                    for i in range(DL):
                        mm = pe.matmul(banks[5 + c % 2][:, 0:P + NS], relx[:, c, i, :], shot[:, i, :], start=(i == 0), stop=(i == DL - 1))
                    mm.then_inc(bias_mm, 1)
                for c in range(KVH):
                    mm = pe.matmul(banks[7][:, c:c + 1], sinkhot[:, c, :], sinkcol[:], start=True, stop=True)
                mm.then_inc(bias_mm, 1)


def stage_kv(nc, ch):
    sem = ch.sem
    w_in, hi_done, lo_done, kv_mm, k_out, v_out, stored, zeroed = (
        ch.w_sems["kv"], sem("kv_hi"), sem("kv_lo"), sem("kv_mm"), sem("kv_kout"), sem("kv_vout"), sem("kv_st"), sem("kv_zero"))
    with ExitStack() as st:
        sb = ch.sbuf(st)
        raw = ch.raw
        wH, wL = sb("kv_wH", [P, KT, 4 * P], F32R), sb("kv_wL", [P, KT, 4 * P], F32R)
        banks = ch.banks
        with nc.Block() as block:
            @block.sync
            def _(sp):
                for q in range(2, 4):
                    sp.wait_ge(lo_done, q - 1)
                    sp.dma_start(raw[:, q % 2], ch.w_in[:, :, C_K + q * P:C_K + (q + 1) * P]).then_inc(w_in[q % 2], 16)
                sp.dma_start(ch.new_k_sample[:, 0:WINDOW - DL, :], ch.cache_k[:, DL:WINDOW, :]).then_inc(stored, 16)
                sp.dma_start(ch.new_v_sample[:, 0:WINDOW - DL, :], ch.cache_v[:, DL:WINDOW, :]).then_inc(stored, 16)
                sp.wait_ge(lo_done, 4)
                first_loads(sp, ch, "attention")
                sp.wait_ge(stored, 16 * 2)

            @block.gpsimd
            def _(pool):
                pool.memset(ch.K[:, NB, :], 0.0).then_inc(zeroed, 1)
                pool.memset(ch.V[:, NB, :], 0.0).then_inc(zeroed, 1)

            @block.scalar
            def _(act):
                for q in range(4):
                    act.wait_ge(w_in[q % 2], 16 * (q // 2 + 1))
                    act.activation(wH[:, :, q * P:(q + 1) * P], raw[:, q % 2], ACT.Copy).then_inc(hi_done, 1)
                act.wait_ge(zeroed, 2)
                for t in range(NT):
                    m = rows_of(t)
                    act.wait_ge(kv_mm, t + 1)
                    act.activation(ch.K[0:m, t, :], banks[t % 2][0:m, 0:2 * P], ACT.Copy).then_inc(k_out, 1)
                    act.activation(ch.V[0:m, t, :], banks[t % 2][0:m, 2 * P:4 * P], ACT.Copy).then_inc(v_out, 1)

            @block.vector
            def _(dve):
                for q in range(4):
                    dve.wait_ge(hi_done, q + 1)
                    dve.tensor_tensor(wL[:, :, q * P:(q + 1) * P], raw[:, q % 2], wH[:, :, q * P:(q + 1) * P].bitcast(F32),
                                      ALU.subtract).then_inc(lo_done, 1)

            @block.tensor
            def _(pe):
                pe.wait_ge(lo_done, 4)
                for t in range(NT):
                    m = rows_of(t)
                    if t >= 2:
                        pe.wait_ge(k_out, t - 1)
                        pe.wait_ge(v_out, t - 1)
                    for k in range(KT):
                        cols = slice(t * P, t * P + m)
                        mm = split_matmuls(pe, banks[t % 2][0:m, :], (ch.xH[:, k, cols], ch.xL[:, k, cols]),
                                           (wH[:, k, :], wL[:, k, :]), k == 0, k == KT - 1)
                    mm.then_inc(kv_mm, 1)


def stage_attention(nc, ch):
    sem = ch.sem
    w_in, stored = ch.w_sems["attention"], sem("a_stored")
    bias_in, ck_in, cv_in = sem("a_bias"), sem("a_ck"), sem("a_cv")
    kd_done, vd_done, kt_turned, kt_done = sem("a_kd"), sem("a_vd"), sem("a_ktt"), sem("a_kt")
    hi_done, lo_done, q_mm, q_out = sem("a_hi"), sem("a_lo"), sem("a_qmm"), sem("a_qout")
    s_mm, s_sum, m_red, nm_done, d_done = sem("a_smm"), sem("a_ssum"), sem("a_mred"), sem("a_nm"), sem("a_d")
    p_exp, sink_exp, den_done, rcp_done, p_norm = sem("a_pexp"), sem("a_sexp"), sem("a_den"), sem("a_rcp"), sem("a_pnorm")
    p_turned, pt_hi, pt_lo, o_mm, o_out = sem("a_pt"), sem("a_pth"), sem("a_ptl"), sem("a_omm"), sem("a_oout")
    z_mm, z_out, z_red, z_nm, z_d, z_exp, z_sexp, z_den, z_rcp, z_norm = (
        sem("z_mm"), sem("z_out"), sem("z_red"), sem("z_nm"), sem("z_d"), sem("z_exp"), sem("z_sexp"), sem("z_den"), sem("z_rcp"), sem("z_norm"))
    sink_in, z_par = sem("a_sink"), sem("z_par")
    zeros_done, y_zeroed = sem("a_zeros"), sem("a_yzero")
    Y_ROWS = (SLOTS - NE * P) // KVH
    S_PER = NB
    KEYS_AT = 6
    Z_PER, Z_OUT = 6, 5
    CHUNK = {1: (0, 0), 2: (0, 1), 4: (1, 0), 5: (1, 1), 6: (2, 0), 7: (2, 1)}
    ORDER = list(CHUNK)
    assert all(min((g + 1) * TG, SEQ) <= (n + 2) * P and (g < 2 or n >= 3) for n, (g, _) in CHUNK.items())
    projected = lambda c, k: 2 + len(CHUNK) * c + k
    with ExitStack() as st:
        sb = ch.sbuf(st)
        raw = ch.raw
        wH, wL = sb("a_wH", [P, 2, KT, P], F32R), sb("a_wL", [P, 2, KT, P], F32R)
        out = ch.attn
        qT = sb("a_qT", [P, 2, T])
        kT = sb("a_kT", [P, T])
        Kd, Vd = sb("a_Kd", [P, NT, 2, HD]), sb("a_Vd", [P, NT, 2, HD])
        bias = sb("a_bias_t", [P, GQA, 2 * P])
        S = sb("a_S", [P, 2, GQA, 2 * P])
        PT = sb("a_PT", [P, 2, GQA, P])
        sinkrow, negsink = sb("a_sinkrow", [P, HEADS]), sb("a_negsink", [P, HEADS])
        nm, dd, es, rs, rcp, ninv = (sb("a_" + n, [P, 2, GQA]) for n in ("nm", "dd", "es", "rs", "rcp", "den"))
        cK, cV = sb("a_cK", [P, DB, 2, HD]), sb("a_cV", [P, DB, 2, HD])
        cKT = sb("a_cKT", [P, DB, P])
        ZT = sb("a_ZT", [P, 2, P])
        Z = sb("a_Z", [P, P + NS])
        zs = sb("a_zs", [P, 6])
        zeros = sb("a_zeros_t", [P, 1, ZW])
        banks = ch.banks
        b7 = banks[7]

        def dup(ap, n):
            return ap.rearrange("p n (o d) -> p n o d", o=1).broadcast_to([P, n, 2, HD])

        def s_bank(n, g):
            return banks[2 * (n % 2) + g % 2][:, (g // 2) * 2 * P:(g // 2 + 1) * 2 * P]

        def cols_of(n):
            return slice(P, 2 * P) if n % NB == 0 else slice(0, 2 * P)

        def walk(eng, body):
            with eng.Fori(0, KVH - 1) as c:
                body(c, False)
            body(KVH - 1, True)

        with nc.Block() as block:
            @block.sync
            def _(sp):
                sp.wait_ge(zeros_done, 1)
                sp.dma_start(sinkrow[:], ch.attn_sink_row.broadcast_to([P, HEADS])).then_inc(sink_in, 16)
                sp.dma_start(ch.new_k_prompt, ch.K[:, NB - 1, :]).then_inc(stored, 16)
                sp.dma_start(ch.new_v_prompt, ch.V[:, NB - 1, :]).then_inc(stored, 16)
                for b in range(DB):
                    sp.dma_start(ch.new_k_sample[b, WINDOW - DL:WINDOW, :], ch.K[b * DL:(b + 1) * DL, NB, :]).then_inc(stored, 16)
                    sp.dma_start(ch.new_v_sample[b, WINDOW - DL:WINDOW, :], ch.V[b * DL:(b + 1) * DL, NB, :]).then_inc(stored, 16)

                def body(c, last):
                    if not last:
                        for f in range(2):
                            sp.wait_ge(lo_done, c * 2 + f + 1)
                            apart(sp, ch)
                            sp.dma_start(raw[:, f], ch.w_in[:, :, ds(c * 256 + 256 + f * P, P)]).then_inc(w_in[f], 16)
                    sp.wait_ge(s_sum, c * S_PER)
                    apart(sp, ch)
                    sp.dma_start(bias[:], ch.skew_read[:, ds(c * GQA, GQA), :]).then_inc(bias_in, 16)
                    sp.dma_start(ch.y_d[ds(c * Y_ROWS + NE * P, Y_ROWS), :].rearrange("(p r) (a b) -> p (r a) b", p=P, b=ZW),
                                 zeros[:].broadcast_to([P, Y_ROWS * D // (P * ZW), ZW])).then_inc(y_zeroed, 16)
                    sp.wait_ge(z_mm, c * Z_PER)
                    for b in range(DB):
                        for o in range(2):
                            sp.dma_start(cK[:, b, o, :], ch.cache_k[b, :, ds(c * HD, HD)]).then_inc(ck_in, 16)
                            sp.dma_start(cV[:, b, o, :], ch.cache_v[b, :, ds(c * HD, HD)]).then_inc(cv_in, 16)

                walk(sp, body)
                sp.wait_ge(lo_done, KVH * 2)
                first_loads(sp, ch, "branch")
                sp.wait_ge(y_zeroed, 16 * KVH)
                sp.wait_ge(stored, 16 * (2 + 2 * DB))

            @block.gpsimd
            def _(pool):
                pool.memset(zeros[:], 0.0).then_inc(zeros_done, 1)
                def keys(c):
                    pool.tensor_copy(Kd[:], dup(ch.K[:, :, ds(c * HD, HD)], NT)).then_inc(kd_done, 1)

                def normalize(c, n):
                    pool.wait_ge(rcp_done, c * NB + n + 1)
                    w = cols_of(n)
                    pool.tensor_tensor(S[:, n % 2, :, w], S[:, n % 2, :, w],
                                       rcp[:, n % 2, :].rearrange("p (g o) -> p g o", o=1).broadcast_to([P, GQA, w.stop - w.start]),
                                       ALU.mult).then_inc(p_norm, 1)

                def body(c, last):
                    pool.wait_ge(o_mm, c * NB)
                    pool.wait_ge(z_mm, c * Z_PER)
                    pool.tensor_copy(Vd[:], dup(ch.V[:, :, ds(c * HD, HD)], NT)).then_inc(vd_done, 1)
                    for n in range(NB):
                        if n < NB - 1 or not last:
                            normalize(c, n + 1)
                        if n == 2 and not last:
                            pool.wait_ge(kt_turned, c * 3 + 3)
                            keys(c + 1)

                keys(0)
                normalize(0, 0)
                walk(pool, body)

            @block.scalar
            def _(act):
                def split_hi(c, f):
                    act.wait_ge(w_in[f], c * 16 + 16)
                    act.activation(wH[:, f], raw[:, f], ACT.Copy).then_inc(hi_done, 1)

                def queries(bank, f, g):
                    return act.activation(qT[:, f, g * TG:(g + 1) * TG], bank[:, 0:TG], ACT.Copy, scale=HD ** -0.5)

                def exps(c, n):
                    s, w = n % 2, cols_of(n)
                    act.wait_ge(nm_done, c * NB + n + 1)
                    for g in range(GQA):
                        ins = act.activation(S[:, s, g, w], S[:, s, g, w], ACT.Exp, bias=nm[:, s, g:g + 1], accum_out=rs[:, s, g:g + 1])
                    ins.then_inc(p_exp, 1)
                    act.wait_ge(d_done, c * NB + n + 1)
                    act.activation(es[:, s, :], dd[:, s, :], ACT.Exp).then_inc(sink_exp, 1)

                def body(c, last):
                    def out_evac(n):
                        act.wait_ge(o_mm, c * NB + n + 1)
                        for par in range(2):
                            r = slice(par * HD, (par + 1) * HD)
                            act.activation(out[r, ds(c * 2, 2), n * P:(n + 1) * P],
                                           banks[6][r, :].rearrange("p (r f i) -> p r f i", r=2, f=2)[:, par], ACT.Copy).then_inc(o_out, 1)

                    def sampled(step):
                        act.wait_ge(z_mm, c * Z_PER + step + 1)
                        if step in (0, 1):
                            act.activation(cKT[:, 4 * step:4 * step + 4, :], b7[:].rearrange("p (b k) -> p b k", b=4), ACT.Copy).then_inc(z_out, 1)
                        if step == 4:
                            act.activation(ZT[:, 0, :], b7[:, 0:P], ACT.Copy)
                            act.activation(ZT[0:NS, 1, :], b7[0:NS, P:2 * P], ACT.Copy).then_inc(z_out, 1)

                    def sampled_exp():
                        act.wait_ge(z_nm, c + 1)
                        act.activation(Z[:], Z[:], ACT.Exp, bias=zs[:, 0:1], accum_out=zs[:, 1:2]).then_inc(z_exp, 1)
                        act.wait_ge(z_d, c + 1)
                        act.activation(zs[:, 3:4], zs[:, 2:3], ACT.Exp).then_inc(z_sexp, 1)

                    for n in range(NB):
                        if n >= 1:
                            out_evac(n - 1)
                        if n in CHUNK and not last:
                            g, f = CHUNK[n]
                            act.wait_ge(q_mm, projected(c, ORDER.index(n)) + 1)
                            queries(b7, f, g).then_inc(q_out, 1)
                        if n < NB - 1 or not last:
                            exps(c, n + 1)
                        if n == 4:
                            sampled_exp()
                        act.wait_ge(p_turned, c * 2 * NB + 2 * n + 1)
                        act.activation(PT[:, 0], banks[4][:].rearrange("p (g i) -> p g i", g=GQA), ACT.Copy).then_inc(pt_hi, 1)
                        if n in (0, 1, 4):
                            sampled(n)
                        if n == 0 and not last:
                            act.wait_ge(q_mm, projected(c, 0))
                            for f in range(2):
                                split_hi(c + 1, f)
                    out_evac(NB - 1)

                for f in range(2):
                    split_hi(0, f)
                for f in range(2):
                    act.wait_ge(q_mm, f + 1)
                    for g in range(3):
                        ins = queries(banks[3 * f + g], f, g)
                    ins.then_inc(q_out, 1)
                exps(0, 0)
                walk(act, body)

            @block.vector
            def _(dve):
                dve.wait_ge(sink_in, 16)
                dve.tensor_scalar(negsink[:].rearrange("p (c r f) -> p c r f", r=2, f=2), sinkrow[:].rearrange("p (c f r) -> p c r f", r=2, f=2),
                                  -1.0, None, ALU.mult).then_inc(z_rcp, 1)
                dve.wait_ge(z_rcp, 1)
                def split_lo(c, f):
                    dve.wait_ge(hi_done, c * 2 + f + 1)
                    dve.tensor_tensor(wL[:, f], raw[:, f], wH[:, f].bitcast(F32), ALU.subtract).then_inc(lo_done, 1)

                def keys(c, where):
                    for q in range(3):
                        dve.wait_ge(kt_turned, c * 3 + q + 1)
                        w = 4 * P if q < 2 else NS
                        dve.tensor_copy(kT[:, q * 4 * P:q * 4 * P + w], banks[where[q]][:, 0:w]).then_inc(kt_done, 1)

                def front(c, n, head):
                    s, w = n % 2, cols_of(n)
                    m = c * NB + n + 1
                    if n % NB == 0:
                        dve.wait_ge(bias_in, head * 16 + 16)
                    dve.wait_ge(s_mm, m)
                    if n >= 2:
                        dve.wait_ge(p_turned, c * 2 * NB + 2 * (n - 1))
                    for h in range(2):
                        ins = dve.tensor_tensor(S[:, s, 2 * h:2 * h + 2, w], banks[2 * s + h][:].rearrange("p (g k) -> p g k", g=2)[:, :, w],
                                                bias[:].rearrange("p (f r) k -> p r f k", r=2)[:, h, :, w], ALU.add)
                    ins.then_inc(s_sum, 1)
                    dve.wait_ge(s_sum, m)
                    dve.tensor_reduce(nm[:, s, :], S[:, s, :, w], AX, ALU.max, negate=True).then_inc(m_red, 1)
                    dve.wait_ge(m_red, m)
                    dve.tensor_tensor(nm[:, s, :], nm[:, s, :], negsink[:, ds(head * GQA, GQA)], ALU.min).then_inc(nm_done, 1)
                    dve.wait_ge(nm_done, m)
                    dve.tensor_tensor(dd[:, s, :], nm[:, s, :], negsink[:, ds(head * GQA, GQA)], ALU.subtract).then_inc(d_done, 1)

                def back(c, n):
                    s = n % 2
                    m = c * NB + n + 1
                    dve.wait_ge(p_exp, m)
                    dve.wait_ge(sink_exp, m)
                    dve.tensor_tensor(ninv[:, s, :], rs[:, s, :], es[:, s, :], ALU.add).then_inc(den_done, 1)
                    dve.wait_ge(den_done, m)
                    dve.reciprocal(rcp[:, s, :], ninv[:, s, :]).then_inc(rcp_done, 1)

                def body(c, last):
                    def turned_copy(n):
                        dve.wait_ge(p_turned, c * 2 * NB + 2 * n + 2)
                        dve.tensor_copy(PT[:, 1], banks[5][:].rearrange("p (g i) -> p g i", g=GQA)).then_inc(pt_lo, 1)

                    def sampled(step):
                        dve.wait_ge(z_mm, c * Z_PER + step + 1)
                        if step == 2:
                            dve.tensor_copy(ZT[:, 0, :], b7[:, 0:P])
                            dve.tensor_copy(ZT[0:NS, 1, :], b7[0:NS, P:2 * P]).then_inc(z_out, 1)
                        if step == 3:
                            dve.tensor_tensor(Z[:], b7[:, 0:P + NS], ch.sampbias[:, ds(c, 1), :].rearrange("p o k -> p (o k)"), ALU.add).then_inc(z_out, 1)
                            dve.wait_ge(z_out, c * Z_OUT + 4)
                            dve.tensor_reduce(zs[:, 0:1], Z[:], AX, ALU.max, negate=True).then_inc(z_red, 1)
                            dve.wait_ge(z_red, c * 2 + 1)
                            dve.tensor_tensor(zs[:, 0:1], zs[:, 0:1], ch.negsink_rows[:, ds(c, 1)], ALU.min).then_inc(z_nm, 1)
                            dve.wait_ge(z_nm, c + 1)
                            dve.tensor_tensor(zs[:, 2:3], zs[:, 0:1], ch.negsink_rows[:, ds(c, 1)], ALU.subtract).then_inc(z_d, 1)
                        if step == 5:
                            for par in range(2):
                                r = slice(par * HD, (par + 1) * HD)
                                for b in range(2):
                                    dve.tensor_copy(out[r, ds(c * 2 + b, 1), SEQ:T].rearrange("p o (b i) -> p (o b) i", i=DL),
                                                    b7[r, 0:P].rearrange("p (b r f i) -> p r f b i", b=DB, r=2, f=2)[:, par, b]).then_inc(z_norm, 1)

                    def sampled_norm():
                        dve.wait_ge(z_exp, c + 1)
                        dve.wait_ge(z_sexp, c + 1)
                        dve.tensor_tensor(zs[:, 4:5], zs[:, 1:2], zs[:, 3:4], ALU.add).then_inc(z_den, 1)
                        dve.wait_ge(z_den, c + 1)
                        dve.reciprocal(zs[:, 5:6], zs[:, 4:5]).then_inc(z_rcp, 1)
                        dve.wait_ge(z_rcp, c + 2)
                        dve.tensor_scalar(Z[:], Z[:], zs[:, 5:6], None, ALU.mult).then_inc(z_red, 1)

                    for n in range(NB):
                        more = n < NB - 1 or not last
                        if more:
                            front(c, n + 1, c if n < NB - 1 else c + 1)
                        if n == 4:
                            sampled_norm()
                        if n == KEYS_AT and not last:
                            keys(c + 1, (0, 1, 7))
                        turned_copy(n)
                        if more:
                            back(c, n + 1)
                        if n in (2, 3, 5):
                            sampled(n)
                        if n == 0 and not last:
                            for f in range(2):
                                split_lo(c + 1, f)

                for f in range(2):
                    split_lo(0, f)
                keys(0, (3, 6, 7))
                front(0, 0, 0)
                back(0, 0)
                walk(dve, body)

            @block.tensor
            def _(pe):
                def turn_keys(c, where):
                    pe.wait_ge(kd_done, c + 1)
                    for q in range(3):
                        for t in range(q * 4, min(q * 4 + 4, NT)):
                            tr = pe.transpose(banks[where[q]][:, (t - q * 4) * P:(t - q * 4 + 1) * P],
                                              Kd[:, t].rearrange("p o d -> p (o d)"), ch.ident[:])
                        tr.then_inc(kt_turned, 1)

                def scores(c, n):
                    if n >= 2:
                        pe.wait_ge(s_sum, c * NB + n - 1)
                    if n == 1:
                        pe.wait_ge(q_out, projected(c, 0))
                    if n == NB:
                        pe.wait_ge(kt_done, c * 3 + 6)
                        pe.wait_ge(q_out, projected(c, 2))
                    b = n % NB
                    keys = slice(max(b - 1, 0) * P, (b + 1) * P)
                    for g in range(GQA):
                        r = slice((g % 2) * HD, (g % 2 + 1) * HD)
                        mm = pe.matmul(s_bank(n, g)[:, cols_of(n)], qT[r, g // 2, b * P:(b + 1) * P], kT[r, keys], start=True, stop=True)
                    mm.then_inc(s_mm, 1)

                def body(c, last):
                    def chunk(n):
                        g, f = CHUNK[n]
                        k = ORDER.index(n)
                        if n <= 5:
                            pe.wait_ge(z_out, c * Z_OUT + n)
                        elif n == 6:
                            pe.wait_ge(z_norm, c * 4 + 4)
                        else:
                            pe.wait_ge(q_out, projected(c, k))
                            pe.wait_ge(kt_done, c * 3 + 6)
                        pe.wait_ge(lo_done, c * 2 + 2 + f + 1)
                        for kk in range(KT):
                            cols = slice(g * TG, (g + 1) * TG)
                            mm = split_matmuls(pe, b7[:, 0:TG], (wH[:, f, kk, :], wL[:, f, kk, :]), (ch.xH[:, kk, cols], ch.xL[:, kk, cols]),
                                               kk == 0, kk == KT - 1)
                        mm.then_inc(q_mm, 1)

                    def turn(n):
                        pe.wait_ge(p_norm, c * NB + n + 1)
                        for kb in range(2):
                            pe.wait_ge(pt_hi if kb == 0 else pt_lo, c * NB + n)
                            for g in range(GQA):
                                src = kb if n > 0 else 1
                                tr = pe.transpose(banks[4 + kb][:, g * P:(g + 1) * P], S[:, n % 2, g, src * P:(src + 1) * P], ch.ident[:])
                            tr.then_inc(p_turned, 1)

                    def weigh(n):
                        pe.wait_ge(pt_hi, c * NB + n + 1)
                        pe.wait_ge(pt_lo, c * NB + n + 1)
                        pe.wait_ge(o_out, c * 2 * NB + 2 * n)
                        for kb in range(0 if n else 1, 2):
                            mm = pe.matmul(banks[6][:], Vd[:, n - 1 + kb].rearrange("p o d -> p (o d)"), PT[:, kb].rearrange("p g i -> p (g i)"),
                                           start=(kb == (0 if n else 1)), stop=(kb == 1))
                        mm.then_inc(o_mm, 1)

                    def sampled(step):
                        if step:
                            pe.wait_ge(z_out, c * Z_OUT + step)
                        else:
                            pe.wait_ge(z_norm, c * 4)
                            pe.wait_ge(q_out, projected(c, 0))
                        if step in CHUNK and not last:
                            pe.wait_ge(q_out, projected(c, ORDER.index(step)) + 1)
                        if step in (0, 1):
                            pe.wait_ge(ck_in, c * (32 * DB) + 32 * DB)
                            for b in range(4):
                                mm = pe.transpose(b7[:, b * P:(b + 1) * P], cK[:, 4 * step + b].rearrange("p o d -> p (o d)"), ch.ident[:])
                        if step == 2:
                            for par in range(2):
                                r = slice(par * HD, (par + 1) * HD)
                                qs = qT[r, :, SEQ:T].rearrange("p f (b i) -> p b f i", b=DB)
                                for b in range(DB):
                                    pe.matmul(b7[:, b * 16 + par * 8:b * 16 + par * 8 + 8].rearrange("p (f i) -> p f i", f=2),
                                              cKT[r, b, :], qs[:, b], start=True, stop=True)
                                mm = pe.matmul(b7[0:NS, P:2 * P].rearrange("p (b r f i) -> p r b f i", r=2, f=2, i=DL)[:, par],
                                               kT[r, SEQ:T], qs, start=True, stop=True)
                                if par == 0:
                                    mm.then_inc(z_par, 1)
                                    pe.wait_ge(z_par, c + 1)
                        if step == 3:
                            pe.transpose(b7[:, 0:P], ZT[:, 0, :], ch.ident[:])
                            mm = pe.transpose(b7[:, P:P + NS], ZT[0:NS, 1, :], ch.ident[0:NS, 0:NS])
                        if step == 4:
                            pe.wait_ge(z_red, c * 2 + 2)
                            pe.transpose(b7[:, 0:P], Z[:, 0:P], ch.ident[:])
                            mm = pe.transpose(b7[0:NS, P:2 * P], Z[:, P:P + NS], ch.ident[:])
                        if step == 5:
                            pe.wait_ge(cv_in, c * (32 * DB) + 32 * DB)
                            pe.matmul(b7[:, 0:P], Vd[0:NS, NB].rearrange("p o d -> p (o d)"), ZT[0:NS, 1, :], start=True, stop=False)
                            for b in range(DB):
                                mm = pe.matmul(b7[:, b * 16:(b + 1) * 16], cV[:, b].rearrange("p o d -> p (o d)"), ZT[:, 0, b * 16:(b + 1) * 16],
                                               start=False, stop=(b == DB - 1))
                        mm.then_inc(z_mm, 1)

                    pe.wait_ge(vd_done, c + 1)
                    for n in range(NB):
                        if n < NB - 1 or not last:
                            scores(c, n + 1)
                        if n >= 1:
                            weigh(n - 1)
                        if n in CHUNK and not last:
                            chunk(n)
                        if n == KEYS_AT and not last:
                            pe.wait_ge(q_out, projected(c, ORDER.index(n)) + 1)
                            turn_keys(c + 1, (0, 1, 7))
                        turn(n)
                        if n < Z_PER:
                            sampled(n)
                    weigh(NB - 1)

                turn_keys(0, (3, 6, 7))
                for f in range(2):
                    pe.wait_ge(lo_done, f + 1)
                    pe.wait_ge(kt_done, 3)
                    t_layout_product(pe, banks[3 * f:3 * f + 3], (wH[:, f], wL[:, f]), (ch.xH, ch.xL)).then_inc(q_mm, 1)
                pe.wait_ge(q_out, 2)
                scores(0, 0)
                walk(pe, body)


def stage_branch_attn(nc, ch):
    sem = ch.sem
    KINDS = 3
    w_in = ch.w_sems["branch"]
    hi_done, lo_done, mm_done = sem("b_hi"), sem("b_lo"), sem("b_mm")
    a_hi, a_lo = sem("b_ahi"), sem("b_alo")
    ga_out, gr_out, m1_out, gr_st, m1_st = sem("b_ga"), sem("b_gr"), sem("b_m1"), sem("b_grst"), sem("b_m1st")
    with ExitStack() as st:
        sb = ch.sbuf(st)
        brL, brH = sb("brL", [P, KT, T], F32R), sb("brH", [P, KT, T], F32R)
        raw = ch.raw
        wH, wL = sb("b_wH", [P, KINDS, KT, P], F32R), sb("b_wL", [P, KINDS, KT, P], F32R)
        ga, gr, m1 = sb("b_ga_s", [P, T]), sb("b_gr_s", [P, T]), sb("b_m1_s", [P, T])
        banks = ch.banks

        def bank_set(m2, q):
            b = 3 * ((m2 * KINDS + q) % 2)
            return banks[b:b + 3]

        def walk(eng, step):
            with eng.Fori(0, KT // 2 - 1) as j:
                for m2 in range(2):
                    step(j * 2 + m2, m2, False)
            step(KT - 2, 0, False)
            step(KT - 1, 1, True)

        with nc.Block() as block:
            @block.sync
            def _(sp):
                def load(m, q):
                    src = (ch.w_in[:, :, ds(m * P + C_GA, P)], ch.w_in[:, :, ds(m * P + C_GRT, P)], ch.w_attn[:, :, ds(m * P, P)])[q]
                    sp.dma_start(raw[:, q], src).then_inc(w_in[q], 16)

                with sp.Fori(1, KT) as m:
                    for q in range(KINDS):
                        sp.wait_ge(lo_done, m * KINDS - KINDS + q + 1)
                        apart(sp, ch)
                        load(m, q)
                sp.wait_ge(lo_done, KT * KINDS)
                first_loads(sp, ch, "retention")

            @block.gpsimd
            def _(pool):
                with pool.Fori(0, KT) as m:
                    pool.wait_ge(gr_out, m + 1)
                    apart(pool, ch)
                    pool.dma_start(ch.gate_t[:, ds(m, 1), :].rearrange("p o t -> p (o t)"), gr[:]).then_inc(gr_st, 16)
                    pool.wait_ge(m1_out, m + 1)
                    apart(pool, ch)
                    pool.dma_start(ch.m1_t[:, ds(m, 1), :].rearrange("p o t -> p (o t)"), m1[:]).then_inc(m1_st, 16)
                pool.wait_ge(gr_st, 16 * KT)
                pool.wait_ge(m1_st, 16 * KT)

            @block.scalar
            def _(act):
                def split_hi(m, q):
                    act.wait_ge(w_in[q], m * 16 + 16)
                    act.activation(wH[:, q], raw[:, q], ACT.Copy).then_inc(hi_done, 1)

                split_hi(0, 0)
                split_hi(0, 1)
                for k in range(KT):
                    act.activation(brH[:, k, :], ch.attn[:, k, :], ACT.Copy).then_inc(a_hi, 1)
                split_hi(0, 2)

                def step(m, m2, last):
                    act.wait_ge(m1_out, m)
                    act.wait_ge(gr_st, m * 16)
                    for q in range(KINDS):
                        act.wait_ge(mm_done, m * KINDS + q + 1)
                        if q < 2:
                            dst, done = ((ga, ga_out), (gr, gr_out))[q]
                            for g in range(3):
                                ins = act.activation(dst[:, g * TG:(g + 1) * TG], bank_set(m2, q)[g][:, 0:TG], ACT.Sigmoid)
                            ins.then_inc(done, 1)
                        if not last:
                            split_hi(m + 1, q)

                walk(act, step)

            @block.vector
            def _(dve):
                def split_lo(m, q):
                    dve.wait_ge(hi_done, m * KINDS + q + 1)
                    dve.tensor_tensor(wL[:, q], raw[:, q], wH[:, q].bitcast(F32), ALU.subtract).then_inc(lo_done, 1)

                split_lo(0, 0)
                split_lo(0, 1)
                for k in range(KT):
                    dve.wait_ge(a_hi, k + 1)
                    dve.tensor_tensor(brL[:, k, :], ch.attn[:, k, :], brH[:, k, :].bitcast(F32), ALU.subtract).then_inc(a_lo, 1)
                split_lo(0, 2)

                def step(m, m2, last):
                    if not last:
                        split_lo(m + 1, 0)
                        split_lo(m + 1, 1)
                    dve.wait_ge(mm_done, m * KINDS + 3)
                    dve.wait_ge(ga_out, m + 1)
                    dve.wait_ge(m1_st, m * 16)
                    for g in range(3):
                        cols = slice(g * TG, (g + 1) * TG)
                        ins = dve.tensor_tensor(m1[:, cols], bank_set(m2, 2)[g][:, 0:TG], ga[:, cols], ALU.mult)
                    ins.then_inc(m1_out, 1)
                    if not last:
                        split_lo(m + 1, 2)

                walk(dve, step)

            @block.tensor
            def _(pe):
                with pe.Fori(0, KT // 2) as j:
                    for m2 in range(2):
                        m = j * 2 + m2
                        for q, free in ((0, (gr_out, m)), (1, (m1_out, m)), (2, (ga_out, m + 1))):
                            pe.wait_ge(lo_done, m * KINDS + q + 1)
                            pe.wait_ge(*free)
                            if q == 2:
                                pe.wait_ge(a_lo, KT)
                            t_layout_product(pe, bank_set(m2, q), (wH[:, q], wL[:, q]), (ch.xH, ch.xL) if q < 2 else (brH, brL)).then_inc(mm_done, 1)


def stage_retention(nc, ch, ret):
    sem = ch.sem
    ORDER = [(C_GR, DV, 4), (C_GR + P, DV, 5), (C_QR, DK, 0), (C_KR, DK, 1), (C_VR, DV, 2), (C_VR + P, DV, 3)]
    PIECES = len(ORDER)
    w_in = ch.w_sems["retention"]
    tab_in, hi_done, lo_done, g_mm, sg_done, g_done = sem("r_tab"), sem("r_hi"), sem("r_lo"), sem("r_gmm"), sem("r_sg"), sem("r_g")
    p_mm, v_out, rot_a, rot_b, rot_done = sem("r_pmm"), sem("r_v"), sem("r_ra"), sem("r_rb"), sem("r_rot")
    turned, t_out, s_mm, s_out, o_mm, st_mm, st_out = (
        sem("r_t"), sem("r_tout"), sem("r_smm"), sem("r_sout"), sem("r_omm"), sem("r_stmm"), sem("r_stout"))
    sq_done, ss_mm, ms_done, root_done, rstd_done, og_done, r_done = (
        sem("r_sq"), sem("r_ssmm"), sem("r_ms"), sem("r_root"), sem("r_rstd"), sem("r_og"), sem("r_r"))
    s0_in, s0_new, s0_stored, stored = sem("r_s0"), sem("r_s0n"), sem("r_s0s"), sem("r_stored")
    km_done, z_mm, dec_done = sem("r_km"), sem("r_zmm"), sem("r_dec")
    with ExitStack() as st:
        sb = ch.sbuf(st)
        raw = ch.raw
        wH, wL = sb("r_wH", [P, KT, PIECES * P], F32R), sb("r_wL", [P, KT, PIECES * P], F32R)
        gs = sb("r_gs", [P, DVT, T])
        cos, sin = sb("r_cos", [P, NT, DK // 2]), sb("r_sin", [P, NT, DK // 2])
        decay, sdecay = sb("r_decay", [P, RH, P]), sb("r_sdecay", [NS, RH, NS])
        qdec, kdec, sqdec, cdec, scdec = (sb("r_" + n, [m, RH]) for n, m in (("qdec", P), ("kdec", P), ("sqdec", NS), ("cdec", P), ("scdec", P)))
        skdec = sb("r_skdec", [NS, DB, RH])
        dec = sb("r_dec_h", [P, 3])
        ones = sb("r_ones", [P, P])
        ta, tb = sb("r_ta", [P, 2, DK]), sb("r_tb", [P, 2, DK])
        rot = sb("r_rotd", [P, 2, 4, DK])
        v = sb("r_vn", [P, 3, DV])
        qkT = sb("r_qkT", [P, 3, P])
        sT = sb("r_sT", [P, P])
        S = sb("r_S", [P, DV])
        sq, og = sb("r_sqv", [P, DVT, P]), sb("r_ogv", [P, DVT, P])
        rstd = sb("r_rstdv", [P, P])
        S0 = sb("r_S0", [P, DB, DV])
        kmask = sb("r_kmask", [NS, 2, DK])
        banks = ch.banks
        half = DK // 2

        def out_bank(t, f):
            m = rows_of(t)
            if t == NB:
                return banks[4 + 3 * f][:, 0:m]
            return banks[4 + 3 * (t % 2)][:, f * P:f * P + m]

        def state_bank(b):
            return banks[5 if b % 2 else 3][:, 0:DV]

        with nc.Block() as block:
            @block.sync
            def _(sp):
                for dst, name in ((cos, "cos"), (sin, "sin"), (decay, "decay"), (sdecay, "samp_decay"), (qdec, "q_decay"), (kdec, "k_decay"),
                                  (sqdec, "samp_q_decay"), (cdec, "c_decay"), (scdec, "samp_c_decay"), (skdec, "samp_k_decay"), (ones, "ones")):
                    sp.dma_start(dst[:], ch.c[name]).then_inc(tab_in, 16)

                def load(h, p):
                    c0, step, _ = ORDER[p % PIECES]
                    sp.wait_ge(lo_done, h * PIECES + p - 1)
                    apart(sp, ch)
                    sp.dma_start(raw[:, p % 2], ch.w_in[:, :, ds((h + p // PIECES) * step + c0, P)]).then_inc(w_in[p % 2], 16)

                with sp.Fori(0, RH - 1) as h:
                    for p in range(2, PIECES + 2):
                        load(h, p)
                for p in range(2, PIECES):
                    load(RH - 1, p)
                sp.wait_ge(lo_done, RH * PIECES)
                first_loads(sp, ch, "merge")

            @block.gpsimd
            def _(pool):
                pool.wait_ge(tab_in, 16 * 11)
                with pool.Fori(0, RH) as h:
                    pool.wait_ge(rot_done, h * NT)
                    pool.tensor_copy(dec[:, 0:1], qdec[:, ds(h, 1)])
                    pool.tensor_copy(dec[:, 1:2], kdec[:, ds(h, 1)])
                    pool.tensor_copy(dec[0:NS, 2:3], sqdec[:, ds(h, 1)]).then_inc(dec_done, 1)
                    pool.wait_ge(s0_stored, h * 16)
                    apart(pool, ch)
                    pool.dma_start(S0[:], ch.state_ret[:, ds(h, 1)].rearrange("b o d e -> d (b o) e")).then_inc(s0_in, 16)
                    for t in range(NT):
                        m = rows_of(t)
                        n = h * NT + t + 1
                        r = rot[0:m, t % 2]
                        a, b = (x[0:m].rearrange("p a (s d) -> p a s d", s=2) for x in (ta, tb))
                        dst = r.rearrange("p (a b) (s d) -> p a b s d", b=2, s=2)[:, :, 0]
                        pool.wait_ge(rot_a, n)
                        if t >= 2:
                            pool.wait_ge(turned, n - 2)
                            pool.wait_ge(st_mm, h * NB + t - 1)
                        else:
                            pool.wait_ge(turned, h * NT)
                            pool.wait_ge(st_mm, h * NB)
                            pool.wait_ge(km_done, h * DB)
                        pool.tensor_tensor(dst[:, :, 0], a[:, :, 0], b[:, :, 1], ALU.subtract)
                        pool.tensor_tensor(dst[:, :, 1], a[:, :, 1], b[:, :, 0], ALU.add).then_inc(rot_b, 1)
                        pool.wait_ge(rot_b, n)
                        pool.wait_ge(dec_done, h + 1)
                        apart(pool, ch)
                        col = 0 if t < NB else 2
                        pool.tensor_scalar(r[:, 1, :], r[:, 0, :], dec[0:m, col:col + 1], None, ALU.mult)
                        pool.tensor_scalar(r[:, 3, :], r[:, 2, :], dec[0:m, 1:2], None, ALU.mult).then_inc(rot_done, 1)
                    pool.wait_ge(st_out, h * NB + NB)
                    apart(pool, ch)
                    pool.dma_start(ch.new_state_prompt[ds(h, 1)].rearrange("o d e -> d (o e)"), S[:]).then_inc(stored, 16)
                    pool.wait_ge(s0_new, h * DB + DB)
                    apart(pool, ch)
                    pool.dma_start(ch.new_state_sample[:, ds(h, 1)].rearrange("b o d e -> d (b o) e"), S0[:]).then_inc(s0_stored, 16)
                pool.wait_ge(stored, 16 * RH)
                pool.wait_ge(s0_stored, 16 * RH)

            @block.scalar
            def _(act):
                with act.Fori(0, RH) as h:
                    for p, (_, _, slot) in enumerate(ORDER):
                        act.wait_ge(w_in[p % 2], h * 48 + 16 * (p // 2 + 1))
                        if p == 0:
                            act.wait_ge(g_mm, h * 2)
                        if p == 2:
                            act.wait_ge(p_mm, h * NT)
                        act.activation(wH[:, :, slot * P:(slot + 1) * P], raw[:, p % 2], ACT.Copy).then_inc(hi_done, 1)
                    act.wait_ge(r_done, h * NT)
                    for f in range(DVT):
                        act.wait_ge(g_mm, h * 2 + f + 1)
                        for g in range(3):
                            ins = act.activation(gs[:, f, g * TG:(g + 1) * TG], banks[3 * f + g][:, 0:TG], ACT.Sigmoid)
                        ins.then_inc(sg_done, 1)

                    def evac_v(t):
                        m = rows_of(t)
                        act.wait_ge(p_mm, h * NT + t + 1)
                        if t >= 3:
                            act.wait_ge(o_mm, h * NT + t - 2)
                            act.wait_ge(st_mm, h * NB + t - 2)
                        else:
                            act.wait_ge(o_mm, h * NT)
                            act.wait_ge(z_mm, h * DB)
                        act.activation(v[0:m, t % 3], banks[t % 2][0:m, 2 * P:4 * P], ACT.Copy).then_inc(v_out, 1)

                    evac_v(0)
                    evac_v(1)
                    for t in range(NT):
                        m = rows_of(t)
                        act.wait_ge(turned, h * NT + t + 1)
                        act.activation(qkT[:, :, 0:m], banks[2][:, 0:3 * P].rearrange("p (a i) -> p a i", a=3)[:, :, 0:m], ACT.Copy).then_inc(t_out, 1)
                        if t + 2 < NT:
                            evac_v(t + 2)
                        act.wait_ge(o_mm, h * NT + t + 1)
                        act.wait_ge(ss_mm, h * NT + t)
                        for f in range(DVT):
                            ins = act.activation(sq[:, f, 0:m], out_bank(t, f), ACT.Square)
                        ins.then_inc(sq_done, 1)
                        act.wait_ge(ms_done, h * NT + t + 1)
                        act.activation(rstd[:, 0:m], rstd[:, 0:m], ACT.Sqrt).then_inc(root_done, 1)

            @block.vector
            def _(dve):
                with dve.Fori(0, RH) as h:
                    for p, (_, _, slot) in enumerate(ORDER):
                        dve.wait_ge(hi_done, h * PIECES + p + 1)
                        cols = slice(slot * P, (slot + 1) * P)
                        dve.tensor_tensor(wL[:, :, cols], raw[:, p % 2], wH[:, :, cols].bitcast(F32), ALU.subtract).then_inc(lo_done, 1)
                    for f in range(DVT):
                        dve.wait_ge(sg_done, h * 2 + f + 1)
                        for g in range(3):
                            cols = slice(g * TG, (g + 1) * TG)
                            ins = dve.tensor_tensor(gs[:, f, cols], banks[3 * f + g][:, 0:TG], gs[:, f, cols], ALU.mult)
                        ins.then_inc(g_done, 1)
                    dve.wait_ge(tab_in, 16 * 11)

                    def products(t):
                        m = rows_of(t)
                        x = banks[t % 2][0:m, 0:2 * P].rearrange("p (a d) -> p a d", a=4)
                        dve.wait_ge(v_out, h * NT + t + 1)
                        dve.wait_ge(rot_b, h * NT + t)
                        for dst, tab in ((ta, cos), (tb, sin)):
                            ins = dve.tensor_tensor(dst[0:m].rearrange("p a (s d) -> p (a s) d", s=2), x,
                                                    tab[0:m, t, :].rearrange("p (a d) -> p a d", a=1).broadcast_to([m, 4, half]), ALU.mult)
                        ins.then_inc(rot_a, 1)

                    products(0)
                    products(1)
                    for t in range(NT):
                        m = rows_of(t)
                        n = h * NT + t + 1
                        dve.wait_ge(s_mm, n)
                        dve.tensor_tensor(sT[0:m, 0:m], banks[3][0:m, 0:m],
                                          (decay if t < NB else sdecay)[0:m, ds(h, 1), 0:m].rearrange("p o i -> p (o i)"), ALU.mult).then_inc(s_out, 1)
                        if t + 2 < NT:
                            products(t + 2)
                        if t < NB:
                            dve.wait_ge(st_mm, h * NB + t + 1)
                            if t == 0:
                                dve.wait_ge(stored, h * 16)
                                dve.tensor_copy(S[:], banks[5][:, 0:DV]).then_inc(st_out, 1)
                            else:
                                dve.scalar_tensor_tensor(out=S[:], in0=S[:], scalar=cdec[:, ds(h, 1)], in1=banks[5][:, 0:DV],
                                                         op0=ALU.mult, op1=ALU.add).then_inc(st_out, 1)
                        else:
                            dve.wait_ge(s0_in, h * 16 + 16)
                            for b in range(DB + 1):
                                if b < DB:
                                    if b >= 2:
                                        dve.wait_ge(z_mm, h * DB + b - 1)
                                    dve.tensor_scalar(kmask[:, b % 2], rot[0:NS, t % 2, 2, :], skdec[:, b, ds(h, 1)], None, ALU.mult).then_inc(km_done, 1)
                                if b >= 1:
                                    dve.wait_ge(z_mm, h * DB + b)
                                    dve.scalar_tensor_tensor(out=S0[:, b - 1], in0=S0[:, b - 1], scalar=scdec[:, ds(h, 1)], in1=state_bank(b - 1),
                                                             op0=ALU.mult, op1=ALU.add).then_inc(s0_new, 1)
                        dve.wait_ge(sq_done, n)
                        dve.wait_ge(r_done, n - 1)
                        for f in range(DVT):
                            ins = dve.tensor_tensor(og[:, f, 0:m], out_bank(t, f), gs[:, f, t * P:t * P + m], ALU.mult)
                        ins.then_inc(og_done, 1)
                        dve.wait_ge(ss_mm, n)
                        dve.tensor_scalar(rstd[:, 0:m], banks[6][:, 0:m], 1.0 / DV, EPS, ALU.mult, ALU.add).then_inc(ms_done, 1)
                        dve.wait_ge(root_done, n)
                        dve.reciprocal(rstd[:, 0:m], rstd[:, 0:m]).then_inc(rstd_done, 1)
                        dve.wait_ge(rstd_done, n)
                        dve.wait_ge(og_done, n)
                        dve.tensor_tensor(ret[:, ds(h * DVT, DVT), t * P:t * P + m], og[:, :, 0:m],
                                          rstd[:, 0:m].rearrange("p (o i) -> p o i", o=1).broadcast_to([P, DVT, m]), ALU.mult).then_inc(r_done, 1)

            @block.tensor
            def _(pe):
                with pe.Fori(0, RH) as h:
                    pe.wait_ge(v_out, h * NT)
                    pe.wait_ge(og_done, h * NT)
                    pe.wait_ge(sq_done, h * NT)
                    pe.wait_ge(s0_new, h * DB)
                    for f in range(DVT):
                        pe.wait_ge(lo_done, h * PIECES + f + 1)
                        w = [x[:, :, (4 + f) * P:(5 + f) * P] for x in (wH, wL)]
                        t_layout_product(pe, banks[3 * f:3 * f + 3], w, (ch.xH, ch.xL)).then_inc(g_mm, 1)

                    def project(t, ks):
                        m = rows_of(t)
                        if ks[0] == 0:
                            if t < 2:
                                pe.wait_ge(g_done, h * 2 + 1)
                            else:
                                pe.wait_ge(v_out, h * NT + t - 1)
                                pe.wait_ge(rot_a, h * NT + t - 1)
                        for k in ks:
                            mm = split_matmuls(pe, banks[t % 2][0:m, :], (ch.xH[:, k, t * P:t * P + m], ch.xL[:, k, t * P:t * P + m]),
                                               (wH[:, k, 0:4 * P], wL[:, k, 0:4 * P]), k == 0, k == KT - 1)
                        if ks[-1] == KT - 1:
                            mm.then_inc(p_mm, 1)

                    def sum_squares(t):
                        m = rows_of(t)
                        pe.wait_ge(sq_done, h * NT + t + 1)
                        pe.wait_ge(ms_done, h * NT + t)
                        for f in range(DVT):
                            mm = pe.matmul(banks[6][:, 0:m], ones[:], sq[:, f, 0:m], start=(f == 0), stop=(f == DVT - 1))
                        mm.then_inc(ss_mm, 1)

                    pe.wait_ge(lo_done, h * PIECES + PIECES)
                    pe.wait_ge(tab_in, 16 * 11)
                    project(0, range(KT))
                    project(1, range(KT))
                    pe.wait_ge(g_done, h * 2 + 2)
                    for t in range(NT):
                        m = rows_of(t)
                        n = h * NT + t + 1
                        pe.wait_ge(rot_done, n)
                        pe.wait_ge(t_out, n - 1)
                        if t == NB:
                            apart(pe, ch)
                        for a in range(3):
                            tr = pe.transpose(banks[2][:, a * P:a * P + m], rot[0:m, t % 2, a, :], ch.ident[0:m, 0:m])
                        tr.then_inc(turned, 1)
                        if t >= 1:
                            sum_squares(t - 1)
                        if t + 2 < NT:
                            project(t + 2, range(KT // 2))
                        pe.wait_ge(t_out, n)
                        pe.wait_ge(s_out, n - 1)
                        pe.matmul(banks[3][0:m, 0:m], qkT[:, 2, 0:m], qkT[:, 0, 0:m], start=True, stop=True).then_inc(s_mm, 1)
                        if t + 2 < NT:
                            project(t + 2, range(KT // 2, KT))
                        pe.wait_ge(s_out, n)
                        pe.wait_ge(v_out, n)
                        if t >= 2:
                            pe.wait_ge(og_done, n - 2 if t < NB else n - 1)
                            pe.wait_ge(sq_done, n - 2 if t < NB else n - 1)
                        if t < NB:
                            if t:
                                pe.wait_ge(st_out, h * NB + t)
                            for f in range(DVT):
                                cols = slice(f * P, (f + 1) * P)
                                mm = pe.matmul(out_bank(t, f), v[:, t % 3, cols], sT[:], start=True, stop=(t == 0))
                                if t:
                                    mm = pe.matmul(out_bank(t, f), S[:, cols], qkT[:, 1, :], start=False, stop=True)
                            mm.then_inc(o_mm, 1)
                            pe.matmul(banks[5][:, 0:DV], rot[:, t % 2, 3, :], v[:, t % 3], start=True, stop=True).then_inc(st_mm, 1)
                        else:
                            pe.wait_ge(s0_in, h * 16 + 16)
                            for f in range(DVT):
                                pe.matmul(out_bank(t, f), v[0:m, t % 3, f * P:(f + 1) * P], sT[0:m, 0:m], start=True, stop=False)
                                for b in range(DB):
                                    mm = pe.matmul(out_bank(t, f)[:, b * DL:(b + 1) * DL], S0[:, b, f * P:(f + 1) * P],
                                                   qkT[:, 1, b * DL:(b + 1) * DL], start=False, stop=(b == DB - 1))
                            mm.then_inc(o_mm, 1)
                            pe.wait_ge(st_out, h * NB + NB)
                            for b in range(DB):
                                if b >= 2:
                                    pe.wait_ge(s0_new, h * DB + b - 1)
                                pe.wait_ge(km_done, h * DB + b + 1)
                                pe.matmul(state_bank(b), kmask[:, b % 2], v[0:NS, t % 3], start=True, stop=True).then_inc(z_mm, 1)
                    sum_squares(NT - 1)


def stage_merge(nc, ch, ret):
    sem = ch.sem
    w_in, hi_done, lo_done, mm_done = ch.w_sems["merge"], sem("m_hi"), sem("m_lo"), sem("m_mm")
    r_hi, r_lo, g_in, m_in, g_mul, sum_done, mh_done, ml_done = (
        sem("m_rhi"), sem("m_rlo"), [sem("m_g0"), sem("m_g1")], [sem("m_m0"), sem("m_m1")], sem("m_gmul"), sem("m_sum"), sem("m_mh"), sem("m_ml"))
    with ExitStack() as st:
        sb = ch.sbuf(st)
        rL, rH = sb("m_rL", [P, KT, T], F32R), sb("m_rH", [P, KT, T], F32R)
        raw = ch.raw
        wH, wL = sb("m_wH", [P, 2, KT, P], F32R), sb("m_wL", [P, 2, KT, P], F32R)
        gate, m1 = sb("m_gate", [P, 2, T]), sb("m_m1", [P, 2, T])
        banks = ch.banks

        def walk(eng, step):
            with eng.Fori(0, KT // 2 - 1) as j:
                for s in range(2):
                    step(j, s, False)
            for s in range(2):
                step(KT // 2 - 1, s, True)

        with nc.Block() as block:
            @block.sync
            def _(sp):
                with sp.Fori(1, KT // 2) as j:
                    for s in range(2):
                        m = j * 2 + s
                        sp.wait_ge(lo_done, m - 1)
                        apart(sp, ch)
                        sp.dma_start(raw[:, s], ch.w_ret[:, :, ds(m * P, P)]).then_inc(w_in[s], 16)
                sp.wait_ge(lo_done, KT)
                first_loads(sp, ch, "out")

            @block.gpsimd
            def _(pool):
                def load(m, s):
                    pool.dma_start(gate[:, s], ch.gate_t[:, ds(m, 1), :].rearrange("p o t -> p (o t)")).then_inc(g_in[s], 16)
                    pool.dma_start(m1[:, s], ch.m1_t[:, ds(m, 1), :].rearrange("p o t -> p (o t)")).then_inc(m_in[s], 16)

                for s in range(2):
                    load(s, s)
                with pool.Fori(1, KT // 2) as j:
                    for s in range(2):
                        pool.wait_ge(ml_done, j * 2 + s - 1)
                        apart(pool, ch)
                        load(j * 2 + s, s)

            @block.scalar
            def _(act):
                def step(j, s, last):
                    m = j * 2 + s
                    if not last:
                        act.wait_ge(w_in[s], j * 16 + 32)
                        act.wait_ge(mm_done, m + 1)
                        act.activation(wH[:, s], raw[:, s], ACT.Copy).then_inc(hi_done, 1)
                    act.wait_ge(sum_done, m + 1)
                    act.activation(ch.xH[:, ds(m, 1), :], gate[:, s:s + 1], ACT.Copy).then_inc(mh_done, 1)

                act.wait_ge(w_in[0], 16)
                act.activation(wH[:, 0], raw[:, 0], ACT.Copy).then_inc(hi_done, 1)
                for k in range(KT):
                    act.activation(rH[:, k, :], ret[:, k, :], ACT.Copy).then_inc(r_hi, 1)
                act.wait_ge(w_in[1], 16)
                act.activation(wH[:, 1], raw[:, 1], ACT.Copy).then_inc(hi_done, 1)
                walk(act, step)

            @block.vector
            def _(dve):
                def split_lo(s, count):
                    dve.wait_ge(hi_done, count)
                    dve.tensor_tensor(wL[:, s], raw[:, s], wH[:, s].bitcast(F32), ALU.subtract).then_inc(lo_done, 1)

                def step(j, s, last):
                    m = j * 2 + s
                    if not last:
                        split_lo(s, m + 3)
                    dve.wait_ge(mm_done, m + 1)
                    dve.wait_ge(g_in[s], j * 16 + 16)
                    dve.wait_ge(m_in[s], j * 16 + 16)
                    for g in range(3):
                        cols = slice(g * TG, (g + 1) * TG)
                        ins = dve.tensor_tensor(gate[:, s, cols], banks[3 * s + g][:, 0:TG], gate[:, s, cols], ALU.mult)
                    ins.then_inc(g_mul, 1)
                    dve.wait_ge(g_mul, m + 1)
                    dve.tensor_tensor(gate[:, s], gate[:, s], m1[:, s], ALU.add).then_inc(sum_done, 1)
                    dve.wait_ge(mh_done, m + 1)
                    dve.tensor_tensor(ch.xL[:, ds(m, 1), :], gate[:, s:s + 1], ch.xH[:, ds(m, 1), :].bitcast(F32), ALU.subtract).then_inc(ml_done, 1)

                split_lo(0, 1)
                for k in range(KT):
                    dve.wait_ge(r_hi, k + 1)
                    dve.tensor_tensor(rL[:, k, :], ret[:, k, :], rH[:, k, :].bitcast(F32), ALU.subtract).then_inc(r_lo, 1)
                split_lo(1, 2)
                walk(dve, step)

            @block.tensor
            def _(pe):
                def product(s, m, ready=None):
                    pe.wait_ge(lo_done, m + 1)
                    t_layout_product(pe, banks[3 * s:3 * s + 3], (wH[:, s], wL[:, s]), (rH, rL), ready).then_inc(mm_done, 1)

                product(0, 0, lambda k: pe.wait_ge(r_lo, k + 1))
                product(1, 1)
                with pe.Fori(1, KT // 2) as j:
                    for s in range(2):
                        m = j * 2 + s
                        pe.wait_ge(g_mul, m - 1)
                        product(s, m)


def stage_out(nc, ch):
    sem = ch.sem
    w_in, hi_done, lo_done, mm_done, x_in = ch.w_sems["out"], sem("o_hi"), sem("o_lo"), sem("o_mm"), [sem("o_x0"), sem("o_x1")]
    tab_in, add_done, sq_done, ms_done, root_done, rstd_done, xn_done = (
        sem("o_tab"), sem("o_add"), sem("o_sq"), sem("o_ms"), sem("o_root"), sem("o_rstd"), sem("o_xn"))
    x2_st, xn_st, turned, t_out0, t_out1, r_mm, r_out = ([sem("o_x2s0"), sem("o_x2s1")], [sem("o_xns0"), sem("o_xns1")], sem("o_t"), sem("o_to0"), sem("o_to1"),
                                                        sem("o_rmm"), sem("o_rout"))
    NH = D // 512
    with ExitStack() as st:
        sb = ch.sbuf(st)
        raw = ch.raw
        wH, wL = sb("o_wH", [P, KT, D], F32R), sb("o_wL", [P, KT, D], F32R)
        xin, x2, xn = sb("o_xin", [P, 2, D]), sb("o_x2s", [P, 2, D]), sb("o_xns", [P, 2, D])
        junk, gain = sb("o_junk", [P, D]), sb("o_gain", [P, D])
        stat = sb("o_stat", [P, 2, 4])
        xT = sb("o_xT", [P, KT, P])
        wr, rb = sb("o_wr", [P, KT, NG + NE]), sb("o_rb", [P, NG + NE])
        banks = ch.banks
        with nc.Block() as block:
            @block.sync
            def _(sp):
                for q in range(2, KT):
                    sp.wait_ge(lo_done, q - 1)
                    sp.dma_start(raw[:, q % 2], ch.w_out[:, :, q * P:(q + 1) * P]).then_inc(w_in[q % 2], 16)
                for t in range(NT):
                    m, s = rows_of(t), t % 2
                    if t >= 2:
                        sp.wait_ge(add_done, t - 1)
                    src = ch.x_sample if t == NB else ch.x_prompt[t * P:(t + 1) * P, :]
                    sp.dma_start(xin[0:m, s], src).then_inc(x_in[s], 16)

            @block.gpsimd
            def _(pool):
                for dst, src in ((gain[:], ch.norm_ffn.broadcast_to([P, D])), (wr[:, :, 0:NG], ch.w_rg), (wr[:, :, NG:], ch.w_re),
                                 (rb[:, 0:NG], ch.b_rg.broadcast_to([P, NG])), (rb[:, NG:], ch.b_re.broadcast_to([P, NE]))):
                    pool.dma_start(dst, src).then_inc(tab_in, 16)
                for t in range(NT):
                    m, s = rows_of(t), t % 2
                    pool.wait_ge(add_done, t + 1)
                    pool.dma_start(ch.x2_d[t * P:t * P + m, :], x2[0:m, s]).then_inc(x2_st[s], 16)
                    pool.wait_ge(xn_done, t + 1)
                    pool.dma_start(ch.xn2_d[t * P:t * P + m, :], xn[0:m, s]).then_inc(xn_st[s], 16)
                for s in range(2):
                    n = 16 * ((NT + 1 - s) // 2)
                    pool.wait_ge(x2_st[s], n)
                    pool.wait_ge(xn_st[s], n)

            @block.scalar
            def _(act):
                for q in range(KT):
                    act.wait_ge(w_in[q % 2], 16 * (q // 2 + 1))
                    act.activation(wH[:, :, q * P:(q + 1) * P], raw[:, q % 2], ACT.Copy).then_inc(hi_done, 1)

                def front(t):
                    m, s = rows_of(t), t % 2
                    act.wait_ge(add_done, t + 1)
                    act.activation(junk[0:m], x2[0:m, s], ACT.Square, accum_out=stat[0:m, s, 0:1]).then_inc(sq_done, 1)
                    act.wait_ge(ms_done, t + 1)
                    act.activation(stat[0:m, s, 2:3], stat[0:m, s, 1:2], ACT.Sqrt).then_inc(root_done, 1)

                def back(t):
                    m = rows_of(t)
                    act.wait_ge(turned, t * 2 + 1)
                    act.wait_ge(r_mm, t)
                    act.activation(xT[:, 0:4, 0:m], banks[4][:].rearrange("p (k i) -> p k i", k=4)[:, :, 0:m], ACT.Copy).then_inc(t_out0, 1)

                for t in range(NT + 1):
                    if t < NT:
                        front(t)
                    if t >= 1:
                        back(t - 1)

            @block.vector
            def _(dve):
                dve.memset(ch.logits[:], 0.0).then_inc(r_out, 1)
                for q in range(KT):
                    dve.wait_ge(hi_done, q + 1)
                    cols = slice(q * P, (q + 1) * P)
                    dve.tensor_tensor(wL[:, :, cols], raw[:, q % 2], wH[:, :, cols].bitcast(F32), ALU.subtract).then_inc(lo_done, 1)
                dve.wait_ge(tab_in, 16 * 5)

                def front(t):
                    m, s = rows_of(t), t % 2
                    dve.wait_ge(mm_done, t + 1)
                    dve.wait_ge(x_in[s], 16 * (t // 2 + 1))
                    if t >= 2:
                        dve.wait_ge(x2_st[s], 16 * (t // 2))
                        dve.wait_ge(sq_done, t - 1)
                    for f in range(NH):
                        cols = slice(f * 512, (f + 1) * 512)
                        ins = dve.tensor_tensor(x2[0:m, s, cols], banks[2 * s + f][0:m, :], xin[0:m, s, cols], ALU.add)
                    ins.then_inc(add_done, 1)
                    dve.wait_ge(sq_done, t + 1)
                    dve.tensor_scalar(stat[0:m, s, 1:2], stat[0:m, s, 0:1], 1.0 / D, EPS, ALU.mult, ALU.add).then_inc(ms_done, 1)
                    dve.wait_ge(root_done, t + 1)
                    dve.reciprocal(stat[0:m, s, 3:4], stat[0:m, s, 2:3]).then_inc(rstd_done, 1)
                    dve.wait_ge(rstd_done, t + 1)
                    if t >= 2:
                        dve.wait_ge(xn_st[s], 16 * (t // 2))
                        dve.wait_ge(turned, 2 * (t - 1))
                    dve.scalar_tensor_tensor(out=xn[0:m, s], in0=x2[0:m, s], scalar=stat[0:m, s, 3:4], in1=gain[0:m],
                                             op0=ALU.mult, op1=ALU.mult).then_inc(xn_done, 1)

                def back(t):
                    m = rows_of(t)
                    dve.wait_ge(turned, t * 2 + 2)
                    dve.wait_ge(r_mm, t)
                    dve.tensor_copy(xT[:, 4:8, 0:m], banks[5][:].rearrange("p (k i) -> p k i", k=4)[:, :, 0:m]).then_inc(t_out1, 1)

                def logits(t):
                    m = rows_of(t)
                    dve.wait_ge(r_mm, t + 1)
                    dve.wait_ge(r_out, 1)
                    dve.tensor_tensor(ch.logits[0:m, t, :], banks[6][0:m, 0:NG + NE], rb[0:m, :], ALU.add).then_inc(r_out, 1)

                for t in range(NT + 2):
                    if t < NT:
                        front(t)
                    if t >= 2:
                        logits(t - 2)
                    if 1 <= t <= NT:
                        back(t - 1)

            @block.tensor
            def _(pe):
                def project(t):
                    m, s = rows_of(t), t % 2
                    if t >= 2:
                        pe.wait_ge(add_done, t - 1)
                    for f in range(NH):
                        pe.wait_ge(lo_done, (f + 1) * KT // NH)
                        for k in range(KT):
                            rows, cols = slice(t * P, t * P + m), slice(f * 512, (f + 1) * 512)
                            mm = split_matmuls(pe, banks[2 * s + f][0:m, :], (ch.xH[:, k, rows], ch.xL[:, k, rows]),
                                               (wH[:, k, cols], wL[:, k, cols]), k == 0, k == KT - 1)
                    mm.then_inc(mm_done, 1)

                def turn(t):
                    m, s = rows_of(t), t % 2
                    pe.wait_ge(xn_done, t + 1)
                    pe.wait_ge(t_out0, t)
                    pe.wait_ge(t_out1, t)
                    for b in range(2):
                        for k in range(4):
                            tr = pe.transpose(banks[4 + b][:, k * P:k * P + m], xn[0:m, s, (4 * b + k) * P:(4 * b + k + 1) * P], ch.ident[0:m, 0:m])
                        tr.then_inc(turned, 1)

                def route(t):
                    m = rows_of(t)
                    pe.wait_ge(t_out0, t + 1)
                    pe.wait_ge(t_out1, t + 1)
                    pe.wait_ge(r_out, t + 1)
                    for k in range(KT):
                        mm = pe.matmul(banks[6][0:m, 0:NG + NE], xT[:, k, 0:m], wr[:, k, :], start=(k == 0), stop=(k == KT - 1))
                    mm.then_inc(r_mm, 1)

                pe.wait_ge(tab_in, 16 * 5)
                for t in range(NT + 2):
                    if t < NT:
                        project(t)
                    if t >= 2:
                        route(t - 2)
                    if 1 <= t <= NT:
                        turn(t - 1)


def stage_route(nc, ch):
    sem = ch.sem
    step, tab_in, e_done, c_mm, scat, zeroed = sem("t_step"), sem("t_tab"), sem("t_exp"), sem("t_mm"), sem("t_scat"), sem("t_zero")
    with ExitStack() as st:
        sb = ch.sbuf(st)
        iota = sb("t_iota", [P, P])
        before, ones = sb("t_before", [P, P]), sb("t_ones", [P, P])
        tokens = sb("t_tokens", [P, NT], I32)
        noexp = sb("t_noexp", [P, NT])
        g8, gm8, f8, fm8 = (sb("t_" + n, [P, NT, 8]) for n in ("g8", "gm8", "f8", "fm8"))
        gi8, fi8 = sb("t_gi8", [P, NT, 8], U32), sb("t_fi8", [P, NT, 8], U32)
        gidx, gw, e2, den = (sb("t_" + n, [P, NT]) for n in ("gidx", "gw", "e2", "den"))
        eg, goh = sb("t_eg", [P, NT, NG]), sb("t_goh", [P, NT, NG])
        prod = sb("t_prod", [P, NT, EPG, NG])
        eid = sb("t_eid", [P, NT, 2])
        hot = sb("t_hot", [P, NT, 2, NE])
        both, tot, before_t, slotv, over = (sb("t_" + n, [P, NT, NE]) for n in ("both", "tot", "tp", "slotv", "over"))
        cnt, nov, delta, scan = sb("t_cnt", [P, NE]), sb("t_nov", [P, NE]), sb("t_delta", [P, NE]), sb("t_scan", [P, 2, NE])
        thr, cmp = sb("t_thr", [P, MAXBLK - 1]), sb("t_cmp", [P, NE, MAXOVER])
        slotp, slotf = sb("t_slotp", [P, NT, 2, NE]), sb("t_slotf", [P, NT, 2])
        tabf = sb("t_tabf", [P, 1 + MAXOVER])
        banks = ch.banks

        def across(ap, n):
            return ap.rearrange("p (a o) -> p a o", o=1).broadcast_to([P, ap.shape[1], n])

        with nc.Block() as block:
            @block.sync
            def _(sp):
                for dst, name in ((iota, "iota"), (before, "before"), (ones, "ones"), (tokens, "tokens"), (noexp, "no_expert")):
                    sp.dma_start(dst[:], ch.c[name]).then_inc(tab_in, 16)
                sp.dma_start(ch.toktab.rearrange("(b p) o -> b (p o)", p=P), ch.c["zero_slots"]).then_inc(zeroed, 16)

            @block.scalar
            def _(act):
                act.wait_ge(step, ch.route_steps["group"])
                act.activation(eg[:], eg[:], ACT.Exp).then_inc(e_done, 1)
                act.wait_ge(step, ch.route_steps["pair"])
                act.activation(e2[:], e2[:], ACT.Exp).then_inc(e_done, 1)

            @block.vector
            def _(dve):
                count = [0]

                def done(ins):
                    ins.then_inc(step, 1)
                    count[0] += 1
                    dve.wait_ge(step, count[0])

                dve.wait_ge(tab_in, 16 * 5)
                LG = ch.logits
                done(dve.memset(g8[:], -3e38))
                done(dve.tensor_copy(g8[:, :, 0:NG], LG[:, :, 0:NG]))
                for t in range(NT):
                    done(dve.max(gm8[:, t, :], g8[:, t, :]))
                    done(dve.max_index(gi8[:, t, :], gm8[:, t, :], g8[:, t, :]))
                done(dve.tensor_tensor(eg[:], LG[:, :, 0:NG], gm8[:, :, 0:1].broadcast_to([P, NT, NG]), ALU.subtract))
                assert count[0] == ch.route_steps["group"]
                done(dve.tensor_copy(gidx[:], gi8[:, :, 0]))
                done(dve.tensor_tensor(goh[:], across(gidx[:], NG), iota[:, None, 0:NG].broadcast_to([P, NT, NG]), ALU.is_equal))
                done(dve.tensor_tensor(prod[:], LG[:, :, NG:].rearrange("p t (g e) -> p t e g", g=NG),
                                       goh[:].rearrange("p t (o g) -> p t o g", o=1).broadcast_to([P, NT, EPG, NG]), ALU.mult))
                done(dve.tensor_reduce(f8[:], prod[:], AX, ALU.add))
                for t in range(NT):
                    done(dve.max(fm8[:, t, :], f8[:, t, :]))
                    done(dve.max_index(fi8[:, t, :], fm8[:, t, :], f8[:, t, :]))
                done(dve.tensor_tensor(e2[:], fm8[:, :, 1], fm8[:, :, 0], ALU.subtract))
                assert count[0] == ch.route_steps["pair"]
                done(dve.tensor_copy(eid[:], fi8[:, :, 0:2]))
                done(dve.scalar_tensor_tensor(out=gidx[:], in0=gidx[:], scalar=float(EPG), in1=noexp[:], op0=ALU.mult, op1=ALU.add))
                done(dve.tensor_tensor(eid[:], eid[:], across(gidx[:], 2), ALU.add))
                done(dve.tensor_tensor(hot[:].rearrange("p t k e -> p (t k) e"), across(eid[:].rearrange("p t k -> p (t k)"), NE),
                                       iota[:, None, 0:NE].broadcast_to([P, 2 * NT, NE]), ALU.is_equal))
                done(dve.tensor_tensor(both[:], hot[:, :, 0, :], hot[:, :, 1, :], ALU.add))
                assert count[0] == ch.route_steps["hot"]
                dve.wait_ge(e_done, 2)
                done(dve.tensor_reduce(den[:], eg[:], AX, ALU.add))
                done(dve.reciprocal(gw[:], den[:]))
                done(dve.tensor_scalar(den[:], e2[:], 1.0, None, ALU.add))
                done(dve.reciprocal(den[:], den[:]))
                done(dve.tensor_tensor(ch.gates[:, :, 0], gw[:], den[:], ALU.mult))
                done(dve.tensor_tensor(ch.gates[:, :, 1], ch.gates[:, :, 0], e2[:], ALU.mult))
                dve.wait_ge(c_mm, 1)
                done(dve.tensor_copy(tot[:], banks[1][:, 0:NT * NE].rearrange("p (t e) -> p t e", t=NT)))
                done(dve.memset(before_t[:, 0, :], 0.0))
                for t in range(1, NT):
                    done(dve.tensor_tensor(before_t[:, t, :], before_t[:, t - 1, :], tot[:, t - 1, :], ALU.add))
                done(dve.tensor_tensor(cnt[:], before_t[:, NT - 1, :], tot[:, NT - 1, :], ALU.add))
                done(dve.tensor_tensor(slotv[:], banks[0][:, 0:NT * NE].rearrange("p (t e) -> p t e", t=NT), before_t[:], ALU.add))
                done(dve.tensor_scalar(thr[:], iota[:, 1:MAXBLK], float(P), None, ALU.mult))
                done(dve.tensor_tensor(cmp[:, :, 0:MAXBLK - 1], across(cnt[:], MAXBLK - 1), thr[:, None, :].broadcast_to([P, NE, MAXBLK - 1]), ALU.is_gt))
                done(dve.tensor_reduce(nov[:], cmp[:, :, 0:MAXBLK - 1], AX, ALU.add))
                done(dve.tensor_copy(scan[:, 0, :], nov[:]))
                a, sh = 0, 1
                while sh < NE:
                    done(dve.tensor_copy(scan[:, 1 - a, 0:sh], scan[:, a, 0:sh]))
                    done(dve.tensor_tensor(scan[:, 1 - a, sh:NE], scan[:, a, sh:NE], scan[:, a, 0:NE - sh], ALU.add))
                    a, sh = 1 - a, sh * 2
                end = scan[:, a, :]
                done(dve.tensor_tensor(delta[:], end, nov[:], ALU.subtract))
                done(dve.tensor_tensor(delta[:], delta[:], iota[:, 0:NE], ALU.subtract))
                done(dve.tensor_scalar(delta[:], delta[:], float(NE - 1), float(P), ALU.add, ALU.mult))
                done(dve.tensor_scalar(over[:], slotv[:], float(P), None, ALU.is_ge))
                done(dve.tensor_tensor(over[:], over[:], delta[:, None, :].broadcast_to([P, NT, NE]), ALU.mult))
                done(dve.tensor_tensor(slotv[:], slotv[:], over[:], ALU.add))
                done(dve.tensor_scalar(delta[:], iota[:, 0:NE], float(P), None, ALU.mult))
                done(dve.tensor_tensor(slotv[:], slotv[:], delta[:, None, :].broadcast_to([P, NT, NE]), ALU.add))
                for k in range(2):
                    done(dve.tensor_tensor(slotp[:, :, k, :], hot[:, :, k, :], slotv[:], ALU.mult))
                done(dve.tensor_reduce(slotf[:], slotp[:], AX, ALU.add))
                done(dve.tensor_copy(ch.slots[:], slotf[:]))
                assert count[0] == ch.route_steps["slots"]
                done(dve.tensor_copy(tabf[:, 0:1], scan[:, a, NE - 1:NE]))
                done(dve.tensor_tensor(cmp[:].rearrange("p e j -> p (e j)").rearrange("p (j e) -> p j e", e=NE),
                                       scan[:, a:a + 1, :].broadcast_to([P, MAXOVER, NE]), across(iota[:, 0:MAXOVER], NE), ALU.is_le))
                done(dve.tensor_reduce(tabf[:, 1:], cmp[:].rearrange("p e j -> p (e j)").rearrange("p (j e) -> p j e", e=NE), AX, ALU.add))
                done(dve.tensor_scalar(tabf[:, 1:], tabf[:, 1:], float(NE - 1), None, ALU.min))
                done(dve.tensor_copy(ch.beyond[:], tabf[0:1, :]))

            @block.tensor
            def _(pe):
                pe.wait_ge(tab_in, 16 * 5)
                pe.wait_ge(step, ch.route_steps["hot"])
                flat = both[:].rearrange("p t e -> p (t e)")
                pe.matmul(banks[0][:, 0:NT * NE], before[:], flat, start=True, stop=True)
                pe.matmul(banks[1][:, 0:NT * NE], ones[:], flat, start=True, stop=True).then_inc(c_mm, 1)

            @block.gpsimd
            def _(pool):
                pool.wait_ge(tab_in, 16 * 5)
                pool.wait_ge(zeroed, 16)
                pool.wait_ge(step, ch.route_steps["slots"])
                for t in range(NT):
                    m = rows_of(t)
                    for k in range(2):
                        pool.indirect_dma_start(out=ch.toktab, out_offset=bass.IndirectOffsetOnAxis(ap=ch.slots[0:m, t, k:k + 1], axis=0),
                                                in_=tokens[0:m, t:t + 1], in_offset=None).then_inc(scat, 16)
                pool.wait_ge(scat, 16 * 2 * NT)


def stage_experts(nc, ch):
    sem = ch.sem
    NQ = 4
    w_in = {kind: [sem(f"e_w{kind}{q}") for q in range(NQ)] for kind in "gud"}
    w_hi, w_lo, used = ({kind: sem(f"e_{n}{kind}") for kind in "gud"} for n in ("hi", "lo", "use"))
    idx_in, rows_in, x_turned, x_hi, x_lo = sem("e_idx"), sem("e_rows"), sem("e_xt"), sem("e_xhi"), sem("e_xlo")
    sig, mul, h_done, h_turned, h_hi, h_lo, y_a, y_b, y_st, go = (
        sem("e_sig"), sem("e_mul"), sem("e_h"), sem("e_ht"), sem("e_hhi"), sem("e_hlo"), sem("e_ya"), sem("e_yb"), sem("e_yst"), sem("e_go"))
    with ExitStack() as st:
        sb = ch.sbuf(st)
        raw = {k: sb(f"e_raw{k}", [P, NQ, 1024]) for k in "gud"}
        H = {k: sb(f"e_H{k}", [P, NQ, 1024], F32R) for k in "gud"}
        L = {k: sb(f"e_L{k}", [P, NQ, 1024], F32R) for k in "gud"}
        idx = sb("e_idxs", [P, 1], I32)
        rows = sb("e_rowss", [P, D])
        xH, xL = sb("e_xH", [P, KT, P], F32R), sb("e_xL", [P, KT, P], F32R)
        hH, hL = sb("e_hH", [P, FT, P], F32R), sb("e_hL", [P, FT, P], F32R)
        sg, h = sb("e_sg", [P, FF]), sb("e_hs", [P, FF])
        y = sb("e_y", [P, D])
        banks = ch.banks
        XT, G, U, HT, Y = banks[0:2], banks[2], banks[3], banks[4], banks[5:7]

        def src(kind, e, q):
            if kind == "d":
                return ch.w_down[ds(e, 1)].rearrange("o (k p) n -> p (o k) n", p=P)[:, q, :]
            w = {"g": ch.w_gate, "u": ch.w_up}[kind]
            return w[ds(e, 1)].rearrange("o (k p) n -> p (o k) n", p=P)[:, 2 * q:2 * q + 2, :]

        def walk(eng, body):
            body(0, True, 2)
            with eng.Fori(1, NE - 2) as e:
                body(e, False, 2)
            body(NE - 2, False, 1)
            body(NE - 1, False, 0)

        with nc.Block() as block:
            @block.sync
            def _(sp):
                def load(kind, e, first=False):
                    for q in range(NQ):
                        if not first:
                            sp.wait_ge(w_lo[kind], (e - 1) * NQ + q + 1)
                        dst = raw[kind][:, q]
                        if kind != "d":
                            dst = dst.rearrange("p (k n) -> p k n", k=2)
                        sp.dma_start(dst, src(kind, e, q)).then_inc(w_in[kind][q], 16)

                def body(e, first, left):
                    if not first:
                        load("d", e)
                    if left >= 2:
                        load("g", e + 2)
                        load("u", e + 2)

                for kind in "gud":
                    load(kind, 0, True)
                for kind in "gu":
                    load(kind, 1)
                walk(sp, body)

            @block.gpsimd
            def _(pool):
                def gather(e):
                    pool.wait_ge(x_turned, e * 2)
                    apart(pool, ch)
                    pool.dma_start(idx[:], ch.toktab[ds(e * P, P), :]).then_inc(idx_in, 16)
                    pool.wait_ge(idx_in, e * 16 + 16)
                    apart(pool, ch)
                    pool.indirect_dma_start(out=rows[:], out_offset=None, in_=ch.xn2_d,
                                            in_offset=bass.IndirectOffsetOnAxis(ap=idx[:, 0:1], axis=0)).then_inc(rows_in, 16)

                def body(e, first, left):
                    if left >= 1:
                        gather(e + 1)

                pool.memset(idx[:], 0).then_inc(go, 1)
                pool.wait_ge(go, 1)
                gather(0)
                walk(pool, body)
                pool.wait_ge(y_st, 16 * NE)

            @block.scalar
            def _(act):
                def split_hi(kind, e):
                    for q in range(NQ):
                        act.wait_ge(w_in[kind][q], e * 16 + 16)
                        act.wait_ge(used[kind], e * NQ + q + 1)
                        act.activation(H[kind][:, q], raw[kind][:, q], ACT.Copy).then_inc(w_hi[kind], 1)

                def rows_hi(e):
                    for b in range(2):
                        act.wait_ge(x_turned, e * 2 + b + 1)
                        act.activation(xH[:, 4 * b:4 * b + 4].rearrange("p k i -> p (k i)"), XT[b][:], ACT.Copy).then_inc(x_hi, 1)

                def hidden_hi(e):
                    act.wait_ge(h_turned, e + 1)
                    act.activation(hH[:].rearrange("p k i -> p (k i)"), HT[:], ACT.Copy).then_inc(h_hi, 1)

                def gate_sigmoid(e):
                    act.wait_ge(used["g"], e * NQ + 2 * NQ)
                    act.wait_ge(h_done, e)
                    act.activation(sg[:], G[:], ACT.Sigmoid).then_inc(sig, 1)

                def out_evac(e):
                    act.wait_ge(used["d"], e * NQ + 2 * NQ)
                    act.wait_ge(y_st, e * 16)
                    act.activation(y[:, 0:512], Y[0][:], ACT.Copy).then_inc(y_a, 1)
                    act.wait_ge(y_a, e + 1)
                    act.wait_ge(y_b, e + 1)
                    apart(act, ch)
                    act.dma_start(ch.y_d[ds(e * P, P), :], y[:]).then_inc(y_st, 16)

                def body(e, first, left):
                    if not first:
                        split_hi("d", e - 1)
                        hidden_hi(e - 1)
                    if left >= 1:
                        split_hi("g", e + 1)
                        rows_hi(e + 1)
                    gate_sigmoid(e)
                    if left >= 1:
                        split_hi("u", e + 1)
                    if not first:
                        out_evac(e - 1)

                split_hi("g", 0)
                rows_hi(0)
                split_hi("u", 0)
                walk(act, body)
                split_hi("d", NE - 1)
                hidden_hi(NE - 1)
                out_evac(NE - 1)

            @block.vector
            def _(dve):
                def split_lo(kind, e):
                    for q in range(NQ):
                        dve.wait_ge(w_hi[kind], e * NQ + q + 1)
                        dve.tensor_tensor(L[kind][:, q], raw[kind][:, q], H[kind][:, q].bitcast(F32), ALU.subtract).then_inc(w_lo[kind], 1)

                def rows_lo(e):
                    for b in range(2):
                        dve.wait_ge(x_hi, e * 2 + b + 1)
                        cols = slice(4 * b, 4 * b + 4)
                        dve.tensor_tensor(xL[:, cols].rearrange("p k i -> p (k i)"), XT[b][:], xH[:, cols].rearrange("p k i -> p (k i)").bitcast(F32),
                                          ALU.subtract).then_inc(x_lo, 1)

                def hidden_lo(e):
                    dve.wait_ge(h_hi, e + 1)
                    dve.tensor_tensor(hL[:].rearrange("p k i -> p (k i)"), HT[:], hH[:].rearrange("p k i -> p (k i)").bitcast(F32),
                                      ALU.subtract).then_inc(h_lo, 1)

                def hidden(e):
                    dve.wait_ge(sig, e + 1)
                    dve.wait_ge(h_turned, e)
                    dve.tensor_tensor(h[:], G[:], sg[:], ALU.mult).then_inc(mul, 1)
                    dve.wait_ge(mul, e + 1)
                    dve.wait_ge(used["u"], e * NQ + 2 * NQ)
                    dve.tensor_tensor(h[:], U[:], h[:], ALU.mult).then_inc(h_done, 1)

                def out_evac(e):
                    dve.wait_ge(used["d"], e * NQ + 2 * NQ)
                    dve.wait_ge(y_st, e * 16)
                    dve.tensor_copy(y[:, 512:1024], Y[1][:]).then_inc(y_b, 1)

                def body(e, first, left):
                    if not first:
                        split_lo("d", e - 1)
                        hidden_lo(e - 1)
                    if left >= 1:
                        split_lo("g", e + 1)
                        rows_lo(e + 1)
                    hidden(e)
                    if left >= 1:
                        split_lo("u", e + 1)
                    if not first:
                        out_evac(e - 1)

                split_lo("g", 0)
                rows_lo(0)
                split_lo("u", 0)
                walk(dve, body)
                split_lo("d", NE - 1)
                hidden_lo(NE - 1)
                out_evac(NE - 1)

            @block.tensor
            def _(pe):
                def product(kind, out, e):
                    for q in range(NQ):
                        pe.wait_ge(w_lo[kind], e * NQ + q + 1)
                        for k2 in range(2):
                            k, cols = 2 * q + k2, slice(k2 * 512, (k2 + 1) * 512)
                            mm = split_matmuls(pe, out[:], (xH[:, k, :], xL[:, k, :]), (H[kind][:, q, cols], L[kind][:, q, cols]), k == 0, k == KT - 1)
                        mm.then_inc(used[kind], 1)

                def down(e):
                    pe.wait_ge(h_lo, e + 1)
                    pe.wait_ge(y_a, e)
                    pe.wait_ge(y_b, e)
                    for q in range(NQ):
                        pe.wait_ge(w_lo["d"], e * NQ + q + 1)
                        for f in range(2):
                            cols = slice(f * 512, (f + 1) * 512)
                            mm = split_matmuls(pe, Y[f][:], (hH[:, q, :], hL[:, q, :]), (H["d"][:, q, cols], L["d"][:, q, cols]), q == 0, q == NQ - 1)
                        mm.then_inc(used["d"], 1)

                def turn_rows(e):
                    pe.wait_ge(rows_in, e * 16 + 16)
                    pe.wait_ge(x_lo, e * 2)
                    for b in range(2):
                        for k in range(4):
                            tr = pe.transpose(XT[b][:, k * P:(k + 1) * P], rows[:, (4 * b + k) * P:(4 * b + k + 1) * P], ch.ident[:])
                        tr.then_inc(x_turned, 1)

                def turn_hidden(e):
                    pe.wait_ge(h_done, e + 1)
                    pe.wait_ge(h_lo, e)
                    for k in range(FT):
                        tr = pe.transpose(HT[:, k * P:(k + 1) * P], h[:, k * P:(k + 1) * P], ch.ident[:])
                    tr.then_inc(h_turned, 1)

                def body(e, first, left):
                    pe.wait_ge(x_lo, e * 2 + 2)
                    pe.wait_ge(h_done, e)
                    product("g", G, e)
                    if not first:
                        turn_hidden(e - 1)
                    product("u", U, e)
                    if left >= 1:
                        turn_rows(e + 1)
                    if not first:
                        down(e - 1)

                for kind in "gud":
                    pe.sem_inc(used[kind], NQ)
                turn_rows(0)
                walk(pe, body)
                turn_hidden(NE - 1)
                down(NE - 1)


def stage_beyond(nc, ch):
    sem = ch.sem
    w_in, idx_in, rows_in, x_turned, x_out, g_mm, u_mm, sig, mul, h_done, h_turned, h_out, d_mm, y_out, y_st, go = (
        sem("v_" + n) for n in ("w", "idx", "rows", "xt", "xo", "g", "u", "sig", "mul", "h", "ht", "ho", "d", "y", "yst", "go"))
    with ExitStack() as st:
        sb = ch.sbuf(st)
        wg, wu = sb("v_wg", [P, KT, FF]), sb("v_wu", [P, KT, FF])
        wd = sb("v_wd", [P, FT, D])
        idx = sb("v_idx_s", [P, 1], I32)
        rows, xT = sb("v_rows_s", [P, D]), sb("v_xT", [P, KT, P])
        sg, h, hT = sb("v_sg", [P, FF]), sb("v_h_s", [P, FF]), sb("v_hT", [P, FT, P])
        y = sb("v_y_s", [P, D])
        banks = ch.banks

        def each(eng, body):
            n = eng.value_load(ch.beyond[0:1, 0:1], min_val=0, max_val=MAXOVER)
            with eng.If(n > 0):
                with eng.Fori(0, n) as j:
                    body(j)

        with nc.Block() as block:
            @block.sync
            def _(sp):
                def body(j):
                    sp.wait_ge(d_mm, j)
                    e = sp.value_load(ch.beyond[0:1, ds(j + 1, 1)], min_val=0, max_val=NE - 1)
                    for dst, w in ((wg, ch.w_gate), (wu, ch.w_up), (wd, ch.w_down)):
                        sp.dma_start(dst[:], w[ds(e, 1)].rearrange("o (k p) n -> p (o k) n", p=P)).then_inc(w_in, 16)
                each(sp, body)

            @block.gpsimd
            def _(pool):
                def body(j):
                    pool.wait_ge(y_st, j * 16)
                    apart(pool, ch)
                    pool.dma_start(idx[:], ch.toktab[ds(j * P + NE * P, P), :]).then_inc(idx_in, 16)
                    pool.wait_ge(idx_in, j * 16 + 16)
                    apart(pool, ch)
                    pool.indirect_dma_start(out=rows[:], out_offset=None, in_=ch.xn2_d,
                                            in_offset=bass.IndirectOffsetOnAxis(ap=idx[:, 0:1], axis=0)).then_inc(rows_in, 16)
                    pool.wait_ge(y_out, j + 1)
                    apart(pool, ch)
                    pool.dma_start(ch.y_d[ds(j * P + NE * P, P), :], y[:]).then_inc(y_st, 16)
                    pool.wait_ge(y_st, j * 16 + 16)
                pool.memset(idx[:], 0).then_inc(go, 1)
                pool.wait_ge(go, 1)
                each(pool, body)

            @block.scalar
            def _(act):
                def body(j):
                    act.wait_ge(x_turned, j + 1)
                    for b in range(2):
                        ins = act.activation(xT[:, 4 * b:4 * b + 4].rearrange("p k i -> p (k i)"), banks[b][:], ACT.Copy)
                    ins.then_inc(x_out, 1)
                    act.wait_ge(u_mm, j + 1)
                    act.activation(sg[:], banks[2][:], ACT.Sigmoid).then_inc(sig, 1)
                    act.wait_ge(h_turned, j + 1)
                    act.activation(hT[:].rearrange("p k i -> p (k i)"), banks[4][:], ACT.Copy).then_inc(h_out, 1)
                    act.wait_ge(d_mm, j + 1)
                    act.wait_ge(y_st, j * 16)
                    for f in range(2):
                        ins = act.activation(y[:, f * 512:(f + 1) * 512], banks[5 + f][:], ACT.Copy)
                    ins.then_inc(y_out, 1)
                each(act, body)

            @block.vector
            def _(dve):
                def body(j):
                    dve.wait_ge(sig, j + 1)
                    dve.tensor_tensor(h[:], banks[2][:], sg[:], ALU.mult).then_inc(mul, 1)
                    dve.wait_ge(mul, j + 1)
                    dve.tensor_tensor(h[:], banks[3][:], h[:], ALU.mult).then_inc(h_done, 1)
                each(dve, body)

            @block.tensor
            def _(pe):
                def body(j):
                    pe.wait_ge(rows_in, j * 16 + 16)
                    for k in range(KT):
                        tr = pe.transpose(banks[k // 4][:, (k % 4) * P:(k % 4 + 1) * P], rows[:, k * P:(k + 1) * P], ch.ident[:])
                    tr.then_inc(x_turned, 1)
                    pe.wait_ge(x_out, j + 1)
                    pe.wait_ge(w_in, j * 48 + 48)
                    for bank, w, done in ((banks[2], wg, g_mm), (banks[3], wu, u_mm)):
                        for k in range(KT):
                            mm = pe.matmul(bank[:], xT[:, k, :], w[:, k, :], start=(k == 0), stop=(k == KT - 1))
                        mm.then_inc(done, 1)
                    pe.wait_ge(h_done, j + 1)
                    for k in range(FT):
                        tr = pe.transpose(banks[4][:, k * P:(k + 1) * P], h[:, k * P:(k + 1) * P], ch.ident[:])
                    tr.then_inc(h_turned, 1)
                    pe.wait_ge(h_out, j + 1)
                    pe.wait_ge(y_out, j)
                    for f in range(2):
                        for k in range(FT):
                            mm = pe.matmul(banks[5 + f][:], hT[:, k, :], wd[:, k, f * 512:(f + 1) * 512], start=(k == 0), stop=(k == FT - 1))
                    mm.then_inc(d_mm, 1)
                each(pe, body)


def stage_combine(nc, ch):
    sem = ch.sem
    AHEAD = 4
    g_in, y_in, x_in, m_done, a_done, sq_done, ms_done, root_done, rstd_done, o_done, o_st = (
        sem("c_gain"), [sem(f"c_y{s}") for s in range(AHEAD)], [sem(f"c_x{s}") for s in range(AHEAD)], sem("c_m"), sem("c_a"), sem("c_sq"), sem("c_ms"), sem("c_root"),
        sem("c_rstd"), sem("c_o"), [sem("c_st0"), sem("c_st1")])
    with ExitStack() as st:
        sb = ch.sbuf(st)
        Y, x2, o = sb("c_Y", [P, AHEAD, 2, D]), sb("c_x2s", [P, AHEAD, D]), sb("c_os", [P, 2, D])
        junk, gain, stat = sb("c_junk", [P, D]), sb("c_gains", [P, D]), sb("c_stat", [P, 2, 4])
        with nc.Block() as block:
            @block.sync
            def _(sp):
                sp.dma_start(gain[:], ch.norm_final.broadcast_to([P, D])).then_inc(g_in, 16)
                for t in range(NT):
                    m, s = rows_of(t), t % AHEAD
                    if t >= AHEAD:
                        sp.wait_ge(m_done, t - AHEAD + 1)
                    sp.dma_start(x2[0:m, s], ch.x2_d[t * P:t * P + m, :]).then_inc(x_in[s], 16)

            @block.gpsimd
            def _(pool):
                for t in range(NT):
                    m, s = rows_of(t), t % AHEAD
                    if t >= AHEAD:
                        pool.wait_ge(o_done, t - AHEAD + 1)
                    for k in range(2):
                        pool.indirect_dma_start(out=Y[0:m, s, k, :], out_offset=None, in_=ch.y_d,
                                                in_offset=bass.IndirectOffsetOnAxis(ap=ch.slots[0:m, t, k:k + 1], axis=0)).then_inc(y_in[s], 16)

            @block.scalar
            def _(act):
                def store(t):
                    m, s = rows_of(t), t % 2
                    act.wait_ge(o_done, t + 1)
                    dst = ch.y_sample if t == NB else ch.y_prompt[t * P:(t + 1) * P, :]
                    act.dma_start(dst, o[0:m, s]).then_inc(o_st[s], 16)

                for t in range(NT):
                    m, s = rows_of(t), t % 2
                    act.wait_ge(a_done, t + 1)
                    act.activation(junk[0:m], Y[0:m, t % AHEAD, 0], ACT.Square, accum_out=stat[0:m, s, 0:1]).then_inc(sq_done, 1)
                    act.wait_ge(ms_done, t + 1)
                    act.activation(stat[0:m, s, 2:3], stat[0:m, s, 1:2], ACT.Sqrt).then_inc(root_done, 1)
                    store(t)
                for s in range(2):
                    act.wait_ge(o_st[s], 16 * ((NT + 1 - s) // 2))

            @block.vector
            def _(dve):
                dve.wait_ge(g_in, 16)
                for t in range(NT):
                    m, s = rows_of(t), t % 2
                    a = t % AHEAD
                    dve.wait_ge(y_in[a], 32 * (t // AHEAD + 1))
                    dve.wait_ge(x_in[a], 16 * (t // AHEAD + 1))
                    y0, y1 = Y[0:m, a, 0], Y[0:m, a, 1]
                    dve.scalar_tensor_tensor(out=y0, in0=y0, scalar=ch.gates[0:m, t, 0:1], in1=x2[0:m, a], op0=ALU.mult, op1=ALU.add).then_inc(m_done, 1)
                    dve.wait_ge(m_done, t + 1)
                    dve.scalar_tensor_tensor(out=y0, in0=y1, scalar=ch.gates[0:m, t, 1:2], in1=y0, op0=ALU.mult, op1=ALU.add).then_inc(a_done, 1)
                    dve.wait_ge(sq_done, t + 1)
                    dve.tensor_scalar(stat[0:m, s, 1:2], stat[0:m, s, 0:1], 1.0 / D, EPS, ALU.mult, ALU.add).then_inc(ms_done, 1)
                    dve.wait_ge(root_done, t + 1)
                    dve.reciprocal(stat[0:m, s, 3:4], stat[0:m, s, 2:3]).then_inc(rstd_done, 1)
                    dve.wait_ge(rstd_done, t + 1)
                    if t >= 2:
                        dve.wait_ge(o_st[s], 16 * (t // 2))
                    dve.scalar_tensor_tensor(out=o[0:m, s], in0=y0, scalar=stat[0:m, s, 3:4], in1=gain[0:m],
                                             op0=ALU.mult, op1=ALU.mult).then_inc(o_done, 1)


CONSTS = ("ident", "skew_hot", "skew_mask", "samp_hot", "samp_mask", "sink_hot", "cos", "sin", "decay", "samp_decay", "q_decay", "k_decay",
          "samp_q_decay", "samp_k_decay", "c_decay", "samp_c_decay", "ones", "before", "iota", "tokens", "no_expert", "zero_slots")
INPUTS = ("x_prompt", "x_sample", "cache_k", "cache_v", "state_ret", "norm_mix", "w_in", "attn_sink", "rel_bias", "w_branch_attn",
          "w_branch_ret", "w_out", "norm_ffn", "w_router_group", "b_router_group", "w_router_expert", "b_router_expert", "w_gate",
          "w_up", "w_down", "norm_final")
OUTPUTS = (("y_prompt", (1, SEQ, D)), ("y_sample", (DB, DL, D)), ("new_k_prompt", (1, 1, WINDOW, KVH, HD)), ("new_v_prompt", (1, 1, WINDOW, KVH, HD)),
           ("new_state_prompt", (1, 1, RH, DK, DV)), ("new_k_sample", (1, DB, WINDOW, KVH, HD)), ("new_v_sample", (1, DB, WINDOW, KVH, HD)),
           ("new_state_sample", (1, DB, RH, DK, DV)))


def hybrid_decoder_layer(nc, ins, outs, consts, stages=99):
    ch = Chip()
    ch.c = consts
    ch.route_steps = {"group": 3 + 2 * NT, "pair": 3 + 2 * NT + 4 + 2 * NT + 1}
    ch.route_steps["hot"] = ch.route_steps["pair"] + 5
    ch.route_steps["slots"] = ch.route_steps["hot"] + 6 + 2 + (NT - 1) + 2 + 4 + 2 * 5 + 8 + 4
    k_tiles = lambda w: w.rearrange("o (k p) n -> p (o k) n", p=P)
    ch.x_prompt = ins["x_prompt"].rearrange("b t d -> (b t) d")
    ch.x_sample = ins["x_sample"].rearrange("b t d -> (b t) d")
    ch.cache_k, ch.cache_v = (ins[n].rearrange("o b w h d -> (o b) w (h d)") for n in ("cache_k", "cache_v"))
    ch.state_ret = ins["state_ret"].rearrange("o b h d e -> (o b) h d e")
    ch.norm_mix, ch.norm_ffn = ins["norm_mix"], ins["norm_ffn"]
    ch.norm_final = ins["norm_final"].rearrange("(o d) -> o d", o=1)
    ch.w_in, ch.w_attn, ch.w_ret, ch.w_out = (k_tiles(ins[n]) for n in ("w_in", "w_branch_attn", "w_branch_ret", "w_out"))
    ch.w_rg, ch.w_re = k_tiles(ins["w_router_group"]), k_tiles(ins["w_router_expert"])
    ch.b_rg, ch.b_re = ins["b_router_group"], ins["b_router_expert"]
    ch.attn_sink, ch.attn_sink_row = ins["attn_sink"].rearrange("o h -> h o"), ins["attn_sink"]
    ch.rel_bias = ins["rel_bias"]
    ch.w_gate, ch.w_up, ch.w_down = (ins[n].rearrange("o e a b -> (o e) a b") for n in ("w_gate", "w_up", "w_down"))
    ch.y_prompt = outs["y_prompt"].rearrange("b t d -> (b t) d")
    ch.y_sample = outs["y_sample"].rearrange("b t d -> (b t) d")
    ch.new_k_prompt, ch.new_v_prompt = (outs[n].rearrange("o b w h d -> (o b w) (h d)") for n in ("new_k_prompt", "new_v_prompt"))
    ch.new_k_sample, ch.new_v_sample = (outs[n].rearrange("o b w h d -> (o b) w (h d)") for n in ("new_k_sample", "new_v_sample"))
    ch.new_state_prompt = outs["new_state_prompt"].rearrange("o b h d e -> (o b h) d e")
    ch.new_state_sample = outs["new_state_sample"].rearrange("o b h d e -> (o b) h d e")

    skew = nc.dram_tensor("skew", [HEADS, P * SKEW], F32).ap()
    ch.skew = skew
    ch.skew_read = bass.AP(skew.tensor, P - 1, [[SKEW - 1, P], [P * SKEW, HEADS], [1, 2 * P]])
    ch.gate_t = nc.dram_tensor("gate_t", [P, KT, T], F32).ap()
    ch.m1_t = nc.dram_tensor("m1_t", [P, KT, T], F32).ap()
    ch.x2_d = nc.dram_tensor("x2_d", [T, D], F32).ap()
    ch.xn2_d = nc.dram_tensor("xn2_d", [T, D], F32).ap()
    ch.toktab = nc.dram_tensor("toktab", [SLOTS, 1], I32).ap()
    ch.y_d = nc.dram_tensor("y_d", [SLOTS, D], F32).ap()

    with ExitStack() as top:
        ch.sem = lambda name: nc.alloc_semaphore(name=name)
        ch.sbuf = lambda st: (lambda name, shape, dt=F32: st.enter_context(nc.sbuf_tensor(name, shape, dt)))
        sb = ch.sbuf(top)
        ch.passed = ch.sem("passed")
        mixer_sems = []

        def mixer_sem(name):
            mixer_sems.append(nc.alloc_semaphore(name=name))
            return mixer_sems[-1]

        ch.sem = mixer_sem
        ch.banks = [top.enter_context(nc.psum_tensor(f"bank{i}", [P, 512], F32)) for i in range(8)]
        ch.ident = sb("identity", [P, P])
        ch.logits = sb("logits", [P, NT, NG + NE])
        ch.slots, ch.gates = sb("slots", [P, NT, 2], I32), sb("gates", [P, NT, 2])
        ch.beyond = sb("beyond", [1, 1 + MAXOVER], I32)
        with ExitStack() as xs:
            sb = ch.sbuf(xs)
            ch.xH, ch.xL = sb("xH", [P, KT, T], F32R), sb("xL", [P, KT, T], F32R)
            ch.raw = sb("raw", [P, 3, KT, P])
            ch.w_sems = {stage: [ch.sem(f"w_{stage}{slot}") for slot in range(3 if stage == "branch" else 2)]
                         for stage in ("kv", "attention", "branch", "retention", "merge", "out")}
            with ExitStack() as ab:
                ch.attn = ch.sbuf(ab)("attn", [P, KT, T])
                with ExitStack() as at:
                    sb = ch.sbuf(at)
                    ch.sampbias, ch.negsink_rows = sb("sampbias", [P, KVH, P + NS]), sb("negsink_rows", [P, KVH])
                    stage_norm(nc, ch)
                    if stages < 2:
                        return ch
                    ch.K, ch.V = sb("K", [P, NT, KVH * HD]), sb("V", [P, NT, KVH * HD])
                    stage_kv(nc, ch)
                    if stages < 3:
                        return ch
                    stage_attention(nc, ch)
                    if stages < 4:
                        return ch
            stage_branch_attn(nc, ch)
            if stages < 5:
                return ch
            with ExitStack() as rs:
                ret = ch.sbuf(rs)("ret", [P, KT, T])
                stage_retention(nc, ch, ret)
                if stages < 6:
                    return ch
            stage_merge(nc, ch, ret)
            if stages < 7:
                return ch
            stage_out(nc, ch)
        if stages < 8:
            return ch
        nc.clear_and_free_semaphores(mixer_sems)
        nc.all_engine_barrier()
        ch.sem = lambda name: nc.alloc_semaphore(name=name)
        stage_route(nc, ch)
        if stages < 9:
            return ch
        stage_experts(nc, ch)
        stage_beyond(nc, ch)
        stage_combine(nc, ch)
    return ch


def kernel(**inputs):
    import concourse.bacc as bacc
    from concourse.bass_utils import run_bass_kernel_spmd

    nc = bacc.Bacc("TRN2", target_bir_lowering=False, num_devices=1)
    arrays, ins, outs, consts = {}, {}, {}, {}
    for name in INPUTS:
        a = np.ascontiguousarray(inputs[name])
        arrays[f"in_{name}"] = a
        ins[name] = nc.dram_tensor(f"in_{name}", a.shape, mybir.dt.from_np(a.dtype), kind="ExternalInput").ap()
    for name, a in constants().items():
        a = np.ascontiguousarray(a)
        arrays[f"const_{name}"] = a
        consts[name] = nc.dram_tensor(f"const_{name}", a.shape, mybir.dt.from_np(a.dtype), kind="ExternalInput").ap()
    for name, shape in OUTPUTS:
        outs[name] = nc.dram_tensor(f"out_{name}", shape, F32, kind="ExternalOutput").ap()
    hybrid_decoder_layer(nc, ins, outs, consts)
    r = run_bass_kernel_spmd(nc, [arrays], core_ids=[0])
    return tuple(r.results[0][f"out_{name}"] for name, _ in OUTPUTS)
```

```python
import math
from contextlib import ExitStack

import numpy as np

import concourse.bass as bass
from concourse import mybir

F32 = mybir.dt.float32
F32R = mybir.dt.float32r
I32 = mybir.dt.int32
U32 = mybir.dt.uint32
ACT = mybir.ActivationFunctionType
ALU = mybir.AluOpType
AX = mybir.AxisListType.X
ds = bass.ds

P = 128
D = 1024
KT = D // P
SEQ = 1024
NB = SEQ // P
DB, DL = 8, 4
NS = DB * DL
T = SEQ + NS
NT = NB + 1
TG = T // 3
HD = 64
KVH, GQA = 4, 4
HEADS = KVH * GQA
WINDOW = 128
BUCKETS = 32
SKEW = 3 * P
RH, DK, DV = 4, 128, 256
DVT = DV // P
PAST = 2048
EPS = 1e-6
NEG = -1e30
C_Q, C_K, C_V = 0, 1024, 1280
C_QR, C_KR, C_VR, C_GR, C_GA, C_GRT = 1536, 2048, 2560, 3584, 4608, 5632
NG, EPG = 4, 8
NE = NG * EPG
FF = 512
FT = FF // P
MAXBLK = T // P + 1
MAXOVER = 2 * T // P
SLOTS = (NE + MAXOVER) * P
ZW = 512


def rows_of(t):
    return P if t < NB else NS


def apart(eng, ch):
    eng.sem_inc(ch.passed, 1)


class Chip:
    pass


def constants():
    c = {}
    c["ident"] = np.eye(P, dtype=np.float32)

    def bucket(dist):
        d = np.maximum(dist, 1).astype(np.float32)
        large = 16 + (np.log(d / np.float32(16)) / np.float32(math.log(8.0)) * np.float32(16)).astype(np.int32)
        return np.where(dist < 16, dist, np.minimum(large, BUCKETS - 1))

    dist = 2 * P - 1 - np.arange(SKEW)
    ok = (dist >= 0) & (dist < WINDOW)
    c["skew_hot"] = ((bucket(np.clip(dist, 0, WINDOW - 1))[None] == np.arange(BUCKETS)[:, None]) & ok[None]).astype(np.float32)
    c["skew_mask"] = np.broadcast_to(np.where(ok, 0.0, NEG), (HEADS, SKEW)).astype(np.float32).copy()
    samp = np.zeros((BUCKETS, DL, P + NS), np.float32)
    mask = np.full((P, P + NS), NEG, np.float32)
    for i in range(DL):
        for col in range(P + NS):
            dd = i + P - col if col < P else i - (col - P) % DL
            if 0 <= dd < WINDOW:
                samp[bucket(np.array(dd)), i, col] = 1.0
                for r in range(P):
                    if r % DL == i and (col < P or (col - P) // DL == r // 16):
                        mask[r, col] = 0.0
    c["samp_hot"] = samp
    c["samp_mask"] = mask
    sink = np.zeros((HEADS, KVH, P), np.float32)
    for r in range(P):
        for k in range(KVH):
            sink[k * GQA + 2 * ((r // DL) % 2) + (r // (2 * DL)) % 2, k, r] = 1.0
    c["sink_hot"] = sink
    half = DK // 2
    inv = np.float32(10000.0) ** (-np.arange(half, dtype=np.float32) * np.float32(2.0) / np.float32(DK))
    pos = np.concatenate([np.arange(SEQ), np.tile(PAST + np.arange(DL), DB), np.zeros(P - NS)]).astype(np.float32)
    ang = (pos[:, None] * inv[None].astype(np.float32)).astype(np.float32)
    c["cos"] = np.cos(ang).astype(np.float32).reshape(NT, P, half).transpose(1, 0, 2).copy()
    c["sin"] = np.sin(ang).astype(np.float32).reshape(NT, P, half).transpose(1, 0, 2).copy()
    lg = np.log(np.float32(1.0) - np.float32(2.0) ** (np.float32(-5.0) - np.arange(RH, dtype=np.float32))).astype(np.float32)
    idx = np.arange(P, dtype=np.float32)
    diff = idx[None, :] - idx[:, None]
    dec = np.where(diff >= 0, np.exp(np.maximum(diff, 0)[None] * lg[:, None, None]), 0)
    c["decay"] = (np.float32(DK ** -0.5) * dec).transpose(1, 0, 2).astype(np.float32).copy()
    tok = np.arange(NS)
    same = tok[:, None] // DL == tok[None] // DL
    sdiff = (tok[None] % DL - tok[:, None] % DL).astype(np.float32)
    sdec = np.where(same & (sdiff >= 0), np.exp(np.maximum(sdiff, 0)[None] * lg[:, None, None]), 0)
    c["samp_decay"] = (np.float32(DK ** -0.5) * sdec).transpose(1, 0, 2).astype(np.float32).copy()
    c["q_decay"] = np.exp((idx + 1)[:, None] * lg).astype(np.float32)
    c["k_decay"] = (np.float32(DK ** -0.5) * np.exp((P - 1 - idx)[:, None] * lg)).astype(np.float32)
    c["samp_q_decay"] = np.exp((tok % DL + 1).astype(np.float32)[:, None] * lg).astype(np.float32)
    kd = np.float32(DK ** -0.5) * np.exp((DL - 1 - tok % DL).astype(np.float32)[:, None] * lg).astype(np.float32)
    c["samp_k_decay"] = ((tok[:, None, None] // DL == np.arange(DB)[None, :, None]) * kd[:, None, :]).astype(np.float32)
    c["c_decay"] = np.broadcast_to(np.exp(P * lg).astype(np.float32), (P, RH)).copy()
    c["samp_c_decay"] = np.broadcast_to(np.exp(DL * lg).astype(np.float32), (P, RH)).copy()
    c["ones"] = np.ones((P, P), np.float32)
    c["before"] = (np.arange(P)[:, None] < np.arange(P)[None]).astype(np.float32)
    c["iota"] = np.broadcast_to(np.arange(P, dtype=np.float32), (P, P)).copy()
    c["tokens"] = (np.arange(NT)[None] * P + np.arange(P)[:, None]).astype(np.int32)
    valid = np.zeros((P, NT), np.float32)
    valid[:, NB] = np.where(np.arange(P) < NS, 0.0, 1000.0)
    c["no_expert"] = valid
    c["zero_slots"] = np.zeros((SLOTS // P, P), np.int32)
    return c


def split_matmuls(pe, out, lhs, rhs, first, last):
    (lh, ll), (rh, rl) = lhs, rhs
    pe.matmul(out, lh, rh, start=first, stop=False)
    pe.matmul(out, lh, rl, start=False, stop=False)
    return pe.matmul(out, ll, rh, start=False, stop=last)


def t_layout_product(pe, banks, w, x, ready=None):
    for k in range(KT):
        if ready:
            ready(k)
        for n, (a, b) in enumerate(((0, 0), (0, 1), (1, 0))):
            for g in range(3):
                mm = pe.matmul(banks[g][:, 0:TG], w[a][:, k, :], x[b][:, k, g * TG:(g + 1) * TG],
                               start=(k == 0 and n == 0), stop=(k == KT - 1 and n == 2))
    return mm


def first_loads(sp, ch, stage):
    sources = {"kv": [ch.w_in[:, :, C_K + q * P:C_K + (q + 1) * P] for q in range(3)],
               "attention": (ch.w_in[:, :, 0:P], ch.w_in[:, :, P:2 * P]),
               "branch": (ch.w_in[:, :, C_GA:C_GA + P], ch.w_in[:, :, C_GRT:C_GRT + P], ch.w_attn[:, :, 0:P]),
               "retention": (ch.w_in[:, :, C_GR:C_GR + P], ch.w_in[:, :, C_GR + P:C_GR + 2 * P]),
               "merge": (ch.w_ret[:, :, 0:P], ch.w_ret[:, :, P:2 * P]),
               "out": [ch.w_out[:, :, q * P:(q + 1) * P] for q in range(3)]}[stage]
    for slot, src in enumerate(sources):
        sp.dma_start(ch.raw[:, slot], src).then_inc(ch.w_sems[stage][slot], 16)


class BiasTables:

    def __init__(self, ch, sb):
        self.relb = sb("n_relb", [BUCKETS, HEADS])
        self.hot = sb("n_skewhot", [BUCKETS, SKEW])
        self.mask = sb("n_skewmask", [HEADS, SKEW])
        self.shot = sb("n_samphot", [BUCKETS, DL, P + NS])
        self.smask = sb("n_sampmask", [P, P + NS])
        self.sinkhot = sb("n_sinkhot", [HEADS, KVH, P])
        self.sinkcol = sb("n_sinkcol", [HEADS, 1])
        self.skew = sb("n_skew", [HEADS, SKEW])
        self.relx = sb("n_relx", [BUCKETS, KVH, DL, P])
        self.tab_in, self.relx_zero, self.relx_done, self.bias_mm, self.bias_sum = (
            ch.sem("n_" + n) for n in ("tab", "relx0", "relx", "bmm", "bsum"))


def stage_norm(nc, ch):
    sem = ch.sem
    x_in, scale_done = [sem("n_x0"), sem("n_x1")], sem("n_scaled")
    gain_in, sq_done, ms_done, root_done, rstd_done = sem("n_gain"), sem("n_sq"), sem("n_ms"), sem("n_root"), sem("n_rstd")
    turned, hi_done, lo_done, ident_in = sem("n_turned"), sem("n_hi"), sem("n_lo"), sem("n_ident")
    tb = ch.tables
    with ExitStack() as st:
        sb = ch.sbuf(st)
        xb = sb("n_xb", [P, 2, D])
        xs = sb("n_xs", [P, 2, D])
        junk = sb("n_junk", [P, D])
        gain = sb("n_gainrow", [P, D])
        stat = sb("n_stat", [P, 2, 4])
        banks = ch.banks

        def walk(eng, front, back):
            front(0, 0, P, True)
            front(1, 1, P, True)
            back(0, 0, P)
            with eng.Fori(1, NB // 2) as i:
                for s in range(2):
                    front(i * 2 + s, s, P, False)
                    back(i * 2 + s - 1, 1 - s, P)
            front(NB, 0, NS, False)
            back(NB - 1, 1, P)
            back(NB, 0, NS)

        with nc.Block() as block:
            @block.sync
            def _(sp):
                def load(t, s, m, first):
                    if not first:
                        sp.wait_ge(scale_done, t - 1)
                        apart(sp, ch)
                    sp.dma_start(xb[0:m, s, :], ch.x_sample if m == NS else ch.x_prompt[ds(t * P, P), :]).then_inc(x_in[s], 16)

                load(0, 0, P, True)
                sp.dma_start(gain[:], ch.norm_mix.broadcast_to([P, D])).then_inc(gain_in, 16)
                sp.dma_start(ch.ident[:], ch.c["ident"]).then_inc(ident_in, 16)
                load(1, 1, P, True)
                with sp.Fori(1, NB // 2) as i:
                    for s in range(2):
                        load(i * 2 + s, s, P, False)
                load(NB, 0, NS, False)
                first_loads(sp, ch, "kv")

            @block.gpsimd
            def _(pool):
                for dst, src in ((tb.relb, ch.rel_bias), (tb.hot, ch.c["skew_hot"]), (tb.mask, ch.c["skew_mask"]), (tb.shot, ch.c["samp_hot"]),
                                 (tb.smask, ch.c["samp_mask"]), (tb.sinkhot, ch.c["sink_hot"]), (tb.sinkcol, ch.attn_sink)):
                    pool.dma_start(dst[:], src).then_inc(tb.tab_in, 16)
                pool.memset(tb.relx[:], 0.0).then_inc(tb.relx_zero, 1)
                pool.wait_ge(tb.relx_zero, 1)
                pool.wait_ge(tb.tab_in, 16 * 7)
                for c in range(KVH):
                    for i in range(DL):
                        for par in range(2):
                            dst = tb.relx[:, c, i, :].rearrange("w (b r f j) -> w b r f j", r=2, f=2, j=DL)[:, :, par, :, i]
                            src = tb.relb[:, c * GQA:(c + 1) * GQA].rearrange("w (f r) -> w r f", r=2)[:, par:par + 1, :]
                            pool.tensor_copy(dst, src.broadcast_to([BUCKETS, DB, 2])).then_inc(tb.relx_done, 1)

            @block.scalar
            def _(act):
                def front(t, s, m, first):
                    act.wait_ge(x_in[s], t * 8 + (16 if s == 0 else 8))
                    act.activation(junk[0:m, :], xb[0:m, s, :], ACT.Square, accum_out=stat[0:m, s, 0:1]).then_inc(sq_done, 1)
                    act.wait_ge(ms_done, t + 1)
                    act.activation(stat[0:m, s, 2:3], stat[0:m, s, 1:2], ACT.Sqrt).then_inc(root_done, 1)

                def back(t, s, m):
                    for b in range(2):
                        act.wait_ge(turned, t * 2 + b + 1)
                        act.activation(ch.xH[:, 4 * b:4 * b + 4, ds(t * P, m)],
                                       banks[2 * s + b][:].rearrange("p (k m) -> p k m", m=P)[:, :, 0:m], ACT.Copy).then_inc(hi_done, 1)

                walk(act, front, back)

            @block.vector
            def _(dve):
                def front(t, s, m, first):
                    dve.wait_ge(sq_done, t + 1)
                    dve.tensor_scalar(stat[0:m, s, 1:2], stat[0:m, s, 0:1], 1.0 / D, EPS, ALU.mult, ALU.add).then_inc(ms_done, 1)
                    dve.wait_ge(root_done, t + 1)
                    dve.reciprocal(stat[0:m, s, 3:4], stat[0:m, s, 2:3]).then_inc(rstd_done, 1)
                    dve.wait_ge(rstd_done, t + 1)
                    if not first:
                        dve.wait_ge(turned, t * 2 - 2)
                    dve.scalar_tensor_tensor(out=xs[0:m, s, :], in0=xb[0:m, s, :], scalar=stat[0:m, s, 3:4], in1=gain[0:m, :],
                                             op0=ALU.mult, op1=ALU.mult).then_inc(scale_done, 1)

                def back(t, s, m):
                    for b in range(2):
                        dve.wait_ge(hi_done, t * 2 + b + 1)
                        cols = ds(t * P, m)
                        dve.tensor_tensor(ch.xL[:, 4 * b:4 * b + 4, cols],
                                          banks[2 * s + b][:].rearrange("p (k m) -> p k m", m=P)[:, :, 0:m],
                                          ch.xH[:, 4 * b:4 * b + 4, cols].bitcast(F32), ALU.subtract).then_inc(lo_done, 1)

                dve.wait_ge(gain_in, 16)
                walk(dve, front, back)

            @block.tensor
            def _(pe):
                def turn(t, s, m, first):
                    pe.wait_ge(scale_done, t + 1)
                    if not first:
                        pe.wait_ge(lo_done, t * 2 - 2)
                        if m == NS:
                            apart(pe, ch)
                    for b in range(2):
                        for k in range(4):
                            tr = pe.transpose(banks[2 * s + b][:, k * P:k * P + m], xs[0:m, s, (4 * b + k) * P:(4 * b + k + 1) * P],
                                              ch.ident[0:m, 0:m])
                        tr.then_inc(turned, 1)

                pe.wait_ge(ident_in, 16)
                walk(pe, turn, lambda t, s, m: None)


def stage_kv(nc, ch):
    sem = ch.sem
    w_in, hi_done, lo_done, kv_mm, k_out, v_out, stored, zeroed = (
        ch.w_sems["kv"] + [sem("kv_w3")], sem("kv_hi"), sem("kv_lo"), sem("kv_mm"), sem("kv_kout"), sem("kv_vout"), sem("kv_st"), sem("kv_zero"))
    tb = ch.tables
    bias_mm, bias_sum, bias_out = tb.bias_mm, tb.bias_sum, sem("n_bout")
    with ExitStack() as st:
        sb = ch.sbuf(st)
        raw3 = sb("kv_raw3", [P, KT, P])
        raw = lambda q: ch.raw[:, q] if q < 3 else raw3[:]
        wH, wL = sb("kv_wH", [P, KT, 4 * P], F32R), sb("kv_wL", [P, KT, 4 * P], F32R)
        banks = ch.banks
        with nc.Block() as block:
            @block.sync
            def _(sp):
                sp.dma_start(raw(3), ch.w_in[:, :, C_K + 3 * P:C_K + 4 * P]).then_inc(w_in[3], 16)
                sp.dma_start(ch.new_k_sample[:, 0:WINDOW - DL, :], ch.cache_k[:, DL:WINDOW, :]).then_inc(stored, 16)
                sp.dma_start(ch.new_v_sample[:, 0:WINDOW - DL, :], ch.cache_v[:, DL:WINDOW, :]).then_inc(stored, 16)
                sp.wait_ge(lo_done, 4)
                first_loads(sp, ch, "attention")
                sp.wait_ge(bias_sum, 1)
                sp.dma_start(ch.skew.rearrange("h (q u) -> h q u", u=SKEW),
                             tb.skew[:].rearrange("h (o u) -> h o u", o=1).broadcast_to([HEADS, P, SKEW])).then_inc(bias_out, 16)
                sp.wait_ge(bias_out, 16)
                sp.wait_ge(stored, 16 * 2)

            @block.gpsimd
            def _(pool):
                pool.memset(ch.K[:, NB, :], 0.0).then_inc(zeroed, 1)
                pool.memset(ch.V[:, NB, :], 0.0).then_inc(zeroed, 1)

            @block.scalar
            def _(act):
                for q in range(4):
                    act.wait_ge(w_in[q], 16)
                    act.activation(wH[:, :, q * P:(q + 1) * P], raw(q), ACT.Copy).then_inc(hi_done, 1)
                act.wait_ge(zeroed, 2)
                for t in range(NT):
                    m = rows_of(t)
                    act.wait_ge(kv_mm, t + 1)
                    act.activation(ch.K[0:m, t, :], banks[t % 2][0:m, 0:2 * P], ACT.Copy).then_inc(k_out, 1)
                    act.activation(ch.V[0:m, t, :], banks[t % 2][0:m, 2 * P:4 * P], ACT.Copy).then_inc(v_out, 1)

            @block.vector
            def _(dve):
                for q in range(4):
                    dve.wait_ge(hi_done, q + 1)
                    dve.tensor_tensor(wL[:, :, q * P:(q + 1) * P], raw(q), wH[:, :, q * P:(q + 1) * P].bitcast(F32),
                                      ALU.subtract).then_inc(lo_done, 1)
                dve.wait_ge(bias_mm, 1)
                dve.tensor_tensor(tb.skew[:], banks[4][0:HEADS, 0:SKEW], tb.mask[:], ALU.add).then_inc(bias_sum, 1)
                for c in range(KVH):
                    dve.wait_ge(bias_mm, c + 2)
                    dve.tensor_tensor(ch.sampbias[:, c, :], banks[5 + c % 2][:, 0:P + NS], tb.smask[:], ALU.add).then_inc(bias_sum, 1)
                dve.wait_ge(bias_mm, KVH + 2)
                dve.tensor_scalar(ch.negsink_rows[:], banks[7][:, 0:KVH], -1.0, None, ALU.mult).then_inc(bias_sum, 1)

            @block.tensor
            def _(pe):
                pe.wait_ge(tb.tab_in, 16 * 7)
                pe.matmul(banks[4][0:HEADS, 0:SKEW], tb.relb[:], tb.hot[:], start=True, stop=True).then_inc(bias_mm, 1)

                def sampled_bias(c):
                    if c >= 2:
                        pe.wait_ge(bias_sum, c)
                    for i in range(DL):
                        mm = pe.matmul(banks[5 + c % 2][:, 0:P + NS], tb.relx[:, c, i, :], tb.shot[:, i, :], start=(i == 0), stop=(i == DL - 1))
                    mm.then_inc(bias_mm, 1)

                pe.wait_ge(tb.relx_done, KVH * DL * 2)
                sampled_bias(0)
                sampled_bias(1)
                pe.wait_ge(lo_done, 4)
                for t in range(NT):
                    m = rows_of(t)
                    if t >= 2:
                        pe.wait_ge(k_out, t - 1)
                        pe.wait_ge(v_out, t - 1)
                    for k in range(KT):
                        cols = slice(t * P, t * P + m)
                        mm = split_matmuls(pe, banks[t % 2][0:m, :], (ch.xH[:, k, cols], ch.xL[:, k, cols]),
                                           (wH[:, k, :], wL[:, k, :]), k == 0, k == KT - 1)
                    mm.then_inc(kv_mm, 1)
                    if t + 2 < KVH:
                        sampled_bias(t + 2)
                    if t == KVH:
                        for c in range(KVH):
                            sink = pe.matmul(banks[7][:, c:c + 1], tb.sinkhot[:, c, :], tb.sinkcol[:], start=True, stop=True)
                        sink.then_inc(bias_mm, 1)


def stage_attention(nc, ch):
    sem = ch.sem
    w_in, stored = ch.w_sems["attention"], sem("a_stored")
    bias_in, ck_in, cv_in = sem("a_bias"), sem("a_ck"), sem("a_cv")
    kd_done, vd_done, kt_turned, kt_done = sem("a_kd"), sem("a_vd"), sem("a_ktt"), sem("a_kt")
    hi_done, lo_done, q_mm, q_out = sem("a_hi"), sem("a_lo"), sem("a_qmm"), sem("a_qout")
    s_mm, s_sum, m_red, nm_done, d_done = sem("a_smm"), sem("a_ssum"), sem("a_mred"), sem("a_nm"), sem("a_d")
    p_exp, sink_exp, den_done, rcp_done, p_norm = sem("a_pexp"), sem("a_sexp"), sem("a_den"), sem("a_rcp"), sem("a_pnorm")
    p_turned, pt_hi, pt_lo, o_mm, o_out = sem("a_pt"), sem("a_pth"), sem("a_ptl"), sem("a_omm"), sem("a_oout")
    z_mm, z_out, z_red, z_nm, z_d, z_exp, z_sexp, z_den, z_rcp, z_norm = (
        sem("z_mm"), sem("z_out"), sem("z_red"), sem("z_nm"), sem("z_d"), sem("z_exp"), sem("z_sexp"), sem("z_den"), sem("z_rcp"), sem("z_norm"))
    sink_in, z_par = sem("a_sink"), sem("z_par")
    zeros_done, y_zeroed = sem("a_zeros"), sem("a_yzero")
    Y_ROWS = (SLOTS - NE * P) // KVH
    S_PER = NB
    KEYS_AT = 6
    Z_PER, Z_OUT = 6, 5
    CHUNK = {1: (0, 0), 2: (0, 1), 4: (1, 0), 5: (1, 1), 6: (2, 0), 7: (2, 1)}
    ORDER = list(CHUNK)
    assert all(min((g + 1) * TG, SEQ) <= (n + 2) * P and (g < 2 or n >= 3) for n, (g, _) in CHUNK.items())
    projected = lambda c, k: 2 + len(CHUNK) * c + k
    with ExitStack() as st:
        sb = ch.sbuf(st)
        raw = ch.raw
        wH, wL = sb("a_wH", [P, 2, KT, P], F32R), sb("a_wL", [P, 2, KT, P], F32R)
        out = ch.attn
        qT = sb("a_qT", [P, 2, T])
        kT = sb("a_kT", [P, T])
        Kd, Vd = sb("a_Kd", [P, NT, 2, HD]), sb("a_Vd", [P, NT, 2, HD])
        bias = sb("a_bias_t", [P, GQA, 2 * P])
        S = sb("a_S", [P, 2, GQA, 2 * P])
        PT = sb("a_PT", [P, 2, GQA, P])
        sinkrow, negsink = sb("a_sinkrow", [P, HEADS]), sb("a_negsink", [P, HEADS])
        nm, dd, es, rs, rcp, ninv = (sb("a_" + n, [P, 2, GQA]) for n in ("nm", "dd", "es", "rs", "rcp", "den"))
        cK, cV = sb("a_cK", [P, DB, 2, HD]), sb("a_cV", [P, DB, 2, HD])
        cKT = sb("a_cKT", [P, DB, P])
        ZT = sb("a_ZT", [P, 2, P])
        Z = sb("a_Z", [P, P + NS])
        zs = sb("a_zs", [P, 6])
        zeros = sb("a_zeros_t", [P, 1, ZW])
        banks = ch.banks
        b7 = banks[7]

        def dup(ap, n):
            return ap.rearrange("p n (o d) -> p n o d", o=1).broadcast_to([P, n, 2, HD])

        def s_bank(n, g):
            return banks[2 * (n % 2) + g % 2][:, (g // 2) * 2 * P:(g // 2 + 1) * 2 * P]

        def cols_of(n):
            return slice(P, 2 * P) if n % NB == 0 else slice(0, 2 * P)

        def walk(eng, body):
            with eng.Fori(0, KVH - 1) as c:
                body(c, False)
            body(KVH - 1, True)

        with nc.Block() as block:
            @block.sync
            def _(sp):
                sp.wait_ge(zeros_done, 1)
                sp.dma_start(sinkrow[:], ch.attn_sink_row.broadcast_to([P, HEADS])).then_inc(sink_in, 16)
                sp.dma_start(ch.new_k_prompt, ch.K[:, NB - 1, :]).then_inc(stored, 16)
                sp.dma_start(ch.new_v_prompt, ch.V[:, NB - 1, :]).then_inc(stored, 16)
                for b in range(DB):
                    sp.dma_start(ch.new_k_sample[b, WINDOW - DL:WINDOW, :], ch.K[b * DL:(b + 1) * DL, NB, :]).then_inc(stored, 16)
                    sp.dma_start(ch.new_v_sample[b, WINDOW - DL:WINDOW, :], ch.V[b * DL:(b + 1) * DL, NB, :]).then_inc(stored, 16)

                def body(c, last):
                    if not last:
                        for f in range(2):
                            sp.wait_ge(lo_done, c * 2 + f + 1)
                            apart(sp, ch)
                            sp.dma_start(raw[:, f], ch.w_in[:, :, ds(c * 256 + 256 + f * P, P)]).then_inc(w_in[f], 16)
                    sp.wait_ge(s_sum, c * S_PER)
                    apart(sp, ch)
                    sp.dma_start(bias[:], ch.skew_read[:, ds(c * GQA, GQA), :]).then_inc(bias_in, 16)
                    sp.dma_start(ch.y_d[ds(c * Y_ROWS + NE * P, Y_ROWS), :].rearrange("(p r) (a b) -> p (r a) b", p=P, b=ZW),
                                 zeros[:].broadcast_to([P, Y_ROWS * D // (P * ZW), ZW])).then_inc(y_zeroed, 16)
                    sp.wait_ge(z_mm, c * Z_PER)
                    for b in range(DB):
                        for o in range(2):
                            sp.dma_start(cK[:, b, o, :], ch.cache_k[b, :, ds(c * HD, HD)]).then_inc(ck_in, 16)
                            sp.dma_start(cV[:, b, o, :], ch.cache_v[b, :, ds(c * HD, HD)]).then_inc(cv_in, 16)

                walk(sp, body)
                sp.wait_ge(lo_done, KVH * 2)
                first_loads(sp, ch, "branch")
                sp.wait_ge(y_zeroed, 16 * KVH)
                sp.wait_ge(stored, 16 * (2 + 2 * DB))

            @block.gpsimd
            def _(pool):
                pool.memset(zeros[:], 0.0).then_inc(zeros_done, 1)
                def keys(c):
                    pool.tensor_copy(Kd[:], dup(ch.K[:, :, ds(c * HD, HD)], NT)).then_inc(kd_done, 1)

                def normalize(c, n):
                    pool.wait_ge(rcp_done, c * NB + n + 1)
                    w = cols_of(n)
                    pool.tensor_tensor(S[:, n % 2, :, w], S[:, n % 2, :, w],
                                       rcp[:, n % 2, :].rearrange("p (g o) -> p g o", o=1).broadcast_to([P, GQA, w.stop - w.start]),
                                       ALU.mult).then_inc(p_norm, 1)

                def values(c):
                    pool.tensor_copy(Vd[:], dup(ch.V[:, :, ds(c * HD, HD)], NT)).then_inc(vd_done, 1)

                def body(c, last):
                    for n in range(NB):
                        if n < NB - 1 or not last:
                            normalize(c, n + 1)
                        if n == 2 and not last:
                            pool.wait_ge(kt_turned, c * 3 + 3)
                            keys(c + 1)
                    if not last:
                        pool.wait_ge(o_mm, c * NB + NB)
                        pool.wait_ge(z_mm, c * Z_PER + Z_PER)
                        values(c + 1)

                keys(0)
                values(0)
                normalize(0, 0)
                walk(pool, body)

            @block.scalar
            def _(act):
                def split_hi(c, f):
                    act.wait_ge(w_in[f], c * 16 + 16)
                    act.activation(wH[:, f], raw[:, f], ACT.Copy).then_inc(hi_done, 1)

                def queries(bank, f, g):
                    return act.activation(qT[:, f, g * TG:(g + 1) * TG], bank[:, 0:TG], ACT.Copy, scale=HD ** -0.5)

                def exps(c, n):
                    s, w = n % 2, cols_of(n)
                    act.wait_ge(nm_done, c * NB + n + 1)
                    for g in range(GQA):
                        ins = act.activation(S[:, s, g, w], S[:, s, g, w], ACT.Exp, bias=nm[:, s, g:g + 1], accum_out=rs[:, s, g:g + 1])
                    ins.then_inc(p_exp, 1)
                    act.wait_ge(d_done, c * NB + n + 1)
                    act.activation(es[:, s, :], dd[:, s, :], ACT.Exp).then_inc(sink_exp, 1)

                def body(c, last):
                    def out_evac(n):
                        act.wait_ge(o_mm, c * NB + n + 1)
                        for par in range(2):
                            r = slice(par * HD, (par + 1) * HD)
                            act.activation(out[r, ds(c * 2, 2), n * P:(n + 1) * P],
                                           banks[6][r, :].rearrange("p (r f i) -> p r f i", r=2, f=2)[:, par], ACT.Copy).then_inc(o_out, 1)

                    def sampled(step):
                        act.wait_ge(z_mm, c * Z_PER + step + 1)
                        if step in (0, 1):
                            act.activation(cKT[:, 4 * step:4 * step + 4, :], b7[:].rearrange("p (b k) -> p b k", b=4), ACT.Copy).then_inc(z_out, 1)
                        if step == 4:
                            act.activation(ZT[:, 0, :], b7[:, 0:P], ACT.Copy)
                            act.activation(ZT[0:NS, 1, :], b7[0:NS, P:2 * P], ACT.Copy).then_inc(z_out, 1)

                    def sampled_exp():
                        act.wait_ge(z_nm, c + 1)
                        act.activation(Z[:], Z[:], ACT.Exp, bias=zs[:, 0:1], accum_out=zs[:, 1:2]).then_inc(z_exp, 1)
                        act.wait_ge(z_d, c + 1)
                        act.activation(zs[:, 3:4], zs[:, 2:3], ACT.Exp).then_inc(z_sexp, 1)

                    for n in range(NB):
                        if n >= 1:
                            out_evac(n - 1)
                        if n in CHUNK and not last:
                            g, f = CHUNK[n]
                            act.wait_ge(q_mm, projected(c, ORDER.index(n)) + 1)
                            queries(b7, f, g).then_inc(q_out, 1)
                        if n < NB - 1 or not last:
                            exps(c, n + 1)
                        if n == 4:
                            sampled_exp()
                        act.wait_ge(p_turned, c * 2 * NB + 2 * n + 1)
                        act.activation(PT[:, 0], banks[4][:].rearrange("p (g i) -> p g i", g=GQA), ACT.Copy).then_inc(pt_hi, 1)
                        if n in (0, 1, 4):
                            sampled(n)
                        if n == 0 and not last:
                            act.wait_ge(q_mm, projected(c, 0))
                            for f in range(2):
                                split_hi(c + 1, f)
                    out_evac(NB - 1)

                for f in range(2):
                    split_hi(0, f)
                for f in range(2):
                    act.wait_ge(q_mm, f + 1)
                    for g in range(3):
                        ins = queries(banks[3 * f + g], f, g)
                    ins.then_inc(q_out, 1)
                exps(0, 0)
                walk(act, body)

            @block.vector
            def _(dve):
                dve.wait_ge(sink_in, 16)
                dve.tensor_scalar(negsink[:].rearrange("p (c r f) -> p c r f", r=2, f=2), sinkrow[:].rearrange("p (c f r) -> p c r f", r=2, f=2),
                                  -1.0, None, ALU.mult).then_inc(z_rcp, 1)
                dve.wait_ge(z_rcp, 1)
                def split_lo(c, f):
                    dve.wait_ge(hi_done, c * 2 + f + 1)
                    dve.tensor_tensor(wL[:, f], raw[:, f], wH[:, f].bitcast(F32), ALU.subtract).then_inc(lo_done, 1)

                def keys(c, where):
                    for q in range(3):
                        dve.wait_ge(kt_turned, c * 3 + q + 1)
                        w = 4 * P if q < 2 else NS
                        dve.tensor_copy(kT[:, q * 4 * P:q * 4 * P + w], banks[where[q]][:, 0:w]).then_inc(kt_done, 1)

                def front(c, n, head):
                    s, w = n % 2, cols_of(n)
                    m = c * NB + n + 1
                    if n % NB == 0:
                        dve.wait_ge(bias_in, head * 16 + 16)
                    dve.wait_ge(s_mm, m)
                    if n >= 2:
                        dve.wait_ge(p_turned, c * 2 * NB + 2 * (n - 1))
                    for h in range(2):
                        ins = dve.tensor_tensor(S[:, s, 2 * h:2 * h + 2, w], banks[2 * s + h][:].rearrange("p (g k) -> p g k", g=2)[:, :, w],
                                                bias[:].rearrange("p (f r) k -> p r f k", r=2)[:, h, :, w], ALU.add)
                    ins.then_inc(s_sum, 1)
                    dve.wait_ge(s_sum, m)
                    dve.tensor_reduce(nm[:, s, :], S[:, s, :, w], AX, ALU.max, negate=True).then_inc(m_red, 1)
                    dve.wait_ge(m_red, m)
                    dve.tensor_tensor(nm[:, s, :], nm[:, s, :], negsink[:, ds(head * GQA, GQA)], ALU.min).then_inc(nm_done, 1)
                    dve.wait_ge(nm_done, m)
                    dve.tensor_tensor(dd[:, s, :], nm[:, s, :], negsink[:, ds(head * GQA, GQA)], ALU.subtract).then_inc(d_done, 1)

                def back(c, n):
                    s = n % 2
                    m = c * NB + n + 1
                    dve.wait_ge(p_exp, m)
                    dve.wait_ge(sink_exp, m)
                    dve.tensor_tensor(ninv[:, s, :], rs[:, s, :], es[:, s, :], ALU.add).then_inc(den_done, 1)
                    dve.wait_ge(den_done, m)
                    dve.reciprocal(rcp[:, s, :], ninv[:, s, :]).then_inc(rcp_done, 1)

                def body(c, last):
                    def turned_copy(n):
                        dve.wait_ge(p_turned, c * 2 * NB + 2 * n + 2)
                        dve.tensor_copy(PT[:, 1], banks[5][:].rearrange("p (g i) -> p g i", g=GQA)).then_inc(pt_lo, 1)

                    def sampled(step):
                        dve.wait_ge(z_mm, c * Z_PER + step + 1)
                        if step == 2:
                            dve.tensor_copy(ZT[:, 0, :], b7[:, 0:P])
                            dve.tensor_copy(ZT[0:NS, 1, :], b7[0:NS, P:2 * P]).then_inc(z_out, 1)
                        if step == 3:
                            dve.tensor_tensor(Z[:], b7[:, 0:P + NS], ch.sampbias[:, ds(c, 1), :].rearrange("p o k -> p (o k)"), ALU.add).then_inc(z_out, 1)
                            dve.wait_ge(z_out, c * Z_OUT + 4)
                            dve.tensor_reduce(zs[:, 0:1], Z[:], AX, ALU.max, negate=True).then_inc(z_red, 1)
                            dve.wait_ge(z_red, c * 2 + 1)
                            dve.tensor_tensor(zs[:, 0:1], zs[:, 0:1], ch.negsink_rows[:, ds(c, 1)], ALU.min).then_inc(z_nm, 1)
                            dve.wait_ge(z_nm, c + 1)
                            dve.tensor_tensor(zs[:, 2:3], zs[:, 0:1], ch.negsink_rows[:, ds(c, 1)], ALU.subtract).then_inc(z_d, 1)
                        if step == 5:
                            for par in range(2):
                                r = slice(par * HD, (par + 1) * HD)
                                for b in range(2):
                                    dve.tensor_copy(out[r, ds(c * 2 + b, 1), SEQ:T].rearrange("p o (b i) -> p (o b) i", i=DL),
                                                    b7[r, 0:P].rearrange("p (b r f i) -> p r f b i", b=DB, r=2, f=2)[:, par, b]).then_inc(z_norm, 1)

                    def sampled_norm():
                        dve.wait_ge(z_exp, c + 1)
                        dve.wait_ge(z_sexp, c + 1)
                        dve.tensor_tensor(zs[:, 4:5], zs[:, 1:2], zs[:, 3:4], ALU.add).then_inc(z_den, 1)
                        dve.wait_ge(z_den, c + 1)
                        dve.reciprocal(zs[:, 5:6], zs[:, 4:5]).then_inc(z_rcp, 1)
                        dve.wait_ge(z_rcp, c + 2)
                        dve.tensor_scalar(Z[:], Z[:], zs[:, 5:6], None, ALU.mult).then_inc(z_red, 1)

                    for n in range(NB):
                        more = n < NB - 1 or not last
                        if more:
                            front(c, n + 1, c if n < NB - 1 else c + 1)
                        if n == 4:
                            sampled_norm()
                        if n == KEYS_AT and not last:
                            keys(c + 1, (0, 1, 7))
                        turned_copy(n)
                        if more:
                            back(c, n + 1)
                        if n in (2, 3, 5):
                            sampled(n)
                        if n == 0 and not last:
                            for f in range(2):
                                split_lo(c + 1, f)

                for f in range(2):
                    split_lo(0, f)
                keys(0, (3, 6, 7))
                front(0, 0, 0)
                back(0, 0)
                walk(dve, body)

            @block.tensor
            def _(pe):
                def turn_keys(c, where):
                    pe.wait_ge(kd_done, c + 1)
                    for q in range(3):
                        for t in range(q * 4, min(q * 4 + 4, NT)):
                            tr = pe.transpose(banks[where[q]][:, (t - q * 4) * P:(t - q * 4 + 1) * P],
                                              Kd[:, t].rearrange("p o d -> p (o d)"), ch.ident[:])
                        tr.then_inc(kt_turned, 1)

                def scores(c, n):
                    if n >= 2:
                        pe.wait_ge(s_sum, c * NB + n - 1)
                    if n == 1:
                        pe.wait_ge(q_out, projected(c, 0))
                    if n == NB:
                        pe.wait_ge(kt_done, c * 3 + 6)
                        pe.wait_ge(q_out, projected(c, 2))
                    b = n % NB
                    keys = slice(max(b - 1, 0) * P, (b + 1) * P)
                    for g in range(GQA):
                        r = slice((g % 2) * HD, (g % 2 + 1) * HD)
                        mm = pe.matmul(s_bank(n, g)[:, cols_of(n)], qT[r, g // 2, b * P:(b + 1) * P], kT[r, keys], start=True, stop=True)
                    mm.then_inc(s_mm, 1)

                def body(c, last):
                    def chunk(n):
                        g, f = CHUNK[n]
                        k = ORDER.index(n)
                        if n <= 5:
                            pe.wait_ge(z_out, c * Z_OUT + n)
                        elif n == 6:
                            pe.wait_ge(z_norm, c * 4 + 4)
                        else:
                            pe.wait_ge(q_out, projected(c, k))
                            pe.wait_ge(kt_done, c * 3 + 6)
                        pe.wait_ge(lo_done, c * 2 + 2 + f + 1)
                        for kk in range(KT):
                            cols = slice(g * TG, (g + 1) * TG)
                            mm = split_matmuls(pe, b7[:, 0:TG], (wH[:, f, kk, :], wL[:, f, kk, :]), (ch.xH[:, kk, cols], ch.xL[:, kk, cols]),
                                               kk == 0, kk == KT - 1)
                        mm.then_inc(q_mm, 1)

                    def turn(n):
                        pe.wait_ge(p_norm, c * NB + n + 1)
                        for kb in range(2):
                            pe.wait_ge(pt_hi if kb == 0 else pt_lo, c * NB + n)
                            for g in range(GQA):
                                src = kb if n > 0 else 1
                                tr = pe.transpose(banks[4 + kb][:, g * P:(g + 1) * P], S[:, n % 2, g, src * P:(src + 1) * P], ch.ident[:])
                            tr.then_inc(p_turned, 1)

                    def weigh(n):
                        if n == 0:
                            pe.wait_ge(vd_done, c + 1)
                        pe.wait_ge(pt_hi, c * NB + n + 1)
                        pe.wait_ge(pt_lo, c * NB + n + 1)
                        pe.wait_ge(o_out, c * 2 * NB + 2 * n)
                        for kb in range(0 if n else 1, 2):
                            mm = pe.matmul(banks[6][:], Vd[:, n - 1 + kb].rearrange("p o d -> p (o d)"), PT[:, kb].rearrange("p g i -> p (g i)"),
                                           start=(kb == (0 if n else 1)), stop=(kb == 1))
                        mm.then_inc(o_mm, 1)

                    def sampled(step):
                        if step:
                            pe.wait_ge(z_out, c * Z_OUT + step)
                        else:
                            pe.wait_ge(z_norm, c * 4)
                            pe.wait_ge(q_out, projected(c, 0))
                        if step in CHUNK and not last:
                            pe.wait_ge(q_out, projected(c, ORDER.index(step)) + 1)
                        if step in (0, 1):
                            pe.wait_ge(ck_in, c * (32 * DB) + 32 * DB)
                            for b in range(4):
                                mm = pe.transpose(b7[:, b * P:(b + 1) * P], cK[:, 4 * step + b].rearrange("p o d -> p (o d)"), ch.ident[:])
                        if step == 2:
                            for par in range(2):
                                r = slice(par * HD, (par + 1) * HD)
                                qs = qT[r, :, SEQ:T].rearrange("p f (b i) -> p b f i", b=DB)
                                for b in range(DB):
                                    pe.matmul(b7[:, b * 16 + par * 8:b * 16 + par * 8 + 8].rearrange("p (f i) -> p f i", f=2),
                                              cKT[r, b, :], qs[:, b], start=True, stop=True)
                                mm = pe.matmul(b7[0:NS, P:2 * P].rearrange("p (b r f i) -> p r b f i", r=2, f=2, i=DL)[:, par],
                                               kT[r, SEQ:T], qs, start=True, stop=True)
                                if par == 0:
                                    mm.then_inc(z_par, 1)
                                    pe.wait_ge(z_par, c + 1)
                        if step == 3:
                            pe.transpose(b7[:, 0:P], ZT[:, 0, :], ch.ident[:])
                            mm = pe.transpose(b7[:, P:P + NS], ZT[0:NS, 1, :], ch.ident[0:NS, 0:NS])
                        if step == 4:
                            pe.wait_ge(z_red, c * 2 + 2)
                            pe.transpose(b7[:, 0:P], Z[:, 0:P], ch.ident[:])
                            mm = pe.transpose(b7[0:NS, P:2 * P], Z[:, P:P + NS], ch.ident[:])
                        if step == 5:
                            pe.wait_ge(cv_in, c * (32 * DB) + 32 * DB)
                            pe.matmul(b7[:, 0:P], Vd[0:NS, NB].rearrange("p o d -> p (o d)"), ZT[0:NS, 1, :], start=True, stop=False)
                            for b in range(DB):
                                mm = pe.matmul(b7[:, b * 16:(b + 1) * 16], cV[:, b].rearrange("p o d -> p (o d)"), ZT[:, 0, b * 16:(b + 1) * 16],
                                               start=False, stop=(b == DB - 1))
                        mm.then_inc(z_mm, 1)

                    for n in range(NB):
                        if n < NB - 1 or not last:
                            scores(c, n + 1)
                        if n >= 1:
                            weigh(n - 1)
                        if n in CHUNK and not last:
                            chunk(n)
                        if n == KEYS_AT and not last:
                            pe.wait_ge(q_out, projected(c, ORDER.index(n)) + 1)
                            turn_keys(c + 1, (0, 1, 7))
                        turn(n)
                        if n < Z_PER:
                            sampled(n)
                    weigh(NB - 1)

                turn_keys(0, (3, 6, 7))
                for f in range(2):
                    pe.wait_ge(lo_done, f + 1)
                    pe.wait_ge(kt_done, 3)
                    t_layout_product(pe, banks[3 * f:3 * f + 3], (wH[:, f], wL[:, f]), (ch.xH, ch.xL)).then_inc(q_mm, 1)
                pe.wait_ge(q_out, 2)
                scores(0, 0)
                walk(pe, body)


def stage_branch_attn(nc, ch):
    sem = ch.sem
    KINDS = 3
    w_in = ch.w_sems["branch"]
    hi_done, lo_done, mm_done = sem("b_hi"), sem("b_lo"), sem("b_mm")
    a_hi, a_lo = sem("b_ahi"), sem("b_alo")
    ga_out, gr_out, m1_out, gr_st, m1_st = sem("b_ga"), sem("b_gr"), sem("b_m1"), sem("b_grst"), sem("b_m1st")
    with ExitStack() as st:
        sb = ch.sbuf(st)
        assert nc.sbuf_base == ch.attn_at
        brL, brH = sb("brL", [P, KT, T], F32R), sb("brH", [P, KT, T], F32R)
        raw = ch.raw
        wH, wL = sb("b_wH", [P, KINDS, KT, P], F32R), sb("b_wL", [P, KINDS, KT, P], F32R)
        ga, gr, m1 = sb("b_ga_s", [P, T]), sb("b_gr_s", [P, T]), sb("b_m1_s", [P, T])
        banks = ch.banks

        def bank_set(m2, q):
            b = 3 * ((m2 * KINDS + q) % 2)
            return banks[b:b + 3]

        def walk(eng, step):
            with eng.Fori(0, KT // 2 - 1) as j:
                for m2 in range(2):
                    step(j * 2 + m2, m2, False)
            step(KT - 2, 0, False)
            step(KT - 1, 1, True)

        with nc.Block() as block:
            @block.sync
            def _(sp):
                def load(m, q):
                    src = (ch.w_in[:, :, ds(m * P + C_GA, P)], ch.w_in[:, :, ds(m * P + C_GRT, P)], ch.w_attn[:, :, ds(m * P, P)])[q]
                    sp.dma_start(raw[:, q], src).then_inc(w_in[q], 16)

                with sp.Fori(1, KT) as m:
                    for q in range(KINDS):
                        sp.wait_ge(lo_done, m * KINDS - KINDS + q + 1)
                        apart(sp, ch)
                        load(m, q)
                sp.wait_ge(lo_done, KT * KINDS)
                first_loads(sp, ch, "retention")

            @block.gpsimd
            def _(pool):
                with pool.Fori(0, KT) as m:
                    pool.wait_ge(gr_out, m + 1)
                    apart(pool, ch)
                    pool.dma_start(ch.gate_t[:, ds(m, 1), :].rearrange("p o t -> p (o t)"), gr[:]).then_inc(gr_st, 16)
                    pool.wait_ge(m1_out, m + 1)
                    apart(pool, ch)
                    pool.dma_start(ch.m1_t[:, ds(m, 1), :].rearrange("p o t -> p (o t)"), m1[:]).then_inc(m1_st, 16)
                pool.wait_ge(gr_st, 16 * KT)
                pool.wait_ge(m1_st, 16 * KT)

            @block.scalar
            def _(act):
                def split_hi(m, q):
                    act.wait_ge(w_in[q], m * 16 + 16)
                    act.activation(wH[:, q], raw[:, q], ACT.Copy).then_inc(hi_done, 1)

                split_hi(0, 0)
                split_hi(0, 1)
                for k in range(KT):
                    act.activation(brH[:, k, :], ch.attn[:, k, :], ACT.Copy).then_inc(a_hi, 1)
                split_hi(0, 2)

                def step(m, m2, last):
                    act.wait_ge(m1_out, m)
                    act.wait_ge(gr_st, m * 16)
                    for q in range(KINDS):
                        act.wait_ge(mm_done, m * KINDS + q + 1)
                        if q < 2:
                            dst, done = ((ga, ga_out), (gr, gr_out))[q]
                            for g in range(3):
                                ins = act.activation(dst[:, g * TG:(g + 1) * TG], bank_set(m2, q)[g][:, 0:TG], ACT.Sigmoid)
                            ins.then_inc(done, 1)
                        if not last:
                            split_hi(m + 1, q)

                walk(act, step)

            @block.vector
            def _(dve):
                def split_lo(m, q):
                    dve.wait_ge(hi_done, m * KINDS + q + 1)
                    dve.tensor_tensor(wL[:, q], raw[:, q], wH[:, q].bitcast(F32), ALU.subtract).then_inc(lo_done, 1)

                split_lo(0, 0)
                split_lo(0, 1)
                for k in range(KT):
                    dve.wait_ge(a_hi, k + 1)
                    dve.tensor_tensor(brL[:, k, :], ch.attn[:, k, :], brH[:, k, :].bitcast(F32), ALU.subtract).then_inc(a_lo, 1)
                split_lo(0, 2)

                def step(m, m2, last):
                    if not last:
                        split_lo(m + 1, 0)
                        split_lo(m + 1, 1)
                    dve.wait_ge(mm_done, m * KINDS + 3)
                    dve.wait_ge(ga_out, m + 1)
                    dve.wait_ge(m1_st, m * 16)
                    for g in range(3):
                        cols = slice(g * TG, (g + 1) * TG)
                        ins = dve.tensor_tensor(m1[:, cols], bank_set(m2, 2)[g][:, 0:TG], ga[:, cols], ALU.mult)
                    ins.then_inc(m1_out, 1)
                    if not last:
                        split_lo(m + 1, 2)

                walk(dve, step)

            @block.tensor
            def _(pe):
                with pe.Fori(0, KT // 2) as j:
                    for m2 in range(2):
                        m = j * 2 + m2
                        for q, free in ((0, (gr_out, m)), (1, (m1_out, m)), (2, (ga_out, m + 1))):
                            pe.wait_ge(lo_done, m * KINDS + q + 1)
                            pe.wait_ge(*free)
                            if q == 2:
                                pe.wait_ge(a_lo, KT)
                            t_layout_product(pe, bank_set(m2, q), (wH[:, q], wL[:, q]), (ch.xH, ch.xL) if q < 2 else (brH, brL)).then_inc(mm_done, 1)


def stage_retention(nc, ch, ret):
    sem = ch.sem
    ORDER = [(C_GR, DV, 4), (C_GR + P, DV, 5), (C_QR, DK, 0), (C_KR, DK, 1), (C_VR, DV, 2), (C_VR + P, DV, 3)]
    PIECES = len(ORDER)
    CHUNKS = [(f, g) for f in range(DVT) for g in range(3)]
    before = lambda h, k=0: DVT + len(CHUNKS) * h + k
    w_in = ch.w_sems["retention"]
    tab_in, hi_done, lo_done, g_mm, sg_done, g_done = sem("r_tab"), sem("r_hi"), sem("r_lo"), sem("r_gmm"), sem("r_sg"), sem("r_g")
    p_mm, v_out, rot_a, rot_b, rot_done = sem("r_pmm"), sem("r_v"), sem("r_ra"), sem("r_rb"), sem("r_rot")
    turned, t_out, s_mm, s_out, o_mm, st_mm, st_out = (
        sem("r_t"), sem("r_tout"), sem("r_smm"), sem("r_sout"), sem("r_omm"), sem("r_stmm"), sem("r_stout"))
    sq_done, ss_mm, ms_done, root_done, rstd_done, og_done, r_done = (
        sem("r_sq"), sem("r_ssmm"), sem("r_ms"), sem("r_root"), sem("r_rstd"), sem("r_og"), sem("r_r"))
    s0_in, s0_new, s0_stored, stored = sem("r_s0"), sem("r_s0n"), sem("r_s0s"), sem("r_stored")
    km_done, z_mm, dec_done = sem("r_km"), sem("r_zmm"), sem("r_dec")
    with ExitStack() as st:
        sb = ch.sbuf(st)
        raw = ch.raw
        wH, wL = sb("r_wH", [P, KT, PIECES * P], F32R), sb("r_wL", [P, KT, PIECES * P], F32R)
        gs = sb("r_gs", [P, DVT, T])
        cos, sin = sb("r_cos", [P, NT, DK // 2]), sb("r_sin", [P, NT, DK // 2])
        decay, sdecay = sb("r_decay", [P, RH, P]), sb("r_sdecay", [NS, RH, NS])
        qdec, kdec, sqdec, cdec, scdec = (sb("r_" + n, [m, RH]) for n, m in (("qdec", P), ("kdec", P), ("sqdec", NS), ("cdec", P), ("scdec", P)))
        skdec = sb("r_skdec", [NS, DB, RH])
        dec = sb("r_dec_h", [P, 3])
        ones = sb("r_ones", [P, P])
        ta, tb = sb("r_ta", [P, 2, DK]), sb("r_tb", [P, 2, DK])
        rot = sb("r_rotd", [P, 2, 4, DK])
        v = sb("r_vn", [P, 3, DV])
        qkT = sb("r_qkT", [P, 3, P])
        sT = sb("r_sT", [P, P])
        S = sb("r_S", [P, DV])
        sq, og = sb("r_sqv", [P, DVT, P]), sb("r_ogv", [P, DVT, P])
        rstd = sb("r_rstdv", [P, P])
        S0 = sb("r_S0", [P, DB, DV])
        kmask = sb("r_kmask", [NS, 2, DK])
        banks = ch.banks
        half = DK // 2

        def out_bank(t, f):
            m = rows_of(t)
            if t == NB:
                return banks[4 + 3 * f][:, 0:m]
            return banks[4 + 3 * (t % 2)][:, f * P:f * P + m]

        def state_bank(b):
            return banks[5 if b % 2 else 3][:, 0:DV]

        def walk(eng, body):
            with eng.Fori(0, RH - 1) as h:
                body(h, False)
            body(RH - 1, True)

        with nc.Block() as block:
            @block.sync
            def _(sp):
                for dst, name in ((cos, "cos"), (sin, "sin"), (decay, "decay"), (sdecay, "samp_decay"), (qdec, "q_decay"), (kdec, "k_decay"),
                                  (sqdec, "samp_q_decay"), (cdec, "c_decay"), (scdec, "samp_c_decay"), (skdec, "samp_k_decay"), (ones, "ones")):
                    sp.dma_start(dst[:], ch.c[name]).then_inc(tab_in, 16)

                def load(h, p):
                    c0, step, _ = ORDER[p % PIECES]
                    sp.wait_ge(lo_done, h * PIECES + p - 1)
                    apart(sp, ch)
                    sp.dma_start(raw[:, p % 2], ch.w_in[:, :, ds((h + p // PIECES) * step + c0, P)]).then_inc(w_in[p % 2], 16)

                with sp.Fori(0, RH - 1) as h:
                    for p in range(2, PIECES + 2):
                        load(h, p)
                for p in range(2, PIECES):
                    load(RH - 1, p)
                sp.wait_ge(lo_done, RH * PIECES)
                first_loads(sp, ch, "merge")

            @block.gpsimd
            def _(pool):
                pool.wait_ge(tab_in, 16 * 11)
                with pool.Fori(0, RH) as h:
                    pool.wait_ge(rot_done, h * NT)
                    pool.tensor_copy(dec[:, 0:1], qdec[:, ds(h, 1)])
                    pool.tensor_copy(dec[:, 1:2], kdec[:, ds(h, 1)])
                    pool.tensor_copy(dec[0:NS, 2:3], sqdec[:, ds(h, 1)]).then_inc(dec_done, 1)
                    pool.wait_ge(s0_stored, h * 16)
                    apart(pool, ch)
                    pool.dma_start(S0[:], ch.state_ret[:, ds(h, 1)].rearrange("b o d e -> d (b o) e")).then_inc(s0_in, 16)
                    for t in range(NT):
                        m = rows_of(t)
                        n = h * NT + t + 1
                        r = rot[0:m, t % 2]
                        a, b = (x[0:m].rearrange("p a (s d) -> p a s d", s=2) for x in (ta, tb))
                        dst = r.rearrange("p (a b) (s d) -> p a b s d", b=2, s=2)[:, :, 0]
                        pool.wait_ge(rot_a, n)
                        if t >= 2:
                            pool.wait_ge(turned, n - 2)
                            pool.wait_ge(st_mm, h * NB + t - 1)
                        else:
                            pool.wait_ge(turned, h * NT)
                            pool.wait_ge(st_mm, h * NB)
                            pool.wait_ge(km_done, h * DB)
                        pool.tensor_tensor(dst[:, :, 0], a[:, :, 0], b[:, :, 1], ALU.subtract)
                        pool.tensor_tensor(dst[:, :, 1], a[:, :, 1], b[:, :, 0], ALU.add).then_inc(rot_b, 1)
                        pool.wait_ge(rot_b, n)
                        pool.wait_ge(dec_done, h + 1)
                        apart(pool, ch)
                        col = 0 if t < NB else 2
                        pool.tensor_scalar(r[:, 1, :], r[:, 0, :], dec[0:m, col:col + 1], None, ALU.mult)
                        pool.tensor_scalar(r[:, 3, :], r[:, 2, :], dec[0:m, 1:2], None, ALU.mult).then_inc(rot_done, 1)
                    pool.wait_ge(st_out, h * NB + NB)
                    apart(pool, ch)
                    pool.dma_start(ch.new_state_prompt[ds(h, 1)].rearrange("o d e -> d (o e)"), S[:]).then_inc(stored, 16)
                    pool.wait_ge(s0_new, h * DB + DB)
                    apart(pool, ch)
                    pool.dma_start(ch.new_state_sample[:, ds(h, 1)].rearrange("b o d e -> d (b o) e"), S0[:]).then_inc(s0_stored, 16)
                pool.wait_ge(stored, 16 * RH)
                pool.wait_ge(s0_stored, 16 * RH)

            @block.scalar
            def _(act):
                def split_hi(h, p, count):
                    slot = ORDER[p][2]
                    act.wait_ge(w_in[p % 2], count)
                    act.activation(wH[:, :, slot * P:(slot + 1) * P], raw[:, p % 2], ACT.Copy).then_inc(hi_done, 1)

                def sigmoid(bank, f, g):
                    return act.activation(gs[:, f, g * TG:(g + 1) * TG], bank[:, 0:TG], ACT.Sigmoid)

                def body(h, last):
                    def next_piece(p):
                        split_hi(h + 1, p, h * 48 + 48 + 16 * (p // 2 + 1))

                    def gate_chunk(k):
                        f, g = CHUNKS[k]
                        act.wait_ge(g_mm, before(h, k) + 1)
                        act.wait_ge(og_done, h * NT + (3, 6, NT)[g])
                        sigmoid(banks[k % 2], f, g).then_inc(sg_done, 1)

                    def evac_v(t):
                        m = rows_of(t)
                        act.wait_ge(p_mm, h * NT + t + 1)
                        if t >= 3:
                            act.wait_ge(o_mm, h * NT + t - 2)
                            act.wait_ge(st_mm, h * NB + t - 2)
                        else:
                            act.wait_ge(o_mm, h * NT)
                            act.wait_ge(z_mm, h * DB)
                        act.activation(v[0:m, t % 3], banks[t % 2][0:m, 2 * P:4 * P], ACT.Copy).then_inc(v_out, 1)

                    evac_v(0)
                    evac_v(1)
                    for t in range(NT):
                        m = rows_of(t)
                        act.wait_ge(turned, h * NT + t + 1)
                        act.activation(qkT[:, :, 0:m], banks[2][:, 0:3 * P].rearrange("p (a i) -> p a i", a=3)[:, :, 0:m], ACT.Copy).then_inc(t_out, 1)
                        if t + 2 < NT:
                            evac_v(t + 2)
                        if t == NB and not last:
                            gate_chunk(0)
                            gate_chunk(1)
                        act.wait_ge(o_mm, h * NT + t + 1)
                        act.wait_ge(ss_mm, h * NT + t)
                        for f in range(DVT):
                            ins = act.activation(sq[:, f, 0:m], out_bank(t, f), ACT.Square)
                        ins.then_inc(sq_done, 1)
                        if t in (2, 3) and not last:
                            act.wait_ge(g_mm, before(h))
                            next_piece(t - 2)
                        if t == NB and not last:
                            act.wait_ge(p_mm, h * NT + NT)
                            for k in range(2, len(CHUNKS)):
                                gate_chunk(k)
                                next_piece(k)
                        act.wait_ge(ms_done, h * NT + t + 1)
                        act.activation(rstd[:, 0:m], rstd[:, 0:m], ACT.Sqrt).then_inc(root_done, 1)

                for p in range(PIECES):
                    split_hi(0, p, 16 * (p // 2 + 1))
                for f in range(DVT):
                    act.wait_ge(g_mm, f + 1)
                    for g in range(3):
                        ins = sigmoid(banks[3 * f + g], f, g)
                    ins.then_inc(sg_done, 1)
                walk(act, body)

            @block.vector
            def _(dve):
                def split_lo(h, p):
                    slot = ORDER[p][2]
                    cols = slice(slot * P, (slot + 1) * P)
                    dve.wait_ge(hi_done, h * PIECES + p + 1)
                    dve.tensor_tensor(wL[:, :, cols], raw[:, p % 2], wH[:, :, cols].bitcast(F32), ALU.subtract).then_inc(lo_done, 1)

                def silu(bank, f, g):
                    cols = slice(g * TG, (g + 1) * TG)
                    return dve.tensor_tensor(gs[:, f, cols], bank[:, 0:TG], gs[:, f, cols], ALU.mult)

                def body(h, last):
                    def gate_chunk(k):
                        f, g = CHUNKS[k]
                        dve.wait_ge(sg_done, before(h, k) + 1)
                        silu(banks[k % 2], f, g).then_inc(g_done, 1)

                    def mask_keys(b):
                        if b >= 2:
                            dve.wait_ge(z_mm, h * DB + b - 1)
                        dve.tensor_scalar(kmask[:, b % 2], rot[0:NS, NB % 2, 2, :], skdec[:, b, ds(h, 1)], None, ALU.mult).then_inc(km_done, 1)

                    def new_state(b):
                        dve.wait_ge(z_mm, h * DB + b + 1)
                        dve.scalar_tensor_tensor(out=S0[:, b], in0=S0[:, b], scalar=scdec[:, ds(h, 1)], in1=state_bank(b),
                                                 op0=ALU.mult, op1=ALU.add).then_inc(s0_new, 1)

                    def gated(t, n):
                        m = rows_of(t)
                        dve.wait_ge(sq_done, n)
                        dve.wait_ge(r_done, n - 1)
                        for f in range(DVT):
                            ins = dve.tensor_tensor(og[:, f, 0:m], out_bank(t, f), gs[:, f, t * P:t * P + m], ALU.mult)
                        ins.then_inc(og_done, 1)

                    def products(t):
                        m = rows_of(t)
                        x = banks[t % 2][0:m, 0:2 * P].rearrange("p (a d) -> p a d", a=4)
                        dve.wait_ge(v_out, h * NT + t + 1)
                        dve.wait_ge(rot_b, h * NT + t)
                        for dst, tab in ((ta, cos), (tb, sin)):
                            ins = dve.tensor_tensor(dst[0:m].rearrange("p a (s d) -> p (a s) d", s=2), x,
                                                    tab[0:m, t, :].rearrange("p (a d) -> p a d", a=1).broadcast_to([m, 4, half]), ALU.mult)
                        ins.then_inc(rot_a, 1)

                    products(0)
                    products(1)
                    for t in range(NT):
                        m = rows_of(t)
                        n = h * NT + t + 1
                        dve.wait_ge(s_mm, n)
                        dve.tensor_tensor(sT[0:m, 0:m], banks[3][0:m, 0:m],
                                          (decay if t < NB else sdecay)[0:m, ds(h, 1), 0:m].rearrange("p o i -> p (o i)"), ALU.mult).then_inc(s_out, 1)
                        if t + 2 < NT:
                            products(t + 2)
                        if t < NB:
                            dve.wait_ge(st_mm, h * NB + t + 1)
                            if t == 0:
                                dve.wait_ge(stored, h * 16)
                                dve.tensor_copy(S[:], banks[5][:, 0:DV]).then_inc(st_out, 1)
                            else:
                                dve.scalar_tensor_tensor(out=S[:], in0=S[:], scalar=cdec[:, ds(h, 1)], in1=banks[5][:, 0:DV],
                                                         op0=ALU.mult, op1=ALU.add).then_inc(st_out, 1)
                            if t in (2, 3) and not last:
                                split_lo(h + 1, t - 2)
                            gated(t, n)
                        else:
                            if not last:
                                gate_chunk(0)
                                gate_chunk(1)
                            dve.wait_ge(s0_in, h * 16 + 16)
                            mask_keys(0)
                            mask_keys(1)
                            gated(t, n)
                            for b in range(0, DB, 2):
                                if not last:
                                    gate_chunk(2 + b // 2)
                                    split_lo(h + 1, 2 + b // 2)
                                new_state(b)
                                if b + 2 < DB:
                                    mask_keys(b + 2)
                                new_state(b + 1)
                                if b + 2 < DB:
                                    mask_keys(b + 3)
                        dve.wait_ge(ss_mm, n)
                        dve.tensor_scalar(rstd[:, 0:m], banks[6][:, 0:m], 1.0 / DV, EPS, ALU.mult, ALU.add).then_inc(ms_done, 1)
                        dve.wait_ge(root_done, n)
                        dve.reciprocal(rstd[:, 0:m], rstd[:, 0:m]).then_inc(rstd_done, 1)
                        dve.wait_ge(rstd_done, n)
                        dve.wait_ge(og_done, n)
                        dve.tensor_tensor(ret[:, ds(h * DVT, DVT), t * P:t * P + m], og[:, :, 0:m],
                                          rstd[:, 0:m].rearrange("p (o i) -> p o i", o=1).broadcast_to([P, DVT, m]), ALU.mult).then_inc(r_done, 1)

                for p in range(PIECES):
                    split_lo(0, p)
                for f in range(DVT):
                    dve.wait_ge(sg_done, f + 1)
                    for g in range(3):
                        ins = silu(banks[3 * f + g], f, g)
                    ins.then_inc(g_done, 1)
                dve.wait_ge(tab_in, 16 * 11)
                walk(dve, body)

            @block.tensor
            def _(pe):
                def body(h, last):
                    def gate_chunk(k):
                        f, g = CHUNKS[k]
                        if k >= 2:
                            pe.wait_ge(g_done, before(h, k - 1))
                        else:
                            pe.wait_ge(v_out, h * NT + NT)
                            pe.wait_ge(rot_a, h * NT + NT)
                        pe.wait_ge(lo_done, (h + 1) * PIECES + f + 1)
                        for kk in range(KT):
                            cols, w = slice(g * TG, (g + 1) * TG), slice((4 + f) * P, (5 + f) * P)
                            mm = split_matmuls(pe, banks[k % 2][:, 0:TG], (wH[:, kk, w], wL[:, kk, w]), (ch.xH[:, kk, cols], ch.xL[:, kk, cols]),
                                               kk == 0, kk == KT - 1)
                        mm.then_inc(g_mm, 1)

                    def project(t, ks):
                        m = rows_of(t)
                        if ks[0] == 0:
                            if t < 2:
                                pe.wait_ge(g_done, before(h))
                            else:
                                pe.wait_ge(v_out, h * NT + t - 1)
                                pe.wait_ge(rot_a, h * NT + t - 1)
                        for k in ks:
                            mm = split_matmuls(pe, banks[t % 2][0:m, :], (ch.xH[:, k, t * P:t * P + m], ch.xL[:, k, t * P:t * P + m]),
                                               (wH[:, k, 0:4 * P], wL[:, k, 0:4 * P]), k == 0, k == KT - 1)
                        if ks[-1] == KT - 1:
                            mm.then_inc(p_mm, 1)

                    def sum_squares(t):
                        m = rows_of(t)
                        pe.wait_ge(sq_done, h * NT + t + 1)
                        pe.wait_ge(ms_done, h * NT + t)
                        for f in range(DVT):
                            mm = pe.matmul(banks[6][:, 0:m], ones[:], sq[:, f, 0:m], start=(f == 0), stop=(f == DVT - 1))
                        mm.then_inc(ss_mm, 1)

                    pe.wait_ge(lo_done, h * PIECES + PIECES)
                    pe.wait_ge(tab_in, 16 * 11)
                    project(0, range(KT))
                    project(1, range(KT))
                    pe.wait_ge(og_done, h * NT)
                    pe.wait_ge(sq_done, h * NT)
                    pe.wait_ge(s0_new, h * DB)
                    for t in range(NT):
                        m = rows_of(t)
                        n = h * NT + t + 1
                        pe.wait_ge(rot_done, n)
                        pe.wait_ge(t_out, n - 1)
                        if t == NB:
                            apart(pe, ch)
                        for a in range(3):
                            tr = pe.transpose(banks[2][:, a * P:a * P + m], rot[0:m, t % 2, a, :], ch.ident[0:m, 0:m])
                        tr.then_inc(turned, 1)
                        if t >= 1:
                            sum_squares(t - 1)
                        if t + 2 < NT:
                            project(t + 2, range(KT // 2))
                        if t == NB and not last:
                            gate_chunk(0)
                        pe.wait_ge(t_out, n)
                        pe.wait_ge(s_out, n - 1)
                        pe.matmul(banks[3][0:m, 0:m], qkT[:, 2, 0:m], qkT[:, 0, 0:m], start=True, stop=True).then_inc(s_mm, 1)
                        if t + 2 < NT:
                            project(t + 2, range(KT // 2, KT))
                        if t == NB and not last:
                            gate_chunk(1)
                        pe.wait_ge(s_out, n)
                        pe.wait_ge(v_out, n)
                        if t >= 2:
                            pe.wait_ge(og_done, n - 2 if t < NB else n - 1)
                            pe.wait_ge(sq_done, n - 2 if t < NB else n - 1)
                        if t < NB:
                            if t:
                                pe.wait_ge(st_out, h * NB + t)
                            for f in range(DVT):
                                cols = slice(f * P, (f + 1) * P)
                                mm = pe.matmul(out_bank(t, f), v[:, t % 3, cols], sT[:], start=True, stop=(t == 0))
                                if t:
                                    mm = pe.matmul(out_bank(t, f), S[:, cols], qkT[:, 1, :], start=False, stop=True)
                            mm.then_inc(o_mm, 1)
                            pe.matmul(banks[5][:, 0:DV], rot[:, t % 2, 3, :], v[:, t % 3], start=True, stop=True).then_inc(st_mm, 1)
                        else:
                            pe.wait_ge(s0_in, h * 16 + 16)
                            for f in range(DVT):
                                pe.matmul(out_bank(t, f), v[0:m, t % 3, f * P:(f + 1) * P], sT[0:m, 0:m], start=True, stop=False)
                                for b in range(DB):
                                    mm = pe.matmul(out_bank(t, f)[:, b * DL:(b + 1) * DL], S0[:, b, f * P:(f + 1) * P],
                                                   qkT[:, 1, b * DL:(b + 1) * DL], start=False, stop=(b == DB - 1))
                            mm.then_inc(o_mm, 1)
                            pe.wait_ge(st_out, h * NB + NB)
                            for b in range(DB):
                                if b % 2 == 0 and not last:
                                    gate_chunk(2 + b // 2)
                                if b >= 2:
                                    pe.wait_ge(s0_new, h * DB + b - 1)
                                pe.wait_ge(km_done, h * DB + b + 1)
                                pe.matmul(state_bank(b), kmask[:, b % 2], v[0:NS, t % 3], start=True, stop=True).then_inc(z_mm, 1)
                    sum_squares(NT - 1)

                for f in range(DVT):
                    pe.wait_ge(lo_done, f + 1)
                    w = [x[:, :, (4 + f) * P:(5 + f) * P] for x in (wH, wL)]
                    t_layout_product(pe, banks[3 * f:3 * f + 3], w, (ch.xH, ch.xL)).then_inc(g_mm, 1)
                walk(pe, body)


def stage_merge(nc, ch, ret):
    sem = ch.sem
    w_in, hi_done, lo_done, mm_done = ch.w_sems["merge"], sem("m_hi"), sem("m_lo"), sem("m_mm")
    r_hi, r_lo, g_in, m_in, g_mul, sum_done, mh_done, ml_done = (
        sem("m_rhi"), sem("m_rlo"), [sem("m_g0"), sem("m_g1")], [sem("m_m0"), sem("m_m1")], sem("m_gmul"), sem("m_sum"), sem("m_mh"), sem("m_ml"))
    with ExitStack() as st:
        sb = ch.sbuf(st)
        assert nc.sbuf_base == ch.ret_at
        rL, rH = sb("m_rL", [P, KT, T], F32R), sb("m_rH", [P, KT, T], F32R)
        raw = ch.raw
        wH, wL = sb("m_wH", [P, 2, KT, P], F32R), sb("m_wL", [P, 2, KT, P], F32R)
        gate, m1 = sb("m_gate", [P, 2, T]), sb("m_m1", [P, 2, T])
        banks = ch.banks

        def walk(eng, step):
            with eng.Fori(0, KT // 2 - 1) as j:
                for s in range(2):
                    step(j, s, False)
            for s in range(2):
                step(KT // 2 - 1, s, True)

        with nc.Block() as block:
            @block.sync
            def _(sp):
                with sp.Fori(1, KT // 2) as j:
                    for s in range(2):
                        m = j * 2 + s
                        sp.wait_ge(lo_done, m - 1)
                        apart(sp, ch)
                        sp.dma_start(raw[:, s], ch.w_ret[:, :, ds(m * P, P)]).then_inc(w_in[s], 16)
                sp.wait_ge(lo_done, KT)
                first_loads(sp, ch, "out")

            @block.gpsimd
            def _(pool):
                def load(m, s):
                    pool.dma_start(gate[:, s], ch.gate_t[:, ds(m, 1), :].rearrange("p o t -> p (o t)")).then_inc(g_in[s], 16)
                    pool.dma_start(m1[:, s], ch.m1_t[:, ds(m, 1), :].rearrange("p o t -> p (o t)")).then_inc(m_in[s], 16)

                for s in range(2):
                    load(s, s)
                with pool.Fori(1, KT // 2) as j:
                    for s in range(2):
                        pool.wait_ge(ml_done, j * 2 + s - 1)
                        apart(pool, ch)
                        load(j * 2 + s, s)

            @block.scalar
            def _(act):
                def step(j, s, last):
                    m = j * 2 + s
                    if not last:
                        act.wait_ge(w_in[s], j * 16 + 32)
                        act.wait_ge(mm_done, m + 1)
                        act.activation(wH[:, s], raw[:, s], ACT.Copy).then_inc(hi_done, 1)
                    act.wait_ge(sum_done, m + 1)
                    act.activation(ch.xH[:, ds(m, 1), :], gate[:, s:s + 1], ACT.Copy).then_inc(mh_done, 1)

                act.wait_ge(w_in[0], 16)
                act.activation(wH[:, 0], raw[:, 0], ACT.Copy).then_inc(hi_done, 1)
                for k in range(KT):
                    act.activation(rH[:, k, :], ret[:, k, :], ACT.Copy).then_inc(r_hi, 1)
                act.wait_ge(w_in[1], 16)
                act.activation(wH[:, 1], raw[:, 1], ACT.Copy).then_inc(hi_done, 1)
                walk(act, step)

            @block.vector
            def _(dve):
                def split_lo(s, count):
                    dve.wait_ge(hi_done, count)
                    dve.tensor_tensor(wL[:, s], raw[:, s], wH[:, s].bitcast(F32), ALU.subtract).then_inc(lo_done, 1)

                def step(j, s, last):
                    m = j * 2 + s
                    if not last:
                        split_lo(s, m + 3)
                    dve.wait_ge(mm_done, m + 1)
                    dve.wait_ge(g_in[s], j * 16 + 16)
                    dve.wait_ge(m_in[s], j * 16 + 16)
                    for g in range(3):
                        cols = slice(g * TG, (g + 1) * TG)
                        ins = dve.tensor_tensor(gate[:, s, cols], banks[3 * s + g][:, 0:TG], gate[:, s, cols], ALU.mult)
                    ins.then_inc(g_mul, 1)
                    dve.wait_ge(g_mul, m + 1)
                    dve.tensor_tensor(gate[:, s], gate[:, s], m1[:, s], ALU.add).then_inc(sum_done, 1)
                    dve.wait_ge(mh_done, m + 1)
                    dve.tensor_tensor(ch.xL[:, ds(m, 1), :], gate[:, s:s + 1], ch.xH[:, ds(m, 1), :].bitcast(F32), ALU.subtract).then_inc(ml_done, 1)

                split_lo(0, 1)
                for k in range(KT):
                    dve.wait_ge(r_hi, k + 1)
                    dve.tensor_tensor(rL[:, k, :], ret[:, k, :], rH[:, k, :].bitcast(F32), ALU.subtract).then_inc(r_lo, 1)
                split_lo(1, 2)
                walk(dve, step)

            @block.tensor
            def _(pe):
                def product(s, m, ready=None):
                    pe.wait_ge(lo_done, m + 1)
                    t_layout_product(pe, banks[3 * s:3 * s + 3], (wH[:, s], wL[:, s]), (rH, rL), ready).then_inc(mm_done, 1)

                product(0, 0, lambda k: pe.wait_ge(r_lo, k + 1))
                product(1, 1)
                with pe.Fori(1, KT // 2) as j:
                    for s in range(2):
                        m = j * 2 + s
                        pe.wait_ge(g_mul, m - 1)
                        product(s, m)


def stage_out(nc, ch):
    sem = ch.sem
    w_in, hi_done, lo_done, mm_done, x_in = ch.w_sems["out"] + [sem(f"o_w{q}") for q in range(3, KT)], sem("o_hi"), sem("o_lo"), sem("o_mm"), [sem("o_x0"), sem("o_x1")]
    tab_in, add_done, sq_done, ms_done, root_done, rstd_done, xn_done = (
        sem("o_tab"), sem("o_add"), sem("o_sq"), sem("o_ms"), sem("o_root"), sem("o_rstd"), sem("o_xn"))
    x2_st, xn_st, turned, t_out0, t_out1, r_mm, r_out = ([sem("o_x2s0"), sem("o_x2s1")], [sem("o_xns0"), sem("o_xns1")], sem("o_t"), sem("o_to0"), sem("o_to1"),
                                                        sem("o_rmm"), sem("o_rout"))
    NH = D // 512
    with ExitStack() as st:
        sb = ch.sbuf(st)
        more = sb("o_raw", [P, KT - 3, KT, P])
        raw = lambda q: ch.raw[:, q] if q < 3 else more[:, q - 3]
        wH, wL = sb("o_wH", [P, KT, D], F32R), sb("o_wL", [P, KT, D], F32R)
        xin, x2, xn = sb("o_xin", [P, 2, D]), sb("o_x2s", [P, 2, D]), sb("o_xns", [P, 2, D])
        junk, gain = sb("o_junk", [P, D]), sb("o_gain", [P, D])
        stat = sb("o_stat", [P, 2, 4])
        xT = sb("o_xT", [P, KT, P])
        wr, rb = sb("o_wr", [P, KT, NG + NE]), sb("o_rb", [P, NG + NE])
        banks = ch.banks
        with nc.Block() as block:
            @block.sync
            def _(sp):
                for q in range(3, KT):
                    sp.dma_start(raw(q), ch.w_out[:, :, q * P:(q + 1) * P]).then_inc(w_in[q], 16)
                for t in range(NT):
                    m, s = rows_of(t), t % 2
                    if t >= 2:
                        sp.wait_ge(add_done, t - 1)
                    src = ch.x_sample if t == NB else ch.x_prompt[t * P:(t + 1) * P, :]
                    sp.dma_start(xin[0:m, s], src).then_inc(x_in[s], 16)

            @block.gpsimd
            def _(pool):
                for dst, src in ((gain[:], ch.norm_ffn.broadcast_to([P, D])), (wr[:, :, 0:NG], ch.w_rg), (wr[:, :, NG:], ch.w_re),
                                 (rb[:, 0:NG], ch.b_rg.broadcast_to([P, NG])), (rb[:, NG:], ch.b_re.broadcast_to([P, NE]))):
                    pool.dma_start(dst, src).then_inc(tab_in, 16)
                for t in range(NT):
                    m, s = rows_of(t), t % 2
                    pool.wait_ge(add_done, t + 1)
                    pool.dma_start(ch.x2_d[t * P:t * P + m, :], x2[0:m, s]).then_inc(x2_st[s], 16)
                    pool.wait_ge(xn_done, t + 1)
                    pool.dma_start(ch.xn2_d[t * P:t * P + m, :], xn[0:m, s]).then_inc(xn_st[s], 16)
                for s in range(2):
                    n = 16 * ((NT + 1 - s) // 2)
                    pool.wait_ge(x2_st[s], n)
                    pool.wait_ge(xn_st[s], n)

            @block.scalar
            def _(act):
                for q in range(KT):
                    act.wait_ge(w_in[q], 16)
                    act.activation(wH[:, :, q * P:(q + 1) * P], raw(q), ACT.Copy).then_inc(hi_done, 1)

                def front(t):
                    m, s = rows_of(t), t % 2
                    act.wait_ge(add_done, t + 1)
                    act.activation(junk[0:m], x2[0:m, s], ACT.Square, accum_out=stat[0:m, s, 0:1]).then_inc(sq_done, 1)
                    act.wait_ge(ms_done, t + 1)
                    act.activation(stat[0:m, s, 2:3], stat[0:m, s, 1:2], ACT.Sqrt).then_inc(root_done, 1)

                def back(t):
                    m = rows_of(t)
                    act.wait_ge(turned, t * 2 + 1)
                    act.wait_ge(r_mm, t)
                    act.activation(xT[:, 0:4, 0:m], banks[4][:].rearrange("p (k i) -> p k i", k=4)[:, :, 0:m], ACT.Copy).then_inc(t_out0, 1)

                for t in range(NT + 1):
                    if t < NT:
                        front(t)
                    if t >= 1:
                        back(t - 1)

            @block.vector
            def _(dve):
                dve.memset(ch.logits[:], 0.0).then_inc(r_out, 1)
                for q in range(KT):
                    dve.wait_ge(hi_done, q + 1)
                    cols = slice(q * P, (q + 1) * P)
                    dve.tensor_tensor(wL[:, :, cols], raw(q), wH[:, :, cols].bitcast(F32), ALU.subtract).then_inc(lo_done, 1)
                dve.wait_ge(tab_in, 16 * 5)

                def front(t):
                    m, s = rows_of(t), t % 2
                    dve.wait_ge(mm_done, t + 1)
                    dve.wait_ge(x_in[s], 16 * (t // 2 + 1))
                    if t >= 2:
                        dve.wait_ge(x2_st[s], 16 * (t // 2))
                        dve.wait_ge(sq_done, t - 1)
                    for f in range(NH):
                        cols = slice(f * 512, (f + 1) * 512)
                        ins = dve.tensor_tensor(x2[0:m, s, cols], banks[2 * s + f][0:m, :], xin[0:m, s, cols], ALU.add)
                    ins.then_inc(add_done, 1)
                    dve.wait_ge(sq_done, t + 1)
                    dve.tensor_scalar(stat[0:m, s, 1:2], stat[0:m, s, 0:1], 1.0 / D, EPS, ALU.mult, ALU.add).then_inc(ms_done, 1)
                    dve.wait_ge(root_done, t + 1)
                    dve.reciprocal(stat[0:m, s, 3:4], stat[0:m, s, 2:3]).then_inc(rstd_done, 1)
                    dve.wait_ge(rstd_done, t + 1)
                    if t >= 2:
                        dve.wait_ge(xn_st[s], 16 * (t // 2))
                        dve.wait_ge(turned, 2 * (t - 1))
                    dve.scalar_tensor_tensor(out=xn[0:m, s], in0=x2[0:m, s], scalar=stat[0:m, s, 3:4], in1=gain[0:m],
                                             op0=ALU.mult, op1=ALU.mult).then_inc(xn_done, 1)

                def back(t):
                    m = rows_of(t)
                    dve.wait_ge(turned, t * 2 + 2)
                    dve.wait_ge(r_mm, t)
                    dve.tensor_copy(xT[:, 4:8, 0:m], banks[5][:].rearrange("p (k i) -> p k i", k=4)[:, :, 0:m]).then_inc(t_out1, 1)

                def logits(t):
                    m = rows_of(t)
                    dve.wait_ge(r_mm, t + 1)
                    dve.wait_ge(r_out, 1)
                    dve.tensor_tensor(ch.logits[0:m, t, :], banks[6][0:m, 0:NG + NE], rb[0:m, :], ALU.add).then_inc(r_out, 1)

                for t in range(NT + 2):
                    if t < NT:
                        front(t)
                    if t >= 2:
                        logits(t - 2)
                    if 1 <= t <= NT:
                        back(t - 1)

            @block.tensor
            def _(pe):
                def project(t):
                    m, s = rows_of(t), t % 2
                    if t >= 2:
                        pe.wait_ge(add_done, t - 1)
                    for f in range(NH):
                        pe.wait_ge(lo_done, (f + 1) * KT // NH)
                        for k in range(KT):
                            rows, cols = slice(t * P, t * P + m), slice(f * 512, (f + 1) * 512)
                            mm = split_matmuls(pe, banks[2 * s + f][0:m, :], (ch.xH[:, k, rows], ch.xL[:, k, rows]),
                                               (wH[:, k, cols], wL[:, k, cols]), k == 0, k == KT - 1)
                    mm.then_inc(mm_done, 1)

                def turn(t):
                    m, s = rows_of(t), t % 2
                    pe.wait_ge(xn_done, t + 1)
                    pe.wait_ge(t_out0, t)
                    pe.wait_ge(t_out1, t)
                    for b in range(2):
                        for k in range(4):
                            tr = pe.transpose(banks[4 + b][:, k * P:k * P + m], xn[0:m, s, (4 * b + k) * P:(4 * b + k + 1) * P], ch.ident[0:m, 0:m])
                        tr.then_inc(turned, 1)

                def route(t):
                    m = rows_of(t)
                    pe.wait_ge(t_out0, t + 1)
                    pe.wait_ge(t_out1, t + 1)
                    pe.wait_ge(r_out, t + 1)
                    for k in range(KT):
                        mm = pe.matmul(banks[6][0:m, 0:NG + NE], xT[:, k, 0:m], wr[:, k, :], start=(k == 0), stop=(k == KT - 1))
                    mm.then_inc(r_mm, 1)

                for t in range(NT + 2):
                    if t < NT:
                        project(t)
                    if t == 2:
                        pe.wait_ge(tab_in, 16 * 5)
                    if t >= 2:
                        route(t - 2)
                    if 1 <= t <= NT:
                        turn(t - 1)


def stage_route(nc, ch):
    sem = ch.sem
    step, tab_in, e_done, c_mm, scat, zeroed = sem("t_step"), sem("t_tab"), sem("t_exp"), sem("t_mm"), sem("t_scat"), sem("t_zero")
    with ExitStack() as st:
        sb = ch.sbuf(st)
        iota = sb("t_iota", [P, P])
        before, ones = sb("t_before", [P, P]), sb("t_ones", [P, P])
        tokens = sb("t_tokens", [P, NT], I32)
        noexp = sb("t_noexp", [P, NT])
        g8, gm8, f8, fm8 = (sb("t_" + n, [P, NT, 8]) for n in ("g8", "gm8", "f8", "fm8"))
        gi8, fi8 = sb("t_gi8", [P, NT, 8], U32), sb("t_fi8", [P, NT, 8], U32)
        gidx, gw, e2, den = (sb("t_" + n, [P, NT]) for n in ("gidx", "gw", "e2", "den"))
        eg, goh = sb("t_eg", [P, NT, NG]), sb("t_goh", [P, NT, NG])
        prod = sb("t_prod", [P, NT, EPG, NG])
        eid = sb("t_eid", [P, NT, 2])
        hot = sb("t_hot", [P, NT, 2, NE])
        both, tot, before_t, slotv, over = (sb("t_" + n, [P, NT, NE]) for n in ("both", "tot", "tp", "slotv", "over"))
        cnt, nov, delta, scan = sb("t_cnt", [P, NE]), sb("t_nov", [P, NE]), sb("t_delta", [P, NE]), sb("t_scan", [P, 2, NE])
        thr, cmp = sb("t_thr", [P, MAXBLK - 1]), sb("t_cmp", [P, NE, MAXOVER])
        slotp, slotf = sb("t_slotp", [P, NT, 2, NE]), sb("t_slotf", [P, NT, 2])
        tabf = sb("t_tabf", [P, 1 + MAXOVER])
        banks = ch.banks

        def across(ap, n):
            return ap.rearrange("p (a o) -> p a o", o=1).broadcast_to([P, ap.shape[1], n])

        with nc.Block() as block:
            @block.sync
            def _(sp):
                for dst, name in ((iota, "iota"), (before, "before"), (ones, "ones"), (tokens, "tokens"), (noexp, "no_expert")):
                    sp.dma_start(dst[:], ch.c[name]).then_inc(tab_in, 16)
                sp.dma_start(ch.toktab.rearrange("(b p) o -> b (p o)", p=P), ch.c["zero_slots"]).then_inc(zeroed, 16)
                for kind in "gud":
                    for q in range(NQ):
                        expert_chunk(sp, ch, kind, 0, q)
                for kind in "gu":
                    for q in range(NQ):
                        sp.wait_ge(ch.e_w_lo[kind], q + 1)
                        expert_chunk(sp, ch, kind, 1, q)

            @block.scalar
            def _(act):
                act.wait_ge(step, ch.route_steps["group"])
                act.activation(eg[:], eg[:], ACT.Exp).then_inc(e_done, 1)
                act.wait_ge(step, ch.route_steps["pair"])
                act.activation(e2[:], e2[:], ACT.Exp).then_inc(e_done, 1)
                for kind in "gu":
                    for q in range(NQ):
                        act.wait_ge(ch.e_w_in[kind][q], 16)
                        act.activation(ch.e_H[kind][:, q], ch.e_raw[kind][:, q], ACT.Copy).then_inc(ch.e_w_hi[kind], 1)

            @block.vector
            def _(dve):
                count = [0]

                def done(ins):
                    ins.then_inc(step, 1)
                    count[0] += 1
                    dve.wait_ge(step, count[0])

                dve.wait_ge(tab_in, 16 * 5)
                LG = ch.logits
                done(dve.memset(g8[:], -3e38))
                done(dve.tensor_copy(g8[:, :, 0:NG], LG[:, :, 0:NG]))
                for t in range(NT):
                    done(dve.max(gm8[:, t, :], g8[:, t, :]))
                    done(dve.max_index(gi8[:, t, :], gm8[:, t, :], g8[:, t, :]))
                done(dve.tensor_tensor(eg[:], LG[:, :, 0:NG], gm8[:, :, 0:1].broadcast_to([P, NT, NG]), ALU.subtract))
                assert count[0] == ch.route_steps["group"]
                done(dve.tensor_copy(gidx[:], gi8[:, :, 0]))
                done(dve.tensor_tensor(goh[:], across(gidx[:], NG), iota[:, None, 0:NG].broadcast_to([P, NT, NG]), ALU.is_equal))
                done(dve.tensor_tensor(prod[:], LG[:, :, NG:].rearrange("p t (g e) -> p t e g", g=NG),
                                       goh[:].rearrange("p t (o g) -> p t o g", o=1).broadcast_to([P, NT, EPG, NG]), ALU.mult))
                done(dve.tensor_reduce(f8[:], prod[:], AX, ALU.add))
                for t in range(NT):
                    done(dve.max(fm8[:, t, :], f8[:, t, :]))
                    done(dve.max_index(fi8[:, t, :], fm8[:, t, :], f8[:, t, :]))
                done(dve.tensor_tensor(e2[:], fm8[:, :, 1], fm8[:, :, 0], ALU.subtract))
                assert count[0] == ch.route_steps["pair"]
                done(dve.tensor_copy(eid[:], fi8[:, :, 0:2]))
                done(dve.scalar_tensor_tensor(out=gidx[:], in0=gidx[:], scalar=float(EPG), in1=noexp[:], op0=ALU.mult, op1=ALU.add))
                done(dve.tensor_tensor(eid[:], eid[:], across(gidx[:], 2), ALU.add))
                done(dve.tensor_tensor(hot[:].rearrange("p t k e -> p (t k) e"), across(eid[:].rearrange("p t k -> p (t k)"), NE),
                                       iota[:, None, 0:NE].broadcast_to([P, 2 * NT, NE]), ALU.is_equal))
                done(dve.tensor_tensor(both[:], hot[:, :, 0, :], hot[:, :, 1, :], ALU.add))
                assert count[0] == ch.route_steps["hot"]
                dve.wait_ge(e_done, 2)
                done(dve.tensor_reduce(den[:], eg[:], AX, ALU.add))
                done(dve.reciprocal(gw[:], den[:]))
                done(dve.tensor_scalar(den[:], e2[:], 1.0, None, ALU.add))
                done(dve.reciprocal(den[:], den[:]))
                done(dve.tensor_tensor(ch.gates[:, :, 0], gw[:], den[:], ALU.mult))
                done(dve.tensor_tensor(ch.gates[:, :, 1], ch.gates[:, :, 0], e2[:], ALU.mult))
                dve.wait_ge(c_mm, 1)
                done(dve.tensor_copy(tot[:], banks[1][:, 0:NT * NE].rearrange("p (t e) -> p t e", t=NT)))
                done(dve.memset(before_t[:, 0, :], 0.0))
                for t in range(1, NT):
                    done(dve.tensor_tensor(before_t[:, t, :], before_t[:, t - 1, :], tot[:, t - 1, :], ALU.add))
                done(dve.tensor_tensor(cnt[:], before_t[:, NT - 1, :], tot[:, NT - 1, :], ALU.add))
                done(dve.tensor_tensor(slotv[:], banks[0][:, 0:NT * NE].rearrange("p (t e) -> p t e", t=NT), before_t[:], ALU.add))
                done(dve.tensor_scalar(thr[:], iota[:, 1:MAXBLK], float(P), None, ALU.mult))
                done(dve.tensor_tensor(cmp[:, :, 0:MAXBLK - 1], across(cnt[:], MAXBLK - 1), thr[:, None, :].broadcast_to([P, NE, MAXBLK - 1]), ALU.is_gt))
                done(dve.tensor_reduce(nov[:], cmp[:, :, 0:MAXBLK - 1], AX, ALU.add))
                done(dve.tensor_copy(scan[:, 0, :], nov[:]))
                a, sh = 0, 1
                while sh < NE:
                    done(dve.tensor_copy(scan[:, 1 - a, 0:sh], scan[:, a, 0:sh]))
                    done(dve.tensor_tensor(scan[:, 1 - a, sh:NE], scan[:, a, sh:NE], scan[:, a, 0:NE - sh], ALU.add))
                    a, sh = 1 - a, sh * 2
                end = scan[:, a, :]
                done(dve.tensor_tensor(delta[:], end, nov[:], ALU.subtract))
                done(dve.tensor_tensor(delta[:], delta[:], iota[:, 0:NE], ALU.subtract))
                done(dve.tensor_scalar(delta[:], delta[:], float(NE - 1), float(P), ALU.add, ALU.mult))
                done(dve.tensor_scalar(over[:], slotv[:], float(P), None, ALU.is_ge))
                done(dve.tensor_tensor(over[:], over[:], delta[:, None, :].broadcast_to([P, NT, NE]), ALU.mult))
                done(dve.tensor_tensor(slotv[:], slotv[:], over[:], ALU.add))
                done(dve.tensor_scalar(delta[:], iota[:, 0:NE], float(P), None, ALU.mult))
                done(dve.tensor_tensor(slotv[:], slotv[:], delta[:, None, :].broadcast_to([P, NT, NE]), ALU.add))
                for k in range(2):
                    done(dve.tensor_tensor(slotp[:, :, k, :], hot[:, :, k, :], slotv[:], ALU.mult))
                done(dve.tensor_reduce(slotf[:], slotp[:], AX, ALU.add))
                done(dve.tensor_copy(ch.slots[:], slotf[:]))
                assert count[0] == ch.route_steps["slots"]
                done(dve.tensor_copy(tabf[:, 0:1], scan[:, a, NE - 1:NE]))
                done(dve.tensor_tensor(cmp[:].rearrange("p e j -> p (e j)").rearrange("p (j e) -> p j e", e=NE),
                                       scan[:, a:a + 1, :].broadcast_to([P, MAXOVER, NE]), across(iota[:, 0:MAXOVER], NE), ALU.is_le))
                done(dve.tensor_reduce(tabf[:, 1:], cmp[:].rearrange("p e j -> p (e j)").rearrange("p (j e) -> p j e", e=NE), AX, ALU.add))
                done(dve.tensor_scalar(tabf[:, 1:], tabf[:, 1:], float(NE - 1), None, ALU.min))
                done(dve.tensor_copy(ch.beyond[:], tabf[0:1, :]))
                for kind in "gu":
                    for q in range(NQ):
                        dve.wait_ge(ch.e_w_hi[kind], q + 1)
                        dve.tensor_tensor(ch.e_L[kind][:, q], ch.e_raw[kind][:, q], ch.e_H[kind][:, q].bitcast(F32), ALU.subtract).then_inc(ch.e_w_lo[kind], 1)

            @block.tensor
            def _(pe):
                pe.wait_ge(tab_in, 16 * 5)
                pe.wait_ge(step, ch.route_steps["hot"])
                flat = both[:].rearrange("p t e -> p (t e)")
                pe.matmul(banks[0][:, 0:NT * NE], before[:], flat, start=True, stop=True)
                pe.matmul(banks[1][:, 0:NT * NE], ones[:], flat, start=True, stop=True).then_inc(c_mm, 1)

            @block.gpsimd
            def _(pool):
                pool.wait_ge(tab_in, 16 * 5)
                pool.wait_ge(zeroed, 16)
                pool.wait_ge(step, ch.route_steps["slots"])
                for t in range(NT):
                    m = rows_of(t)
                    for k in range(2):
                        pool.indirect_dma_start(out=ch.toktab, out_offset=bass.IndirectOffsetOnAxis(ap=ch.slots[0:m, t, k:k + 1], axis=0),
                                                in_=tokens[0:m, t:t + 1], in_offset=None).then_inc(scat, 16)
                pool.wait_ge(scat, 16 * 2 * NT)


AHEAD = 4
NQ = 4


def expert_chunk(sp, ch, kind, e, q):
    w = {"g": ch.w_gate, "u": ch.w_up, "d": ch.w_down}[kind][ds(e, 1)].rearrange("o (k p) n -> p (o k) n", p=P)
    dst = ch.e_raw[kind][:, q]
    if kind == "d":
        sp.dma_start(dst, w[:, q, :]).then_inc(ch.e_w_in[kind][q], 16)
    else:
        sp.dma_start(dst.rearrange("p (k n) -> p k n", k=2), w[:, 2 * q:2 * q + 2, :]).then_inc(ch.e_w_in[kind][q], 16)


def stage_experts(nc, ch):
    sem = ch.sem
    w_in = ch.e_w_in
    w_hi, w_lo, used = ch.e_w_hi, ch.e_w_lo, {kind: sem(f"e_use{kind}") for kind in "gud"}
    idx_in, rows_in, x_turned, x_hi, x_lo = sem("e_idx"), sem("e_rows"), sem("e_xt"), sem("e_xhi"), sem("e_xlo")
    sig, mul, h_done, h_turned, h_hi, h_lo, y_a, y_b, y_st, go = (
        sem("e_sig"), sem("e_mul"), sem("e_h"), sem("e_ht"), sem("e_hhi"), sem("e_hlo"), sem("e_ya"), sem("e_yb"), sem("e_yst"), sem("e_go"))
    with ExitStack() as st:
        sb = ch.sbuf(st)
        raw, H, L = ch.e_raw, ch.e_H, ch.e_L
        idx = sb("e_idxs", [P, 1], I32)
        rows = sb("e_rowss", [P, D])
        xH, xL = sb("e_xH", [P, KT, P], F32R), sb("e_xL", [P, KT, P], F32R)
        hH, hL = sb("e_hH", [P, FT, P], F32R), sb("e_hL", [P, FT, P], F32R)
        sg, h = sb("e_sg", [P, FF]), sb("e_hs", [P, FF])
        y = sb("e_y", [P, D])
        banks = ch.banks
        XT, G, U, HT, Y = banks[0:2], banks[2], banks[3], banks[4], banks[5:7]

        def walk(eng, body):
            body(0, True, 2)
            with eng.Fori(1, NE - 2) as e:
                body(e, False, 2)
            body(NE - 2, False, 1)
            body(NE - 1, False, 0)

        with nc.Block() as block:
            @block.sync
            def _(sp):
                def load(kind, e):
                    for q in range(NQ):
                        sp.wait_ge(w_lo[kind], (e - 1) * NQ + q + 1)
                        expert_chunk(sp, ch, kind, e, q)

                def body(e, first, left):
                    if not first:
                        load("d", e)
                    if left >= 2:
                        load("g", e + 2)
                        load("u", e + 2)

                walk(sp, body)
                for t in range(AHEAD):
                    sp.dma_start(ch.x2_tiles[:, t], ch.x2_d[t * P:(t + 1) * P, :]).then_inc(ch.x2_in[t], 16)

            @block.gpsimd
            def _(pool):
                def gather(e):
                    pool.wait_ge(x_turned, e * 2)
                    apart(pool, ch)
                    pool.dma_start(idx[:], ch.toktab[ds(e * P, P), :]).then_inc(idx_in, 16)
                    pool.wait_ge(idx_in, e * 16 + 16)
                    apart(pool, ch)
                    pool.indirect_dma_start(out=rows[:], out_offset=None, in_=ch.xn2_d,
                                            in_offset=bass.IndirectOffsetOnAxis(ap=idx[:, 0:1], axis=0)).then_inc(rows_in, 16)

                def body(e, first, left):
                    if left >= 1:
                        gather(e + 1)

                pool.memset(idx[:], 0).then_inc(go, 1)
                pool.wait_ge(go, 1)
                gather(0)
                walk(pool, body)
                pool.wait_ge(y_st, 16 * NE)

            @block.scalar
            def _(act):
                def split_hi(kind, e):
                    for q in range(NQ):
                        act.wait_ge(w_in[kind][q], e * 16 + 16)
                        act.wait_ge(used[kind], e * NQ + q + 1)
                        act.activation(H[kind][:, q], raw[kind][:, q], ACT.Copy).then_inc(w_hi[kind], 1)

                def rows_hi(e):
                    for b in range(2):
                        act.wait_ge(x_turned, e * 2 + b + 1)
                        act.activation(xH[:, 4 * b:4 * b + 4].rearrange("p k i -> p (k i)"), XT[b][:], ACT.Copy).then_inc(x_hi, 1)

                def hidden_hi(e):
                    act.wait_ge(h_turned, e + 1)
                    act.activation(hH[:].rearrange("p k i -> p (k i)"), HT[:], ACT.Copy).then_inc(h_hi, 1)

                def gate_sigmoid(e):
                    act.wait_ge(used["g"], e * NQ + 2 * NQ)
                    act.wait_ge(h_done, e)
                    act.activation(sg[:], G[:], ACT.Sigmoid).then_inc(sig, 1)

                def out_evac(e):
                    act.wait_ge(used["d"], e * NQ + 2 * NQ)
                    act.wait_ge(y_st, e * 16)
                    act.activation(y[:, 0:512], Y[0][:], ACT.Copy).then_inc(y_a, 1)
                    act.wait_ge(y_a, e + 1)
                    act.wait_ge(y_b, e + 1)
                    apart(act, ch)
                    act.dma_start(ch.y_d[ds(e * P, P), :], y[:]).then_inc(y_st, 16)

                def body(e, first, left):
                    if not first:
                        split_hi("d", e - 1)
                        hidden_hi(e - 1)
                    if left >= 1:
                        split_hi("g", e + 1)
                        rows_hi(e + 1)
                    gate_sigmoid(e)
                    if left >= 1:
                        split_hi("u", e + 1)
                    if not first:
                        out_evac(e - 1)

                rows_hi(0)
                walk(act, body)
                split_hi("d", NE - 1)
                hidden_hi(NE - 1)
                out_evac(NE - 1)

            @block.vector
            def _(dve):
                def split_lo(kind, e):
                    for q in range(NQ):
                        dve.wait_ge(w_hi[kind], e * NQ + q + 1)
                        dve.tensor_tensor(L[kind][:, q], raw[kind][:, q], H[kind][:, q].bitcast(F32), ALU.subtract).then_inc(w_lo[kind], 1)

                def rows_lo(e):
                    for b in range(2):
                        dve.wait_ge(x_hi, e * 2 + b + 1)
                        cols = slice(4 * b, 4 * b + 4)
                        dve.tensor_tensor(xL[:, cols].rearrange("p k i -> p (k i)"), XT[b][:], xH[:, cols].rearrange("p k i -> p (k i)").bitcast(F32),
                                          ALU.subtract).then_inc(x_lo, 1)

                def hidden_lo(e):
                    dve.wait_ge(h_hi, e + 1)
                    dve.tensor_tensor(hL[:].rearrange("p k i -> p (k i)"), HT[:], hH[:].rearrange("p k i -> p (k i)").bitcast(F32),
                                      ALU.subtract).then_inc(h_lo, 1)

                def hidden(e):
                    dve.wait_ge(sig, e + 1)
                    dve.wait_ge(h_turned, e)
                    dve.tensor_tensor(h[:], G[:], sg[:], ALU.mult).then_inc(mul, 1)
                    dve.wait_ge(mul, e + 1)
                    dve.wait_ge(used["u"], e * NQ + 2 * NQ)
                    dve.tensor_tensor(h[:], U[:], h[:], ALU.mult).then_inc(h_done, 1)

                def out_evac(e):
                    dve.wait_ge(used["d"], e * NQ + 2 * NQ)
                    dve.wait_ge(y_st, e * 16)
                    dve.tensor_copy(y[:, 512:1024], Y[1][:]).then_inc(y_b, 1)

                def body(e, first, left):
                    if not first:
                        split_lo("d", e - 1)
                        hidden_lo(e - 1)
                    if left >= 1:
                        split_lo("g", e + 1)
                        rows_lo(e + 1)
                    hidden(e)
                    if left >= 1:
                        split_lo("u", e + 1)
                    if not first:
                        out_evac(e - 1)

                rows_lo(0)
                walk(dve, body)
                split_lo("d", NE - 1)
                hidden_lo(NE - 1)
                out_evac(NE - 1)

            @block.tensor
            def _(pe):
                def product(kind, out, e):
                    for q in range(NQ):
                        pe.wait_ge(w_lo[kind], e * NQ + q + 1)
                        for k2 in range(2):
                            k, cols = 2 * q + k2, slice(k2 * 512, (k2 + 1) * 512)
                            mm = split_matmuls(pe, out[:], (xH[:, k, :], xL[:, k, :]), (H[kind][:, q, cols], L[kind][:, q, cols]), k == 0, k == KT - 1)
                        mm.then_inc(used[kind], 1)

                def down(e):
                    pe.wait_ge(h_lo, e + 1)
                    pe.wait_ge(y_a, e)
                    pe.wait_ge(y_b, e)
                    for q in range(NQ):
                        pe.wait_ge(w_lo["d"], e * NQ + q + 1)
                        for f in range(2):
                            cols = slice(f * 512, (f + 1) * 512)
                            mm = split_matmuls(pe, Y[f][:], (hH[:, q, :], hL[:, q, :]), (H["d"][:, q, cols], L["d"][:, q, cols]), q == 0, q == NQ - 1)
                        mm.then_inc(used["d"], 1)

                def turn_rows(e):
                    pe.wait_ge(rows_in, e * 16 + 16)
                    pe.wait_ge(x_lo, e * 2)
                    for b in range(2):
                        for k in range(4):
                            tr = pe.transpose(XT[b][:, k * P:(k + 1) * P], rows[:, (4 * b + k) * P:(4 * b + k + 1) * P], ch.ident[:])
                        tr.then_inc(x_turned, 1)

                def turn_hidden(e):
                    pe.wait_ge(h_done, e + 1)
                    pe.wait_ge(h_lo, e)
                    for k in range(FT):
                        tr = pe.transpose(HT[:, k * P:(k + 1) * P], h[:, k * P:(k + 1) * P], ch.ident[:])
                    tr.then_inc(h_turned, 1)

                def body(e, first, left):
                    pe.wait_ge(x_lo, e * 2 + 2)
                    pe.wait_ge(h_done, e)
                    product("g", G, e)
                    if not first:
                        turn_hidden(e - 1)
                    product("u", U, e)
                    if left >= 1:
                        turn_rows(e + 1)
                    if not first:
                        down(e - 1)

                for kind in "gud":
                    pe.sem_inc(used[kind], NQ)
                turn_rows(0)
                walk(pe, body)
                turn_hidden(NE - 1)
                down(NE - 1)


def stage_beyond(nc, ch):
    sem = ch.sem
    w_in, idx_in, rows_in, x_turned, x_out, g_mm, u_mm, sig, mul, h_done, h_turned, h_out, d_mm, y_out, y_st, go = (
        sem("v_" + n) for n in ("w", "idx", "rows", "xt", "xo", "g", "u", "sig", "mul", "h", "ht", "ho", "d", "y", "yst", "go"))
    with ExitStack() as st:
        sb = ch.sbuf(st)
        wg, wu = sb("v_wg", [P, KT, FF]), sb("v_wu", [P, KT, FF])
        wd = sb("v_wd", [P, FT, D])
        idx = sb("v_idx_s", [P, 1], I32)
        rows, xT = sb("v_rows_s", [P, D]), sb("v_xT", [P, KT, P])
        sg, h, hT = sb("v_sg", [P, FF]), sb("v_h_s", [P, FF]), sb("v_hT", [P, FT, P])
        y = sb("v_y_s", [P, D])
        banks = ch.banks

        def each(eng, body):
            n = eng.value_load(ch.beyond[0:1, 0:1], min_val=0, max_val=MAXOVER)
            with eng.If(n > 0):
                with eng.Fori(0, n) as j:
                    body(j)

        with nc.Block() as block:
            @block.sync
            def _(sp):
                def body(j):
                    sp.wait_ge(d_mm, j)
                    e = sp.value_load(ch.beyond[0:1, ds(j + 1, 1)], min_val=0, max_val=NE - 1)
                    for dst, w in ((wg, ch.w_gate), (wu, ch.w_up), (wd, ch.w_down)):
                        sp.dma_start(dst[:], w[ds(e, 1)].rearrange("o (k p) n -> p (o k) n", p=P)).then_inc(w_in, 16)
                each(sp, body)

            @block.gpsimd
            def _(pool):
                def body(j):
                    pool.wait_ge(y_st, j * 16)
                    apart(pool, ch)
                    pool.dma_start(idx[:], ch.toktab[ds(j * P + NE * P, P), :]).then_inc(idx_in, 16)
                    pool.wait_ge(idx_in, j * 16 + 16)
                    apart(pool, ch)
                    pool.indirect_dma_start(out=rows[:], out_offset=None, in_=ch.xn2_d,
                                            in_offset=bass.IndirectOffsetOnAxis(ap=idx[:, 0:1], axis=0)).then_inc(rows_in, 16)
                    pool.wait_ge(y_out, j + 1)
                    apart(pool, ch)
                    pool.dma_start(ch.y_d[ds(j * P + NE * P, P), :], y[:]).then_inc(y_st, 16)
                    pool.wait_ge(y_st, j * 16 + 16)
                pool.memset(idx[:], 0).then_inc(go, 1)
                pool.wait_ge(go, 1)
                each(pool, body)

            @block.scalar
            def _(act):
                def body(j):
                    act.wait_ge(x_turned, j + 1)
                    for b in range(2):
                        ins = act.activation(xT[:, 4 * b:4 * b + 4].rearrange("p k i -> p (k i)"), banks[b][:], ACT.Copy)
                    ins.then_inc(x_out, 1)
                    act.wait_ge(u_mm, j + 1)
                    act.activation(sg[:], banks[2][:], ACT.Sigmoid).then_inc(sig, 1)
                    act.wait_ge(h_turned, j + 1)
                    act.activation(hT[:].rearrange("p k i -> p (k i)"), banks[4][:], ACT.Copy).then_inc(h_out, 1)
                    act.wait_ge(d_mm, j + 1)
                    act.wait_ge(y_st, j * 16)
                    for f in range(2):
                        ins = act.activation(y[:, f * 512:(f + 1) * 512], banks[5 + f][:], ACT.Copy)
                    ins.then_inc(y_out, 1)
                each(act, body)

            @block.vector
            def _(dve):
                def body(j):
                    dve.wait_ge(sig, j + 1)
                    dve.tensor_tensor(h[:], banks[2][:], sg[:], ALU.mult).then_inc(mul, 1)
                    dve.wait_ge(mul, j + 1)
                    dve.tensor_tensor(h[:], banks[3][:], h[:], ALU.mult).then_inc(h_done, 1)
                each(dve, body)

            @block.tensor
            def _(pe):
                def body(j):
                    pe.wait_ge(rows_in, j * 16 + 16)
                    for k in range(KT):
                        tr = pe.transpose(banks[k // 4][:, (k % 4) * P:(k % 4 + 1) * P], rows[:, k * P:(k + 1) * P], ch.ident[:])
                    tr.then_inc(x_turned, 1)
                    pe.wait_ge(x_out, j + 1)
                    pe.wait_ge(w_in, j * 48 + 48)
                    for bank, w, done in ((banks[2], wg, g_mm), (banks[3], wu, u_mm)):
                        for k in range(KT):
                            mm = pe.matmul(bank[:], xT[:, k, :], w[:, k, :], start=(k == 0), stop=(k == KT - 1))
                        mm.then_inc(done, 1)
                    pe.wait_ge(h_done, j + 1)
                    for k in range(FT):
                        tr = pe.transpose(banks[4][:, k * P:(k + 1) * P], h[:, k * P:(k + 1) * P], ch.ident[:])
                    tr.then_inc(h_turned, 1)
                    pe.wait_ge(h_out, j + 1)
                    pe.wait_ge(y_out, j)
                    for f in range(2):
                        for k in range(FT):
                            mm = pe.matmul(banks[5 + f][:], hT[:, k, :], wd[:, k, f * 512:(f + 1) * 512], start=(k == 0), stop=(k == FT - 1))
                    mm.then_inc(d_mm, 1)
                each(pe, body)


def stage_combine(nc, ch):
    sem = ch.sem
    g_in, y_in, x_in, m_done, a_done, sq_done, ms_done, root_done, rstd_done, o_done, o_st = (
        sem("c_gain"), [sem(f"c_y{s}") for s in range(AHEAD)], ch.x2_in, sem("c_m"), sem("c_a"), sem("c_sq"), sem("c_ms"), sem("c_root"),
        sem("c_rstd"), sem("c_o"), [sem("c_st0"), sem("c_st1")])
    with ExitStack() as st:
        sb = ch.sbuf(st)
        Y, x2, o = sb("c_Y", [P, AHEAD, 2, D]), ch.x2_tiles, sb("c_os", [P, 2, D])
        junk, gain, stat = sb("c_junk", [P, D]), sb("c_gains", [P, D]), sb("c_stat", [P, 2, 4])
        with nc.Block() as block:
            @block.sync
            def _(sp):
                sp.dma_start(gain[:], ch.norm_final.broadcast_to([P, D])).then_inc(g_in, 16)
                for t in range(AHEAD, NT):
                    m, s = rows_of(t), t % AHEAD
                    sp.wait_ge(m_done, t - AHEAD + 1)
                    sp.dma_start(x2[0:m, s], ch.x2_d[t * P:t * P + m, :]).then_inc(x_in[s], 16)

            @block.gpsimd
            def _(pool):
                for t in range(NT):
                    m, s = rows_of(t), t % AHEAD
                    if t >= AHEAD:
                        pool.wait_ge(o_done, t - AHEAD + 1)
                    for k in range(2):
                        pool.indirect_dma_start(out=Y[0:m, s, k, :], out_offset=None, in_=ch.y_d,
                                                in_offset=bass.IndirectOffsetOnAxis(ap=ch.slots[0:m, t, k:k + 1], axis=0)).then_inc(y_in[s], 16)

            @block.scalar
            def _(act):
                def store(t):
                    m, s = rows_of(t), t % 2
                    act.wait_ge(o_done, t + 1)
                    dst = ch.y_sample if t == NB else ch.y_prompt[t * P:(t + 1) * P, :]
                    act.dma_start(dst, o[0:m, s]).then_inc(o_st[s], 16)

                for t in range(NT):
                    m, s = rows_of(t), t % 2
                    act.wait_ge(a_done, t + 1)
                    act.activation(junk[0:m], Y[0:m, t % AHEAD, 0], ACT.Square, accum_out=stat[0:m, s, 0:1]).then_inc(sq_done, 1)
                    act.wait_ge(ms_done, t + 1)
                    act.activation(stat[0:m, s, 2:3], stat[0:m, s, 1:2], ACT.Sqrt).then_inc(root_done, 1)
                    store(t)
                for s in range(2):
                    act.wait_ge(o_st[s], 16 * ((NT + 1 - s) // 2))

            @block.vector
            def _(dve):
                def weigh(t):
                    m, a = rows_of(t), t % AHEAD
                    dve.wait_ge(y_in[a], 32 * (t // AHEAD + 1))
                    dve.wait_ge(x_in[a], 16 * (t // AHEAD + 1))
                    y0, y1 = Y[0:m, a, 0], Y[0:m, a, 1]
                    dve.scalar_tensor_tensor(out=y0, in0=y0, scalar=ch.gates[0:m, t, 0:1], in1=x2[0:m, a], op0=ALU.mult, op1=ALU.add).then_inc(m_done, 1)
                    dve.wait_ge(m_done, t + 1)
                    dve.scalar_tensor_tensor(out=y0, in0=y1, scalar=ch.gates[0:m, t, 1:2], in1=y0, op0=ALU.mult, op1=ALU.add).then_inc(a_done, 1)

                def normalize(t):
                    m, s = rows_of(t), t % 2
                    y0 = Y[0:m, t % AHEAD, 0]
                    dve.wait_ge(sq_done, t + 1)
                    dve.tensor_scalar(stat[0:m, s, 1:2], stat[0:m, s, 0:1], 1.0 / D, EPS, ALU.mult, ALU.add).then_inc(ms_done, 1)
                    dve.wait_ge(root_done, t + 1)
                    dve.reciprocal(stat[0:m, s, 3:4], stat[0:m, s, 2:3]).then_inc(rstd_done, 1)
                    dve.wait_ge(rstd_done, t + 1)
                    if t >= 2:
                        dve.wait_ge(o_st[s], 16 * (t // 2))
                    dve.scalar_tensor_tensor(out=o[0:m, s], in0=y0, scalar=stat[0:m, s, 3:4], in1=gain[0:m],
                                             op0=ALU.mult, op1=ALU.mult).then_inc(o_done, 1)

                dve.wait_ge(g_in, 16)
                weigh(0)
                for t in range(NT):
                    if t + 1 < NT:
                        weigh(t + 1)
                    normalize(t)


CONSTS = ("ident", "skew_hot", "skew_mask", "samp_hot", "samp_mask", "sink_hot", "cos", "sin", "decay", "samp_decay", "q_decay", "k_decay",
          "samp_q_decay", "samp_k_decay", "c_decay", "samp_c_decay", "ones", "before", "iota", "tokens", "no_expert", "zero_slots")
INPUTS = ("x_prompt", "x_sample", "cache_k", "cache_v", "state_ret", "norm_mix", "w_in", "attn_sink", "rel_bias", "w_branch_attn",
          "w_branch_ret", "w_out", "norm_ffn", "w_router_group", "b_router_group", "w_router_expert", "b_router_expert", "w_gate",
          "w_up", "w_down", "norm_final")
OUTPUTS = (("y_prompt", (1, SEQ, D)), ("y_sample", (DB, DL, D)), ("new_k_prompt", (1, 1, WINDOW, KVH, HD)), ("new_v_prompt", (1, 1, WINDOW, KVH, HD)),
           ("new_state_prompt", (1, 1, RH, DK, DV)), ("new_k_sample", (1, DB, WINDOW, KVH, HD)), ("new_v_sample", (1, DB, WINDOW, KVH, HD)),
           ("new_state_sample", (1, DB, RH, DK, DV)))


def hybrid_decoder_layer(nc, ins, outs, consts):
    ch = Chip()
    ch.c = consts
    ch.route_steps = {"group": 3 + 2 * NT, "pair": 3 + 2 * NT + 4 + 2 * NT + 1}
    ch.route_steps["hot"] = ch.route_steps["pair"] + 5
    ch.route_steps["slots"] = ch.route_steps["hot"] + 6 + 2 + (NT - 1) + 2 + 4 + 2 * 5 + 8 + 4
    k_tiles = lambda w: w.rearrange("o (k p) n -> p (o k) n", p=P)
    ch.x_prompt = ins["x_prompt"].rearrange("b t d -> (b t) d")
    ch.x_sample = ins["x_sample"].rearrange("b t d -> (b t) d")
    ch.cache_k, ch.cache_v = (ins[n].rearrange("o b w h d -> (o b) w (h d)") for n in ("cache_k", "cache_v"))
    ch.state_ret = ins["state_ret"].rearrange("o b h d e -> (o b) h d e")
    ch.norm_mix, ch.norm_ffn = ins["norm_mix"], ins["norm_ffn"]
    ch.norm_final = ins["norm_final"].rearrange("(o d) -> o d", o=1)
    ch.w_in, ch.w_attn, ch.w_ret, ch.w_out = (k_tiles(ins[n]) for n in ("w_in", "w_branch_attn", "w_branch_ret", "w_out"))
    ch.w_rg, ch.w_re = k_tiles(ins["w_router_group"]), k_tiles(ins["w_router_expert"])
    ch.b_rg, ch.b_re = ins["b_router_group"], ins["b_router_expert"]
    ch.attn_sink, ch.attn_sink_row = ins["attn_sink"].rearrange("o h -> h o"), ins["attn_sink"]
    ch.rel_bias = ins["rel_bias"]
    ch.w_gate, ch.w_up, ch.w_down = (ins[n].rearrange("o e a b -> (o e) a b") for n in ("w_gate", "w_up", "w_down"))
    ch.y_prompt = outs["y_prompt"].rearrange("b t d -> (b t) d")
    ch.y_sample = outs["y_sample"].rearrange("b t d -> (b t) d")
    ch.new_k_prompt, ch.new_v_prompt = (outs[n].rearrange("o b w h d -> (o b w) (h d)") for n in ("new_k_prompt", "new_v_prompt"))
    ch.new_k_sample, ch.new_v_sample = (outs[n].rearrange("o b w h d -> (o b) w (h d)") for n in ("new_k_sample", "new_v_sample"))
    ch.new_state_prompt = outs["new_state_prompt"].rearrange("o b h d e -> (o b h) d e")
    ch.new_state_sample = outs["new_state_sample"].rearrange("o b h d e -> (o b) h d e")

    skew = nc.dram_tensor("skew", [HEADS, P * SKEW], F32).ap()
    ch.skew = skew
    ch.skew_read = bass.AP(skew.tensor, P - 1, [[SKEW - 1, P], [P * SKEW, HEADS], [1, 2 * P]])
    ch.gate_t = nc.dram_tensor("gate_t", [P, KT, T], F32).ap()
    ch.m1_t = nc.dram_tensor("m1_t", [P, KT, T], F32).ap()
    ch.x2_d = nc.dram_tensor("x2_d", [T, D], F32).ap()
    ch.xn2_d = nc.dram_tensor("xn2_d", [T, D], F32).ap()
    ch.toktab = nc.dram_tensor("toktab", [SLOTS, 1], I32).ap()
    ch.y_d = nc.dram_tensor("y_d", [SLOTS, D], F32).ap()

    with ExitStack() as top:
        ch.sbuf = lambda st: (lambda name, shape, dt=F32: st.enter_context(nc.sbuf_tensor(name, shape, dt)))
        sb = ch.sbuf(top)
        ch.passed = nc.alloc_semaphore(name="passed")
        mixer_sems = []

        def mixer_sem(name):
            mixer_sems.append(nc.alloc_semaphore(name=name))
            return mixer_sems[-1]

        ch.sem = mixer_sem
        ch.banks = [top.enter_context(nc.psum_tensor(f"bank{i}", [P, 512], F32)) for i in range(8)]
        ch.ident = sb("identity", [P, P])
        ch.logits = sb("logits", [P, NT, NG + NE])
        ch.slots, ch.gates = sb("slots", [P, NT, 2], I32), sb("gates", [P, NT, 2])
        ch.beyond = sb("beyond", [1, 1 + MAXOVER], I32)
        with ExitStack() as xs:
            sb = ch.sbuf(xs)
            ch.xH, ch.xL = sb("xH", [P, KT, T], F32R), sb("xL", [P, KT, T], F32R)
            ch.raw = sb("raw", [P, 3, KT, P])
            ch.w_sems = {stage: [ch.sem(f"w_{stage}{slot}") for slot in range(3 if stage in ("kv", "branch") else 2)]
                         for stage in ("kv", "attention", "branch", "retention", "merge")}
            ch.w_sems["out"] = [nc.alloc_semaphore(name=f"w_out{slot}") for slot in range(3)]
            with ExitStack() as ab:
                ch.attn_at = nc.sbuf_base
                ch.attn = ch.sbuf(ab)("attn", [P, KT, T])
                with ExitStack() as at:
                    sb = ch.sbuf(at)
                    ch.sampbias, ch.negsink_rows = sb("sampbias", [P, KVH, P + NS]), sb("negsink_rows", [P, KVH])
                    ch.K, ch.V = sb("K", [P, NT, KVH * HD]), sb("V", [P, NT, KVH * HD])
                    with ExitStack() as bt:
                        ch.tables = BiasTables(ch, ch.sbuf(bt))
                        stage_norm(nc, ch)
                        stage_kv(nc, ch)
                    stage_attention(nc, ch)
            stage_branch_attn(nc, ch)
            with ExitStack() as rs:
                ch.ret_at = nc.sbuf_base
                ret = ch.sbuf(rs)("ret", [P, KT, T])
                stage_retention(nc, ch, ret)
            stage_merge(nc, ch, ret)
            nc.clear_and_free_semaphores(mixer_sems)
            nc.all_engine_barrier()
            ch.sem = lambda name: nc.alloc_semaphore(name=name)
            stage_out(nc, ch)
        ch.x2_tiles, ch.x2_in = ch.sbuf(top)("x2_tiles", [P, AHEAD, D]), [ch.sem(f"c_x{s}") for s in range(AHEAD)]
        with ExitStack() as es:
            sb = ch.sbuf(es)
            ch.e_raw = {kind: sb(f"e_raw{kind}", [P, NQ, 1024]) for kind in "gud"}
            ch.e_H, ch.e_L = ({kind: sb(f"e_{part}{kind}", [P, NQ, 1024], F32R) for kind in "gud"} for part in "HL")
            ch.e_w_hi, ch.e_w_lo = ({kind: ch.sem(f"e_{part}{kind}") for kind in "gud"} for part in ("hi", "lo"))
            ch.e_w_in = {kind: [ch.sem(f"e_w{kind}{q}") for q in range(NQ)] for kind in "gud"}
            stage_route(nc, ch)
            stage_experts(nc, ch)
        stage_beyond(nc, ch)
        stage_combine(nc, ch)


def kernel(**inputs):
    import concourse.bacc as bacc
    from concourse.bass_utils import run_bass_kernel_spmd

    nc = bacc.Bacc("TRN2", target_bir_lowering=False, num_devices=1)
    arrays, ins, outs, consts = {}, {}, {}, {}
    for name in INPUTS:
        a = np.ascontiguousarray(inputs[name])
        arrays[f"in_{name}"] = a
        ins[name] = nc.dram_tensor(f"in_{name}", a.shape, mybir.dt.from_np(a.dtype), kind="ExternalInput").ap()
    for name, a in constants().items():
        a = np.ascontiguousarray(a)
        arrays[f"const_{name}"] = a
        consts[name] = nc.dram_tensor(f"const_{name}", a.shape, mybir.dt.from_np(a.dtype), kind="ExternalInput").ap()
    for name, shape in OUTPUTS:
        outs[name] = nc.dram_tensor(f"out_{name}", shape, F32, kind="ExternalOutput").ap()
    hybrid_decoder_layer(nc, ins, outs, consts)
    r = run_bass_kernel_spmd(nc, [arrays], core_ids=[0])
    return tuple(r.results[0][f"out_{name}"] for name, _ in OUTPUTS)
```
